# Optimizing a Trainium2 kernel written in Bass

```python
import jax, jax.numpy as jnp
from jax import lax
import numpy as np

D_MODEL = 2048
BATCH = 1
SEQ = 256
DEPTH = 1

CHUNK = 64
M_HEADS = 4
M_QK_DIM = 128
M_V_DIM = 256
M_CONV = 4
A_HEADS = 8
A_HEAD_DIM = 128
A_PAST_CHUNKS = 8
A_MAX_REL = 128
D_FF = 5632
FFN_CONV = 3

EPS = 1e-6
NEG = -1e30

M_QK = M_HEADS * M_QK_DIM
M_V = M_HEADS * M_V_DIM
A_W = A_HEADS * A_HEAD_DIM
SPLITS = (M_QK, M_QK, M_V, M_V, M_HEADS, M_HEADS, A_W, A_W, A_W, D_MODEL, D_MODEL)
PROJ_WIDTH = sum(SPLITS)

kernel_name = "hybrid_mlstm_chunkattn_convffn"

def rmsnorm(x, g):
    xf = x.astype(jnp.float32)
    y = xf * lax.rsqrt(jnp.mean(xf * xf, axis=-1, keepdims=True) + EPS)
    return (y * g.astype(jnp.float32)).astype(x.dtype)

def causal_dwconv(x, w, b):
    K = w.shape[0]
    S = x.shape[1]
    xp = jnp.pad(x, ((0, 0), (K - 1, 0), (0, 0)))
    y = b
    for tap in range(K):
        y = y + xp[:, tap:tap + S] * w[tap]
    return y

def to_heads(t, n_heads):
    B, S, _ = t.shape
    return t.reshape(B, S, n_heads, -1).transpose(0, 2, 1, 3)

def from_heads(t):
    B, H, S, d = t.shape
    return t.transpose(0, 2, 1, 3).reshape(B, S, H * d)

def mlstm_chunkwise(q, k, v, li, lf):
    B, H, S, dk = q.shape
    dv = v.shape[-1]
    L = CHUNK
    NC = S // L
    q = q.reshape(B, H, NC, L, dk)
    k = k.reshape(B, H, NC, L, dk)
    v = v.reshape(B, H, NC, L, dv)
    li = li.reshape(B, H, NC, L)
    lf = lf.reshape(B, H, NC, L)
    b = jnp.cumsum(lf, axis=-1)
    b_tot = b[..., -1]
    causal = jnp.tril(jnp.ones((L, L), dtype=bool))
    d_log = jnp.where(causal, b[..., :, None] - b[..., None, :] + li[..., None, :], NEG)
    w_log = b_tot[..., None] - b + li
    m_loc = jnp.max(w_log, axis=-1)
    wk = jnp.exp(w_log - m_loc[..., None])[..., None] * k
    c_loc = jnp.einsum('bhcsk,bhcsv->bhckv', wk, v)
    n_loc = jnp.sum(wk, axis=3)

    def step(carry, inp):
        c_st, n_st, m_st = carry
        c_l, n_l, m_l, bt = inp
        m_new = jnp.maximum(bt + m_st, m_l)
        a = jnp.exp(bt + m_st - m_new)
        cl = jnp.exp(m_l - m_new)
        c_new = a[..., None, None] * c_st + cl[..., None, None] * c_l
        n_new = a[..., None] * n_st + cl[..., None] * n_l
        return (c_new, n_new, m_new), (c_st, n_st, m_st)

    init = (jnp.zeros((B, H, dk, dv), jnp.float32),
            jnp.zeros((B, H, dk), jnp.float32),
            jnp.full((B, H), NEG, jnp.float32))
    xs = (jnp.moveaxis(c_loc, 2, 0), jnp.moveaxis(n_loc, 2, 0),
          jnp.moveaxis(m_loc, 2, 0), jnp.moveaxis(b_tot, 2, 0))
    _, (c_prev, n_prev, m_prev) = lax.scan(step, init, xs)
    c_prev = jnp.moveaxis(c_prev, 0, 2)
    n_prev = jnp.moveaxis(n_prev, 0, 2)
    m_prev = jnp.moveaxis(m_prev, 0, 2)

    inter_log = b + m_prev[..., None]
    m_t = jnp.maximum(jnp.max(d_log, axis=-1), inter_log)
    p = jnp.exp(d_log - m_t[..., None]) * jnp.einsum('bhctk,bhcsk->bhcts', q, k)
    a_inter = jnp.exp(inter_log - m_t)
    num = jnp.einsum('bhcts,bhcsv->bhctv', p, v) + a_inter[..., None] * jnp.einsum('bhctk,bhckv->bhctv', q, c_prev)
    den = jnp.sum(p, axis=-1) + a_inter * jnp.einsum('bhctk,bhck->bhct', q, n_prev)
    h = num / jnp.maximum(jnp.abs(den), jnp.exp(-m_t))[..., None]
    return h.reshape(B, H, S, dv)

def chunk_band_attention(q, k, v, rel_table):
    B, H, S, dh = q.shape
    L = CHUNK
    NC = S // L
    W = A_PAST_CHUNKS + 1
    qc = q.reshape(B, H, NC, L, dh)
    pad = ((0, 0), (0, 0), (A_PAST_CHUNKS, 0), (0, 0), (0, 0))
    kp = jnp.pad(k.reshape(B, H, NC, L, dh), pad)
    vp = jnp.pad(v.reshape(B, H, NC, L, dh), pad)
    idx = jnp.arange(NC)[:, None] + jnp.arange(W)[None, :]
    kb = kp[:, :, idx].reshape(B, H, NC, W * L, dh)
    vb = vp[:, :, idx].reshape(B, H, NC, W * L, dh)
    s = jnp.einsum('bhcqd,bhckd->bhcqk', qc, kb).astype(jnp.float32) * (dh ** -0.5)
    qpos = A_PAST_CHUNKS * L + jnp.arange(L)
    kpos = jnp.arange(W * L)
    rel = jnp.clip(qpos[:, None] - kpos[None, :], -A_MAX_REL, A_MAX_REL) + A_MAX_REL
    bias = rel_table.astype(jnp.float32)[:, rel]
    valid = (jnp.arange(NC)[:, None] - A_PAST_CHUNKS + jnp.arange(W)[None, :]) >= 0
    valid = jnp.repeat(valid, L, axis=1)
    s = jnp.where(valid[None, None, :, None, :], s + bias[None, :, None], NEG)
    p = jax.nn.softmax(s, axis=-1).astype(v.dtype)
    o = jnp.einsum('bhcqk,bhckd->bhcqd', p, vb)
    return o.reshape(B, H, S, dh)

def setup_inputs(seed: int = 0) -> dict:
    key = jax.random.key(seed)
    ks = jax.random.split(key, 24)
    f32 = jnp.float32

    def nrm(k, shape, scale):
        return jax.random.normal(k, shape, f32) * scale

    return {
        "x": nrm(ks[0], (BATCH, SEQ, D_MODEL), 1.0),
        "norm_mix": 1.0 + nrm(ks[1], (DEPTH, D_MODEL), 0.02),
        "w_in": nrm(ks[2], (DEPTH, D_MODEL, PROJ_WIDTH), D_MODEL ** -0.5),
        "conv_qk_w": nrm(ks[3], (DEPTH, M_CONV, 2 * M_QK), M_CONV ** -0.5),
        "conv_qk_b": nrm(ks[4], (DEPTH, 2 * M_QK), 0.02),
        "b_igate": nrm(ks[5], (DEPTH, M_HEADS), 0.1),
        "b_fgate": jnp.linspace(3.0, 6.0, M_HEADS, dtype=f32)[None, :] + nrm(ks[6], (DEPTH, M_HEADS), 0.1),
        "m_norm": 1.0 + nrm(ks[7], (DEPTH, M_V), 0.02),
        "rel_bias": nrm(ks[8], (DEPTH, A_HEADS, 2 * A_MAX_REL + 1), 0.5),
        "gate_bias": nrm(ks[9], (DEPTH, 2, D_MODEL), 0.02),
        "w_branch_m": nrm(ks[10], (DEPTH, M_V, D_MODEL), M_V ** -0.5),
        "w_branch_a": nrm(ks[11], (DEPTH, A_W, D_MODEL), A_W ** -0.5),
        "w_out": nrm(ks[12], (DEPTH, D_MODEL, D_MODEL), D_MODEL ** -0.5),
        "norm_ffn": 1.0 + nrm(ks[13], (DEPTH, D_MODEL), 0.02),
        "w_up": nrm(ks[14], (DEPTH, D_MODEL, 2 * D_FF), D_MODEL ** -0.5),
        "conv_ffn_w": nrm(ks[15], (DEPTH, FFN_CONV, D_FF), FFN_CONV ** -0.5),
        "conv_ffn_b": nrm(ks[16], (DEPTH, D_FF), 0.02),
        "w_down": nrm(ks[17], (DEPTH, D_FF, D_MODEL), D_FF ** -0.5),
        "norm_final": 1.0 + nrm(ks[18], (D_MODEL,), 0.02),
    }

def reference(x, norm_mix, w_in, conv_qk_w, conv_qk_b, b_igate, b_fgate, m_norm, rel_bias,
              gate_bias, w_branch_m, w_branch_a, w_out, norm_ffn, w_up, conv_ffn_w, conv_ffn_b,
              w_down, norm_final):
    f32 = jnp.float32
    split_idx = [int(i) for i in np.cumsum(SPLITS)[:-1]]
    for l in range(DEPTH):
        h = rmsnorm(x, norm_mix[l])
        proj = h @ w_in[l]
        mq, mk, mv, mo, mi, mf, aq, ak, av, g_m, g_a = jnp.split(proj, split_idx, axis=-1)

        qk = jax.nn.silu(causal_dwconv(jnp.concatenate([mq, mk], axis=-1), conv_qk_w[l], conv_qk_b[l]))
        mq, mk = jnp.split(qk, 2, axis=-1)
        q_h = to_heads(mq, M_HEADS).astype(f32)
        k_h = to_heads(mk, M_HEADS).astype(f32) * (M_QK_DIM ** -0.5)
        v_h = to_heads(mv, M_HEADS).astype(f32)
        li = (mi.astype(f32) + b_igate[l].astype(f32)).transpose(0, 2, 1)
        lf = jax.nn.log_sigmoid(mf.astype(f32) + b_fgate[l].astype(f32)).transpose(0, 2, 1)
        hm = mlstm_chunkwise(q_h, k_h, v_h, li, lf)
        hm = hm * lax.rsqrt(jnp.mean(hm * hm, axis=-1, keepdims=True) + EPS)
        hm = from_heads(hm) * m_norm[l].astype(f32)
        hm = (hm * jax.nn.sigmoid(mo.astype(f32))).astype(x.dtype)
        y_m = hm @ w_branch_m[l]

        ha = chunk_band_attention(to_heads(aq, A_HEADS), to_heads(ak, A_HEADS), to_heads(av, A_HEADS), rel_bias[l])
        y_a = from_heads(ha) @ w_branch_a[l]

        merged = jax.nn.sigmoid(g_m + gate_bias[l, 0]) * y_m + jax.nn.sigmoid(g_a + gate_bias[l, 1]) * y_a
        x = x + merged @ w_out[l]

        h = rmsnorm(x, norm_ffn[l])
        u_gate, u_val = jnp.split(h @ w_up[l], 2, axis=-1)
        u_gate = causal_dwconv(u_gate, conv_ffn_w[l], conv_ffn_b[l])
        x = x + (jax.nn.silu(u_gate) * u_val) @ w_down[l]
    return rmsnorm(x, norm_final)


_drawn_inputs = setup_inputs


def setup_inputs(seed=0):
    import zlib

    import numpy as np

    out = dict(_drawn_inputs(seed))
    spreads = {}
    factors = {'norm_mix': 4.713,
     'conv_qk_b': 64.0,
     'b_igate': 200.0,
     'm_norm': 22.757,
     'gate_bias': 8.0,
     'norm_ffn': 10.454,
     'conv_ffn_b': 15.061,
     'norm_final': 22.861}
    for name, (base, spread) in spreads.items():
        noise = np.random.default_rng([zlib.crc32(name.encode()), seed]).standard_normal(out[name].shape)
        drawn = base * np.exp(spread * noise) if base else spread * noise
        out[name] = __import__('jax').numpy.asarray(drawn.astype(out[name].dtype))
    for name, factor in factors.items():
        out[name] = (out[name] * factor).astype(out[name].dtype)
    return out
```

```python
from contextlib import ExitStack

import concourse.bass as bass
from concourse import mybir

F32 = mybir.dt.float32
F32R = mybir.dt.float32r
ALU = mybir.AluOpType
ACT = mybir.ActivationFunctionType
AX_X = mybir.AxisListType.X

P = 128
CHUNK = 64
EPS = 1e-6
BIG = 1e30
COLS = 256
TILE_K = 8
AHEAD = 2
HALF_K = TILE_K // 2
RAW_SLOTS = 4
HALF_SLOTS = 2 * AHEAD


class OwnSteps:

    def __init__(self, eng, sem):
        self.eng, self.sem, self.base, self.count = eng, sem, 0, 0

    def add(self, ins):
        ins.then_inc(self.sem, 1)
        self.count += 1

    def settle(self):
        self.eng.wait_ge(self.sem, self.base + self.count)

    def enter(self, i, per):
        self.loop_base, self.per = self.base + self.count, per
        self.base, self.count = self.loop_base + i * per, 0

    def leave(self, times):
        assert self.count == self.per, (self.count, self.per)
        self.base, self.count = self.loop_base + times * self.per, 0


def hybrid_block(nc, x, norm_mix, w_in, conv_qk_w, conv_qk_b, b_igate, b_fgate, m_norm, rel_bias, gate_bias,
                 w_branch_m, w_branch_a, w_out, norm_ffn, w_up, conv_ffn_w, conv_ffn_b, w_down, norm_final, out):
    _, S, D = x.shape
    D_FF = w_down.shape[1]
    M_H = b_igate.shape[1]
    M_V = m_norm.shape[1]
    M_QK = conv_qk_w.shape[2] // 2
    DK, DV = M_QK // M_H, M_V // M_H
    A_H = rel_bias.shape[1]
    A_W = w_branch_a.shape[1]
    DH = A_W // A_H
    REL = rel_bias.shape[2]
    A_MAX_REL = REL // 2
    TT = S // P
    KD, KV, KF = D // P, M_V // P, D_FF // P
    assert (S, DK, DV, DH, TT, M_H, A_H, COLS) == (256, P, 2 * P, P, 2, 4, 8, S)
    assert KV == A_W // P == TILE_K and KD == 2 * TILE_K and KF % 4 == 0 and A_MAX_REL == P
    offset = {}
    at = 0
    for name, width in (("mq", M_QK), ("mk", M_QK), ("mv", M_V), ("mo", M_V), ("mi", M_H), ("mf", M_H),
                        ("aq", A_W), ("ak", A_W), ("av", A_W), ("gates", 2 * D)):
        offset[name] = at
        at += width
    assert at == w_in.shape[2]

    DOWN_TILES = [TILE_K] * (KF // TILE_K) + [KF % TILE_K]
    NDT = len(DOWN_TILES)
    M_IT, A_IT, G_IT, B_IT, O_IT, U_IT, D_IT = 2, A_H // 2, 2, 4, 4, D_FF // COLS, 4
    seg, t, g = {}, 0, 0
    for name, times, tiles, groups in (("M", M_IT, 12, 6), ("A", A_IT, 12, 6), ("G", G_IT, 4, 2), ("B", B_IT, 4, 4),
                                       ("O", O_IT, 4, 2), ("U", U_IT, 4, 2), ("D", D_IT, 2 * NDT, 2)):
        seg[name] = (t, g, tiles, groups)
        assert t % RAW_SLOTS == 0 and g % 2 == 0
        t, g = t + times * tiles, g + times * groups
    LAST_TILE, LAST_GROUP = t, g
    A_GATES = 3 * A_IT

    def place(name, i):
        t0, g0, tiles, groups = seg[name]
        return t0 + i * tiles, g0 + i * groups

    tpad = nc.dram_tensor("tpad_scratch", (A_H, 3 * P), F32, kind="Internal")
    x2_dram = nc.dram_tensor("x2_scratch", (P, KD * S), F32, kind="Internal").ap()

    with ExitStack() as ctx:
        def sb(name, shape, dt=F32):
            return ctx.enter_context(nc.sbuf_tensor(name, shape, dt))

        def sem(name):
            return ctx.enter_context(nc.semaphore(name))

        def region(kib, *sets):
            made = []
            for one in sets:
                with ExitStack() as s:
                    made += [s.enter_context(nc.sbuf_tensor(n, shape, dt)) for n, shape, dt in one]
            ctx.enter_context(nc.sbuf_tensor(f"hold_{made[0].name}", [P, kib * 256], F32))
            return made

        raw, rows_out = region(32, [("raw", [P, RAW_SLOTS, TILE_K, COLS], F32)], [("rows_out", [P, TT, D], F32)])
        parts = sb("parts", [P, HALF_SLOTS, HALF_K, 2, COLS], F32R)
        h_parts, x3 = region(32, [("h_parts", [P, KD, 2 * S], F32R)], [("x3", [P, KD, S], F32)])
        hm_size, ga_size = KV * 2 * S, 2 * KD * S
        stages = region(
            96,
            [("hm_parts", [P, KV, 2 * S], F32R), ("hold_a", [P, hm_size + ga_size], F32),
             ("merged_parts", [P, KD, 2 * S], F32R)],
            [("hold_b", [P, hm_size], F32), ("ha_parts", [P, KV, 2 * S], F32R), ("gates", [P, 2 * KD, S], F32),
             ("x_rows", [P, TT, D], F32), ("wif_raw", [P, KD, P], F32), ("vec_rows", [P, 3, P], F32),
             ("rel_rows", [A_H, 3 * P], F32)],
            [("junk", [P, D], F32), ("if_low_sb", [64, S], F32), ("if_sum", [64, S], F32), ("li_row", [M_H, S], F32),
             ("z_row", [M_H, S], F32), ("abs_row", [M_H, S], F32), ("log_row", [M_H, S], F32),
             ("if_bias", [64, 8], F32), ("hold_c", [P, hm_size - D - 6 * S - 8], F32), ("wif_parts", [P, KD, 2, P], F32R),
             ("x_again", [P, TT, D], F32), ("x_stage", [P, TT, 2 * P], F32),
             ("hold_d", [P, ga_size - TT * D - 2 * S], F32), ("bias_qk", [P, A_H, 3 * P], F32),
             ("hankel", [P, A_H, 2, P], F32), ("aq", [P, 2, S], F32), ("ak", [P, 2, S], F32), ("av", [P, TT, 2 * P], F32),
             ("scores", [P, 2, 3 * P], F32), ("probs_t", [P, 2, 3 * P], F32)],
            [("hold_e", [P, hm_size], F32), ("mo_sum", [P, 2, 2, S], F32), ("conv_in", [P, 2, S + 4], F32),
             ("hold_f", [P, hm_size - 4 * S - 2 * (S + 4)], F32),
             ("mv", [P, TT, 2 * DV], F32), ("conv_out", [P, 2, S], F32), ("mq", [P, 2, S], F32), ("mk", [P, 2, S], F32),
             ("decay", [P, 2, 3 * P], F32), ("mprobs", [P, 2, 3 * P], F32), ("inv", [P, 2, S], F32),
             ("hval", [P, 2, 2, S], F32), ("hsq", [P, 2, 2, S], F32), ("pick", [M_H, M_H, P], F32),
             ("g_row", [M_H, S], F32), ("m_row", [M_H, S], F32), ("future", [P, P], F32), ("anti", [P, P], F32)],
            [("act_parts", [P, KF, 2 * S], F32R), ("u_conv_in", [P, 2, S + 2], F32), ("u_conv_out", [P, 2, S], F32),
             ("u_silu", [P, 2, S], F32)])
        named = {r.name: r for r in stages}
        hm_parts, ha_parts, gates, merged_parts = (named[n] for n in ("hm_parts", "ha_parts", "gates", "merged_parts"))
        x_rows, wif_raw, wif_parts, x_again, x_stage = (named[n] for n in ("x_rows", "wif_raw", "wif_parts", "x_again", "x_stage"))
        vec_rows, rel_rows, junk, if_low_sb, if_sum = (named[n] for n in ("vec_rows", "rel_rows", "junk", "if_low_sb", "if_sum"))
        li_row, z_row, abs_row, log_row, if_bias = (named[n] for n in ("li_row", "z_row", "abs_row", "log_row", "if_bias"))
        bias_qk, hankel, aq, ak, av = (named[n] for n in ("bias_qk", "hankel", "aq", "ak", "av"))
        scores, probs_t, mo_sum, conv_in, mv = (named[n] for n in ("scores", "probs_t", "mo_sum", "conv_in", "mv"))
        conv_out, mq, mk, decay, mprobs = (named[n] for n in ("conv_out", "mq", "mk", "decay", "mprobs"))
        inv, hval, hsq, pick, g_row, m_row = (named[n] for n in ("inv", "hval", "hsq", "pick", "g_row", "m_row"))
        future, anti = (named[n] for n in ("future", "anti"))
        act_parts, u_conv_in, u_conv_out, u_silu = (named[n] for n in ("act_parts", "u_conv_in", "u_conv_out", "u_silu"))

        ident = sb("ident", [P, P])
        ones = sb("ones", [P, S])
        lows = sb("lows", [P, 2, 2, S])
        sums = sb("sums", [P, 2, 2, S])
        squares = sb("squares", [P, 2, S])
        acc = sb("acc", [P, 2, S])
        r_bc = sb("r_bc", [P, S])
        vec = sb("vec", [P, P + 4 * KF])
        small = sb("small", [P, 32 + TT * M_H])
        ccol = small[:, 32:32 + TT * M_H]
        main = ctx.enter_context(nc.psum_tensor("main", [P, 2, 2, 512], F32))
        aux = ctx.enter_context(nc.psum_tensor("aux", [P, 4, 512], F32))

        def row_bank(f):
            return main[:, f // 2, f % 2, :] if f < 4 else aux[:, f - 4, :]

        x_in = [sem(f"x_in{k}") for k in range(TT)]
        w_loaded = [sem(f"w_loaded{k}") for k in range(RAW_SLOTS)]
        vec_in, wif_in, rel_in, tpad_out, hankel_in = (sem(n) for n in ("vec_in", "wif_in", "rel_in", "tpad_out", "hankel_in"))
        x_again_in, x3_in, rows_stored = (sem(n) for n in ("x_again_in", "x3_in", "rows_stored"))
        x2_stored = [sem(f"x2_stored{k}") for k in range(2)]
        hi_ready, lo_ready, half_used, low_copied, group_summed = (
            sem(n) for n in ("hi_ready", "lo_ready", "half_used", "low_copied", "group_summed"))
        pool_const, wif_zero, wif_hi, wif_lo, vec_t, vec_ready, rel_pad = (
            sem(n) for n in ("pool_const", "wif_zero", "wif_hi", "wif_lo", "vec_t", "vec_ready", "rel_pad"))
        x_sq, x_rms, x_scaled, x_turned, h_hi, h_lo = (
            sem(n) for n in ("x_sq", "x_rms", "x_scaled", "x_turned", "h_hi", "h_lo"))
        if_done, if_low, z_ready, log_term, c_row_ready, c_turned, c_ready, hankel_masked, bias_mm, bias_ready = (
            sem(n) for n in ("if_done", "if_low", "z_ready", "log_term", "c_row_ready", "c_turned", "c_ready",
                            "hankel_masked", "bias_mm", "bias_ready"))
        first_tap, conv_done, mqk_ready, mqk_done, decay_ready, mprob_ready, mnum_done, floor_ready = (
            sem(n) for n in ("first_tap", "conv_done", "mqk_ready", "mqk_done", "decay_ready", "mprob_ready",
                            "mnum_done", "floor_ready"))
        h_ready, hsq_ready, mss_done, mrms_ready, mo_ready, hm_ready, hm_hi, hm_lo, eps_ready = (
            sem(n) for n in ("h_ready", "hsq_ready", "mss_done", "mrms_ready", "mo_ready", "hm_ready", "hm_hi", "hm_lo",
                            "eps_ready"))
        a_scored, a_max, a_exp, a_prob, a_turned, a_copied, a_out, ha_hi, ha_lo, gate_done = (
            sem(n) for n in ("a_scored", "a_max", "a_exp", "a_prob", "a_turned", "a_copied", "a_out", "ha_hi", "ha_lo",
                            "gate_done"))
        merged_ready, merged_hi, merged_lo, xs_copied, x2_sq, h2_hi, h2_lo, acc_ready, ss_done, rms_ready, r_ready = (
            sem(n) for n in ("merged_ready", "merged_hi", "merged_lo", "xs_copied", "x2_sq", "h2_hi", "h2_lo",
                            "acc_ready", "ss_done", "rms_ready", "r_ready"))
        u_scaled, u_tap, u_conv, u_act, u_silu_done, act_hi, act_lo = (
            sem(n) for n in ("u_scaled", "u_tap", "u_conv", "u_act", "u_silu_done", "act_hi", "act_lo"))
        x3_ready, x3_sq, x3_final, fin_ss, fin_rms, fin_r, rows_turned, rows_a, rows_v = (
            sem(n) for n in ("x3_ready", "x3_sq", "x3_final", "fin_ss", "fin_rms", "fin_r", "rows_turned", "rows_a",
                            "rows_v"))
        act_own, dve_own, pool_own = sem("act_own"), sem("dve_own"), sem("pool_own")

        V_MIX, V_FFN, V_FIN, V_CW, V_CB, V_MN, V_GB = 0, 16, 32, 48, 80, 88, 96
        V_UW, V_UB = P, P + 3 * KF

        def vcol(c):
            return vec[:, bass.ds(c, 1)]

        TURN_ORDER = [4 * f + q for f in range(KD // 4) for q in (0, 2, 1, 3)]

        block = ctx.enter_context(nc.Block())

        def tile_rows(j_in_seg, name):
            return DOWN_TILES[j_in_seg % NDT] if name == "D" else TILE_K

        @block.sync
        def _(sp):
            xr = x[0].rearrange("(t p) d -> p t d", p=P)
            for k in range(TT):
                sp.dma_start(x_rows[:, k, :], xr[:, k, :]).then_inc(x_in[k], 16)

            def load(n, j, w, k0, kn, col):
                if not (isinstance(n, int) and n < RAW_SLOTS):
                    sp.wait_ge(lo_ready, 2 * (n - RAW_SLOTS + 1))
                src = w[0, k0 * P:(k0 + kn) * P, bass.ds(col, COLS)].rearrange("(k p) c -> p k c", p=P)
                sp.dma_start(raw[:, j % RAW_SLOTS, 0:kn, :], src).then_inc(w_loaded[j % RAW_SLOTS], 16)

            def load_group(n, j, w, col, count=2):
                for k in range(count):
                    load(n + k, j + k, w, k * TILE_K, TILE_K, col)

            for i in range(M_IT):
                n, _ = place("M", i)
                for c, col in enumerate((offset["mq"] + i * COLS, offset["mk"] + i * COLS,
                                         offset["mv"] + 2 * i * COLS, offset["mv"] + (2 * i + 1) * COLS,
                                         offset["mo"] + 2 * i * COLS, offset["mo"] + (2 * i + 1) * COLS)):
                    load_group(n + 2 * c, 2 * c, w_in, col)
            with sp.Fori(0, A_IT) as i:
                n, _ = place("A", i)
                for c, name in enumerate(("aq", "ak", "av")):
                    load_group(n + 2 * c, 2 * c, w_in, offset[name] + i * COLS)
                for c in range(3):
                    load_group(n + 6 + 2 * c, 6 + 2 * c, w_in, offset["gates"] + (3 * i + c) * COLS)
            with sp.Fori(0, G_IT) as i:
                n, _ = place("G", i)
                for c in range(2):
                    load_group(n + 2 * c, 2 * c, w_in, offset["gates"] + A_GATES * COLS + (2 * i + c) * COLS)
            with sp.Fori(0, B_IT) as i:
                n, _ = place("B", i)
                for c in range(2):
                    load_group(n + 2 * c, 2 * c, w_branch_m, (2 * i + c) * COLS, 1)
                    load_group(n + 2 * c + 1, 2 * c + 1, w_branch_a, (2 * i + c) * COLS, 1)
            with sp.Fori(0, O_IT) as i:
                n, _ = place("O", i)
                for c in range(2):
                    load_group(n + 2 * c, 2 * c, w_out, (2 * i + c) * COLS)
            with sp.Fori(0, U_IT) as i:
                n, _ = place("U", i)
                load_group(n, 0, w_up, i * COLS)
                load_group(n + 2, 2, w_up, D_FF + i * COLS)
            with sp.Fori(0, D_IT) as i:
                n, _ = place("D", i)
                for c in range(2):
                    for k, kn in enumerate(DOWN_TILES):
                        load(n + NDT * c + k, NDT * c + k, w_down, k * TILE_K, kn, (2 * i + c) * COLS)
            outr = out[0].rearrange("(t p) d -> p t d", p=P)
            for f in range(8):
                tt, q = f // 4, f % 4
                sp.wait_ge(rows_a if f % 2 == 0 else rows_v, f // 2 + 1)
                sp.dma_start(outr[:, tt, q * 512:(q + 1) * 512], rows_out[:, tt, q * 512:(q + 1) * 512]).then_inc(rows_stored, 16)
            sp.wait_ge(rows_stored, 8 * 16)

        @block.gpsimd
        def _(pool):
            own = OwnSteps(pool, pool_own)
            own.add(nc.gpsimd.memset(wif_raw[:], 0.0))
            own.settle()
            wi = w_in[0].rearrange("(k p) c -> p k c", p=P)
            with nc.allow_non_contiguous_dma(reason="four columns of each gate"):
                pool.dma_start(wif_raw[:, :, 0:M_H], wi[:, :, offset["mi"]:offset["mi"] + M_H]).then_inc(wif_in, 16)
                pool.dma_start(wif_raw[:, :, 32:32 + M_H], wi[:, :, offset["mf"]:offset["mf"] + M_H]).then_inc(wif_in, 16)
                pool.dma_start(if_bias[0:M_H, 0:1], b_igate.rearrange("a h -> h a")).then_inc(wif_in, 16)
                pool.dma_start(if_bias[32:32 + M_H, 0:1], b_fgate.rearrange("a h -> h a")).then_inc(wif_in, 16)
            pool.dma_start(rel_rows[:, 0:REL], rel_bias[0]).then_inc(rel_in, 16)
            for buf, value in ((ident, 0.0), (anti, 0.0), (future, 0.0), (pick, 0.0), (ones, 1.0)):
                own.add(nc.gpsimd.memset(buf[:], value))
            own.settle()
            nc.gpsimd.affine_select(out=ident[:], in_=ident[:], compare_op=ALU.not_equal, fill=1.0, base=0,
                                    pattern=[[-1, P]], channel_multiplier=1).then_inc(pool_const, 1)
            nc.gpsimd.affine_select(out=anti[:], in_=anti[:], compare_op=ALU.not_equal, fill=1.0, base=1 - P,
                                    pattern=[[1, P]], channel_multiplier=1).then_inc(pool_const, 1)
            nc.gpsimd.affine_select(out=future[:], in_=future[:], compare_op=ALU.is_ge, fill=BIG, base=0,
                                    pattern=[[1, P]], channel_multiplier=-1).then_inc(pool_const, 1)
            nc.gpsimd.affine_select(out=pick[:], in_=pick[:], compare_op=ALU.not_equal, fill=1.0, base=0,
                                    pattern=[[-1, M_H], [0, P]], channel_multiplier=1).then_inc(pool_const, 1)
            pool.wait_ge(rel_pad, 1)
            pool.dma_start(tpad.ap(), rel_rows[:]).then_inc(tpad_out, 16)
            pool.wait_ge(tpad_out, 16)
            pool.wait_ge(x_turned, 4)
            pool.wait_ge(wif_lo, 1)
            for b in range(2):
                src = bass.AP(tensor=tpad, offset=1 + P * b, ap=[[1, P], [3 * P, A_H], [1, P]])
                pool.dma_start(hankel[:, :, b, :], src).then_inc(hankel_in, 16)
            pool.wait_ge(hankel_in, 32)
            nc.gpsimd.memset(hankel[0:CHUNK, :, 0, 0:CHUNK], -BIG).then_inc(hankel_masked, 1)
            pool.wait_ge(merged_ready, 2 * B_IT)
            pool.dma_start(x_again[:], x[0].rearrange("(t p) d -> p t d", p=P)).then_inc(x_again_in, 16)
            with pool.Fori(0, O_IT) as i:
                _, g = place("O", i)
                for c in range(2):
                    pool.wait_ge(group_summed, g + c + 1)
                    pool.dma_start(x2_dram[:, bass.ds((2 * i + c) * 2 * S, 2 * S)],
                                   sums[:, c].rearrange("p a s -> p (a s)")).then_inc(x2_stored[c], 16)
            for c in range(2):
                pool.wait_ge(x2_stored[c], O_IT * 16)
            pool.wait_ge(half_used, 2 * seg["D"][0])
            pool.dma_start(x3[:].rearrange("p k s -> p (k s)"), x2_dram).then_inc(x3_in, 16)

        @block.scalar
        def _(act):
            own = OwnSteps(act, act_own)
            A = nc.scalar.activation
            for r0, ap in ((V_MIX, norm_mix[0].rearrange("(r p) -> r p", p=P)), (V_FFN, norm_ffn[0].rearrange("(r p) -> r p", p=P)),
                           (V_FIN, norm_final.rearrange("(r p) -> r p", p=P)),
                           (V_CW, conv_qk_w[0].rearrange("k (r p) -> (k r) p", p=P)),
                           (V_CB, conv_qk_b[0].rearrange("(r p) -> r p", p=P)), (V_MN, m_norm[0].rearrange("(r p) -> r p", p=P)),
                           (V_GB, gate_bias[0].rearrange("k (r p) -> (k r) p", p=P))):
                act.dma_start(vec_rows[r0:r0 + ap.shape[0], 0, :], ap).then_inc(vec_in, 16)
            cw = conv_ffn_w[0].rearrange("k (r p) -> (k r) p", p=P)
            act.dma_start(vec_rows[0:2 * KF, 1, :], cw[0:2 * KF, :]).then_inc(vec_in, 16)
            act.dma_start(vec_rows[0:KF, 2, :], cw[2 * KF:3 * KF, :]).then_inc(vec_in, 16)
            act.dma_start(vec_rows[KF:2 * KF, 2, :], conv_ffn_b[0].rearrange("(r p) -> r p", p=P)).then_inc(vec_in, 16)

            def ahead(name, i, j):
                t0, _, tiles, _ = seg[name]
                slot, kh = (j + AHEAD) % RAW_SLOTS, tile_rows(j + AHEAD, name) // 2
                act.wait_ge(w_loaded[slot], 16 * ((t0 + j + AHEAD) // RAW_SLOTS + 1) + i * (16 * tiles // RAW_SLOTS))
                for f in range(2):
                    act.wait_ge(half_used, 2 * (t0 + j) + f + 1 + i * (2 * tiles))
                    A(parts[:, (2 * j + f) % HALF_SLOTS, 0:kh, 0, :], raw[:, slot, f * kh:(f + 1) * kh, :],
                      ACT.Copy).then_inc(hi_ready, 1)

            def copy_low(name, i, c, last_j, scale=1.0):
                t0, g0, tiles, groups = seg[name]
                act.wait_ge(half_used, 2 * (t0 + last_j + 1) + i * (2 * tiles))
                A(lows[:, c % 2], main[:, c % 2, :, S:2 * S], ACT.Copy, scale=scale).then_inc(low_copied, 1)

            def summed(name, i, c):
                _, g0, _, groups = seg[name]
                act.wait_ge(group_summed, g0 + c + 1 + i * groups)

            for k in range(TT):
                act.wait_ge(x_in[k], 16)
                if k:
                    act.wait_ge(x_sq, k)
                A(junk[:], x_rows[:, k, :], ACT.Square, accum_out=small[:, k:k + 1]).then_inc(x_sq, 1)
            act.wait_ge(x_sq, TT)
            act.wait_ge(eps_ready, 1)
            A(small[:, 2:4], small[:, 0:2], ACT.Sqrt, bias=small[:, 31:32], scale=1.0 / D).then_inc(x_rms, 1)
            act.wait_ge(vec_t, 1)
            A(vec[:], aux[:, 3, 0:P + 4 * KF], ACT.Copy).then_inc(vec_ready, 1)
            act.wait_ge(vec_ready, 1)
            for n, k in enumerate(TURN_ORDER):
                act.wait_ge(x_turned, k // 4 + 1)
                if n >= 2:
                    act.wait_ge(h_lo, n - 1)
                A(h_parts[:, k, 0:S], main[:, (k // 4) % 2, (k // 2) % 2, (k % 2) * S:(k % 2 + 1) * S], ACT.Copy,
                  scale=vcol(V_MIX + k)).then_inc(h_hi, 1)
            act.wait_ge(wif_in, 4 * 16)
            A(wif_parts[:, :, 0, :], wif_raw[:], ACT.Copy).then_inc(wif_hi, 1)
            for j in range(AHEAD):
                act.wait_ge(w_loaded[j], 16)
                for f in range(2):
                    A(parts[:, 2 * j + f, :, 0, :], raw[:, j, f * HALF_K:(f + 1) * HALF_K], ACT.Copy).then_inc(hi_ready, 1)
            act.wait_ge(if_done, 1)
            A(if_low_sb[:], aux[0:64, 0, S:2 * S], ACT.Copy).then_inc(if_low, 1)
            act.wait_ge(z_ready, 1)
            own.add(A(abs_row[:], z_row[:], ACT.Abs))
            own.settle()
            own.add(A(log_row[:], abs_row[:], ACT.Exp, scale=-1.0))
            own.settle()
            A(log_row[:], log_row[:], ACT.Ln, bias=1.0).then_inc(log_term, 1)

            def turn_c():
                act.wait_ge(c_turned, 1)
                A(ccol, aux[:, 1, 0:TT * M_H], ACT.Copy).then_inc(c_ready, 1)

            def bias_copies():
                for b in range(4):
                    act.wait_ge(bias_mm, b + 1)
                    src = aux[:, b, :].rearrange("p (h c) -> p h c", h=2)
                    A(bias_qk[:, 2 * b:2 * b + 2, 0:2 * P], src, ACT.Copy).then_inc(bias_ready, 1)
                    A(bias_qk[:, 2 * b:2 * b + 2, 2 * P:3 * P], src[:, :, 0:P], ACT.Copy).then_inc(bias_ready, 1)

            for i in range(M_IT):
                def first_taps(which):
                    summed("M", i, which)
                    for c in range(2):
                        ch = M_H * which + 2 * i + c
                        A(conv_out[:, c, :], conv_in[:, c, 4:4 + S], ACT.Identity, scale=vcol(V_CW + 3 * 8 + ch),
                          bias=vcol(V_CB + ch)).then_inc(first_tap, 1)

                def conv_silu(which):
                    act.wait_ge(conv_done, 2 * i + which + 1)
                    A((mq, mk)[which][:], conv_out[:], ACT.Silu).then_inc(mqk_ready, 1)

                ahead("M", i, 0)
                ahead("M", i, 1)
                copy_low("M", i, 0, 1)
                first_taps(0)
                ahead("M", i, 2)
                conv_silu(0)
                if i == 0:
                    turn_c()
                ahead("M", i, 3)
                copy_low("M", i, 1, 3)
                first_taps(1)
                ahead("M", i, 4)
                conv_silu(1)
                ahead("M", i, 5)
                copy_low("M", i, 2, 5)
                if i == 0:
                    bias_copies()
                ahead("M", i, 6)
                ahead("M", i, 7)
                copy_low("M", i, 3, 7)
                ahead("M", i, 8)
                for h in range(2):
                    act.wait_ge(mqk_done, 2 * i + h + 1)
                    if h == 0 and i == 0:
                        act.wait_ge(c_ready, 1)
                    hd = 2 * i + h
                    own.add(A(decay[:, h, 0:S], aux[:, 2 + h, 0:S], ACT.Exp, bias=ccol[:, hd:hd + 1], scale=-1.0))
                    A(decay[:, h, S:S + P], aux[:, 2 + h, S:S + P], ACT.Exp, bias=ccol[:, M_H + hd:M_H + hd + 1],
                      scale=-1.0).then_inc(decay_ready, 1)
                ahead("M", i, 9)
                copy_low("M", i, 4, 9)
                summed("M", i, 4)
                A(mo_sum[:, 0], mo_sum[:, 0], ACT.Sigmoid).then_inc(mo_ready, 1)
                ahead("M", i, 10)
                for h in range(2):
                    act.wait_ge(mnum_done, 2 * i + h + 1)
                    A(inv[:, h, :], aux[:, 2 + h, S:2 * S], ACT.Exp, scale=-1.0).then_inc(floor_ready, 1)
                for h in range(2):
                    act.wait_ge(h_ready, 2 * i + h + 1)
                    A(hsq[:, h], hval[:, h], ACT.Square).then_inc(hsq_ready, 1)
                ahead("M", i, 11)
                copy_low("M", i, 5, 11)
                summed("M", i, 5)
                A(mo_sum[:, 1], mo_sum[:, 1], ACT.Sigmoid).then_inc(mo_ready, 1)
                act.wait_ge(mss_done, i + 1)
                A(inv[:], aux[:, 2, :].rearrange("p (h s) -> p h s", h=2), ACT.Sqrt, bias=small[:, 31:32],
                  scale=1.0 / DV).then_inc(mrms_ready, 1)
                for h in range(2):
                    act.wait_ge(hm_ready, 2 * i + h + 1)
                    A(hm_parts[:, 4 * i + 2 * h:4 * i + 2 * h + 2, 0:S], hval[:, h], ACT.Copy).then_inc(hm_hi, 1)

            def gate(name, i, c, index):
                summed(name, i, c)
                for k in range(2):
                    A(gates[:, bass.ds(2 * index + k, 1), :], sums[:, 0, k:k + 1, :], ACT.Sigmoid,
                      bias=vcol(2 * index + k + V_GB)).then_inc(gate_done, 1)

            act.wait_ge(hm_lo, M_H)
            with act.Fori(0, A_IT) as i:
                for c in range(3):
                    ahead("A", i, 2 * c)
                    ahead("A", i, 2 * c + 1)
                    copy_low("A", i, c, 2 * c + 1, scale=DH ** -0.5 if c == 0 else 1.0)
                ahead("A", i, 6)
                for h in range(2):
                    act.wait_ge(a_max, 2 * i + h + 1)
                    A(scores[:, h, 0:P], scores[:, h, 0:P], ACT.Exp, bias=small[:, 8 + 2 * h:9 + 2 * h],
                      accum_out=small[:, 12 + 2 * h:13 + 2 * h]).then_inc(a_exp, 1)
                    A(scores[:, h, P:3 * P], scores[:, h, P:3 * P], ACT.Exp, bias=small[:, 9 + 2 * h:10 + 2 * h],
                      accum_out=small[:, 13 + 2 * h:14 + 2 * h]).then_inc(a_exp, 1)
                ahead("A", i, 7)
                copy_low("A", i, 3, 7)
                gate("A", i, 3, 3 * i)
                ahead("A", i, 8)
                for h in range(2):
                    act.wait_ge(a_turned, 2 * i + h + 1)
                    A(probs_t[:, h], aux[:, 2 + h, 0:3 * P], ACT.Copy).then_inc(a_copied, 1)
                ahead("A", i, 9)
                copy_low("A", i, 4, 9)
                gate("A", i, 4, 3 * i + 1)
                ahead("A", i, 10)
                act.wait_ge(a_out, i + 1)
                A(ha_parts[:, bass.ds(2 * i, 2), 0:S], aux[:, 0, :].rearrange("p (h s) -> p h s", h=2), ACT.Copy).then_inc(ha_hi, 1)
                ahead("A", i, 11)
                copy_low("A", i, 5, 11)
                gate("A", i, 5, 3 * i + 2)
            with act.Fori(0, G_IT) as i:
                for c in range(2):
                    ahead("G", i, 2 * c)
                    ahead("G", i, 2 * c + 1)
                    copy_low("G", i, c, 2 * c + 1)
                    gate("G", i, c, 2 * i + c + A_GATES)
            act.wait_ge(ha_lo, A_IT)
            with act.Fori(0, B_IT) as i:
                for c in range(2):
                    ahead("B", i, 2 * c)
                    copy_low("B", i, 2 * c, 2 * c)
                    ahead("B", i, 2 * c + 1)
                    copy_low("B", i, 2 * c + 1, 2 * c + 1)
                    act.wait_ge(merged_ready, 2 * i + c + 1)
                    A(merged_parts[:, bass.ds(4 * i + 2 * c, 2), 0:S], sums[:, 0], ACT.Copy).then_inc(merged_hi, 1)
            act.wait_ge(x_again_in, 16)
            with act.Fori(0, O_IT) as i:
                for c in range(2):
                    A(x_stage[:], x_again[:, :, bass.ds((4 * i + 2 * c) * P, 2 * P)], ACT.Copy).then_inc(xs_copied, 1)
                    ahead("O", i, 2 * c)
                    ahead("O", i, 2 * c + 1)
                    copy_low("O", i, c, 2 * c + 1)
                    summed("O", i, c)
                    for k in range(2):
                        A(h_parts[:, bass.ds(4 * i + 2 * c + k, 1), 0:S], sums[:, c, k:k + 1, :], ACT.Copy,
                          scale=vcol(4 * i + 2 * c + k + V_FFN)).then_inc(h2_hi, 1)
                    A(squares[:], sums[:, c], ACT.Square).then_inc(x2_sq, 1)
            act.wait_ge(ss_done, 1)
            A(r_bc[:], aux[:, 0, 0:S], ACT.Sqrt, bias=small[:, 31:32], scale=1.0 / D).then_inc(rms_ready, 1)
            with act.Fori(0, U_IT) as i:
                ahead("U", i, 0)
                ahead("U", i, 1)
                copy_low("U", i, 0, 1)
                for k in range(2):
                    act.wait_ge(u_scaled, i + 1)
                    A(u_conv_out[:, k, :], u_conv_in[:, k, 2:2 + S], ACT.Identity, scale=vcol(2 * i + k + V_UW + 2 * KF),
                      bias=vcol(2 * i + k + V_UB)).then_inc(u_tap, 1)
                ahead("U", i, 2)
                act.wait_ge(u_conv, i + 1)
                A(u_silu[:], u_conv_out[:], ACT.Silu).then_inc(u_silu_done, 1)
                ahead("U", i, 3)
                copy_low("U", i, 1, 3)
                act.wait_ge(u_act, i + 1)
                A(act_parts[:, bass.ds(2 * i, 2), 0:S], sums[:, 1], ACT.Copy).then_inc(act_hi, 1)

            def down(i, last):
                for c in range(2):
                    for k in range(NDT):
                        j = NDT * c + k
                        if not (last and j >= 2 * NDT - AHEAD):
                            ahead("D", i, j)
                    copy_low("D", i, c, NDT * (c + 1) - 1)
                    act.wait_ge(x3_ready, 2 * i + c + 1)
                    A(squares[:], x3[:, bass.ds(4 * i + 2 * c, 2), :], ACT.Square).then_inc(x3_sq, 1)

            with act.Fori(0, D_IT - 1) as i:
                down(i, False)
            down(D_IT - 1, True)
            act.wait_ge(fin_ss, 1)
            A(small[:, 2:4], aux[:, 3, 0:TT], ACT.Sqrt, bias=small[:, 31:32], scale=1.0 / D).then_inc(fin_rms, 1)
            act.wait_ge(fin_r, 1)
            for f in range(0, 8, 2):
                tt, q = f // 4, f % 4
                act.wait_ge(rows_turned, f + 1)
                A(rows_out[:, tt, q * 512:(q + 1) * 512], row_bank(f), ACT.Copy, scale=small[:, 4 + tt:5 + tt]).then_inc(rows_a, 1)

        @block.vector
        def _(dve):
            own = OwnSteps(dve, dve_own)
            V = nc.vector

            def ahead(name, i, j):
                t0, _, tiles, _ = seg[name]
                slot, kh = (j + AHEAD) % RAW_SLOTS, tile_rows(j + AHEAD, name) // 2
                for f in range(2):
                    dve.wait_ge(hi_ready, 2 * (t0 + j + AHEAD) + f + 1 + i * (2 * tiles))
                    place = parts[:, (2 * j + f) % HALF_SLOTS, 0:kh]
                    V.tensor_tensor(place[:, :, 1, :], raw[:, slot, f * kh:(f + 1) * kh, :],
                                    place[:, :, 0, :].bitcast(F32), ALU.subtract).then_inc(lo_ready, 1)

            def add_group(name, i, c, dst, scale=1.0):
                _, g0, _, groups = seg[name]
                dve.wait_ge(low_copied, g0 + c + 1 + i * groups)
                V.scalar_tensor_tensor(dst, main[:, c % 2, :, 0:S], scale, lows[:, c % 2], ALU.mult, ALU.add).then_inc(group_summed, 1)

            def summed(name, i, c):
                _, g0, _, groups = seg[name]
                dve.wait_ge(group_summed, g0 + c + 1 + i * groups)

            V.memset(small[:, 31:32], EPS).then_inc(eps_ready, 1)
            own.add(V.memset(acc[:], 0.0))
            dve.wait_ge(rel_in, 16)
            V.tensor_copy(rel_rows[:, REL:3 * P],
                          rel_rows[:, REL - 1:REL].to_broadcast([A_H, 3 * P - REL])).then_inc(rel_pad, 1)
            dve.wait_ge(x_rms, 1)
            own.add(V.reciprocal(small[:, 4:6], small[:, 2:4]))
            own.settle()
            for k in range(TT):
                V.tensor_scalar(x_rows[:, k, :], x_rows[:, k, :], small[:, 4 + k:5 + k], None, ALU.mult).then_inc(x_scaled, 1)
            for n, k in enumerate(TURN_ORDER):
                dve.wait_ge(h_hi, n + 1)
                V.scalar_tensor_tensor(h_parts[:, k, S:2 * S],
                                       main[:, (k // 4) % 2, (k // 2) % 2, (k % 2) * S:(k % 2 + 1) * S], vcol(V_MIX + k),
                                       h_parts[:, k, 0:S].bitcast(F32), ALU.mult, ALU.subtract).then_inc(h_lo, 1)
            dve.wait_ge(wif_hi, 1)
            V.tensor_tensor(wif_parts[:, :, 1, :], wif_raw[:], wif_parts[:, :, 0, :].bitcast(F32), ALU.subtract).then_inc(wif_lo, 1)
            for j in range(AHEAD):
                for f in range(2):
                    dve.wait_ge(hi_ready, 2 * j + f + 1)
                    V.tensor_tensor(parts[:, 2 * j + f, :, 1, :], raw[:, j, f * HALF_K:(f + 1) * HALF_K],
                                    parts[:, 2 * j + f, :, 0, :].bitcast(F32), ALU.subtract).then_inc(lo_ready, 1)
            dve.wait_ge(if_low, 1)
            own.add(V.tensor_tensor(if_sum[:], aux[0:64, 0, 0:S], if_low_sb[:], ALU.add))
            own.add(V.memset(conv_in[:, :, 0:4], 0.0))
            own.settle()
            own.add(V.tensor_scalar(li_row[:], if_sum[0:M_H, :], if_bias[0:M_H, 0:1], None, ALU.add))
            V.tensor_scalar(z_row[:], if_sum[32:32 + M_H, :], if_bias[32:32 + M_H, 0:1], None, ALU.add).then_inc(z_ready, 1)
            dve.wait_ge(log_term, 1)
            own.add(V.scalar_tensor_tensor(z_row[:], z_row[:], 0.0, log_row[:], ALU.min, ALU.subtract))
            own.settle()
            own.add(V.tensor_tensor_scan(abs_row[:], ones[0:M_H, :], z_row[:], 0.0, ALU.mult, ALU.add))
            own.settle()
            V.tensor_tensor(li_row[:], li_row[:], abs_row[:], ALU.subtract).then_inc(c_row_ready, 1)
            dve.wait_ge(c_row_ready, 1)
            own.add(V.tensor_tensor_scan(g_row[:], li_row[:], li_row[:], -3e38, ALU.max, ALU.max))
            own.settle()
            V.tensor_tensor(m_row[:], abs_row[:], g_row[:], ALU.add).then_inc(c_row_ready, 1)

            for i in range(M_IT):
                def conv(which):
                    for k, tap in enumerate((2, 1, 0)):
                        for c in range(2):
                            ch = M_H * which + 2 * i + c
                            if k == 0:
                                dve.wait_ge(first_tap, 4 * i + 2 * which + c + 1)
                            ins = V.scalar_tensor_tensor(conv_out[:, c, :], conv_in[:, c, tap + 1:tap + 1 + S],
                                                         vcol(V_CW + tap * 8 + ch), conv_out[:, c, :], ALU.mult, ALU.add)
                            if tap == 0 and c == 1:
                                ins.then_inc(conv_done, 1)
                            else:
                                own.add(ins)
                        if tap:
                            own.settle()

                for which in range(2):
                    ahead("M", i, 2 * which)
                    ahead("M", i, 2 * which + 1)
                    add_group("M", i, which, conv_in[:, :, 4:4 + S])
                    conv(which)
                for c in range(2):
                    ahead("M", i, 4 + 2 * c)
                    ahead("M", i, 5 + 2 * c)
                    add_group("M", i, 2 + c, mv[:, :, c * DV:(c + 1) * DV])
                ahead("M", i, 8)
                for h in range(2):
                    dve.wait_ge(decay_ready, 2 * i + h + 1)
                    V.scalar_tensor_tensor(mprobs[:, h], aux[:, h, 0:3 * P], DK ** -0.5, decay[:, h], ALU.mult,
                                           ALU.mult).then_inc(mprob_ready, 1)
                ahead("M", i, 9)
                add_group("M", i, 4, mo_sum[:, 0])
                ahead("M", i, 10)
                for h in range(2):
                    dve.wait_ge(floor_ready, 2 * i + h + 1)
                    own.add(V.scalar_tensor_tensor(inv[:, h, :], aux[:, 2 + h, 0:S], -1.0, inv[:, h, :], ALU.mult, ALU.max))
                    own.settle()
                    own.add(V.tensor_tensor(inv[:, h, :], aux[:, 2 + h, 0:S], inv[:, h, :], ALU.max))
                    own.settle()
                    own.add(V.reciprocal(inv[:, h, :], inv[:, h, :]))
                    own.settle()
                    V.tensor_tensor(hval[:, h], aux[:, h, :].rearrange("p (v s) -> p v s", v=2),
                                    inv[:, h:h + 1, :].to_broadcast([P, 2, S]), ALU.mult).then_inc(h_ready, 1)
                ahead("M", i, 11)
                add_group("M", i, 5, mo_sum[:, 1])
                dve.wait_ge(mrms_ready, i + 1)
                own.add(V.reciprocal(inv[:], inv[:]))
                own.settle()
                for h in range(2):
                    own.add(V.tensor_tensor(hval[:, h], hval[:, h], inv[:, h:h + 1, :].to_broadcast([P, 2, S]), ALU.mult))
                    own.settle()
                    dve.wait_ge(mo_ready, 2 * i + h + 1)
                    for c in range(2):
                        ins = V.scalar_tensor_tensor(hval[:, h, c, :], hval[:, h, c, :], vcol(V_MN + 4 * i + 2 * h + c),
                                                     mo_sum[:, h, c, :], ALU.mult, ALU.mult)
                        if c:
                            ins.then_inc(hm_ready, 1)
                        else:
                            own.add(ins)
                for h in range(2):
                    dve.wait_ge(hm_hi, 2 * i + h + 1)
                    dst = hm_parts[:, 4 * i + 2 * h:4 * i + 2 * h + 2]
                    V.tensor_tensor(dst[:, :, S:2 * S], hval[:, h], dst[:, :, 0:S].bitcast(F32), ALU.subtract).then_inc(hm_lo, 1)

            with dve.Fori(0, A_IT) as i:
                own.enter(i, 10)
                for c, dst in enumerate((aq[:], ak[:], av[:])):
                    ahead("A", i, 2 * c)
                    ahead("A", i, 2 * c + 1)
                    add_group("A", i, c, dst, scale=DH ** -0.5 if c == 0 else 1.0)
                ahead("A", i, 6)
                for h in range(2):
                    dve.wait_ge(a_scored, 2 * i + h + 1)
                    own.add(V.tensor_tensor(scores[:, h:h + 1, :], aux[:, h:h + 1, 0:3 * P],
                                            bias_qk[:, bass.ds(2 * i + h, 1), :], ALU.add))
                    own.settle()
                    own.add(V.tensor_reduce(small[:, 16 + 2 * h:17 + 2 * h], scores[:, h, 0:P], AX_X, ALU.max))
                    own.add(V.tensor_reduce(small[:, 17 + 2 * h:18 + 2 * h], scores[:, h, P:3 * P], AX_X, ALU.max))
                    own.settle()
                    V.tensor_scalar(small[:, 8 + 2 * h:10 + 2 * h], small[:, 16 + 2 * h:18 + 2 * h], -1.0, None,
                                    ALU.mult).then_inc(a_max, 1)
                for h in range(2):
                    dve.wait_ge(a_exp, 4 * i + 2 * h + 2)
                    own.add(V.reciprocal(small[:, 20 + 2 * h:22 + 2 * h], small[:, 12 + 2 * h:14 + 2 * h]))
                    own.settle()
                    own.add(V.tensor_scalar(scores[:, h, 0:P], scores[:, h, 0:P], small[:, 20 + 2 * h:21 + 2 * h], None, ALU.mult))
                    V.tensor_scalar(scores[:, h, P:3 * P], scores[:, h, P:3 * P], small[:, 21 + 2 * h:22 + 2 * h], None,
                                    ALU.mult).then_inc(a_prob, 1)
                for c in range(2):
                    ahead("A", i, 7 + 2 * c)
                    add_group("A", i, 3 + c, sums[:, 0])
                    ahead("A", i, 8 + 2 * c)
                dve.wait_ge(ha_hi, i + 1)
                dst = ha_parts[:, bass.ds(2 * i, 2), :]
                V.tensor_tensor(dst[:, :, S:2 * S], aux[:, 0, :].rearrange("p (h s) -> p h s", h=2),
                                dst[:, :, 0:S].bitcast(F32), ALU.subtract).then_inc(ha_lo, 1)
                ahead("A", i, 11)
                add_group("A", i, 5, sums[:, 0])
            own.leave(A_IT)
            with dve.Fori(0, G_IT) as i:
                for c in range(2):
                    ahead("G", i, 2 * c)
                    ahead("G", i, 2 * c + 1)
                    add_group("G", i, c, sums[:, 0])
            dve.wait_ge(gate_done, 2 * KD)
            with dve.Fori(0, B_IT) as i:
                own.enter(i, 4)
                for c in range(2):
                    for b in range(2):
                        ahead("B", i, 2 * c + b)
                        add_group("B", i, 2 * c + b, sums[:, b])
                        summed("B", i, 2 * c + b)
                        own.add(V.tensor_tensor(sums[:, b], sums[:, b], gates[:, bass.ds(4 * i + 2 * c + b * KD, 2), :], ALU.mult))
                    own.settle()
                    V.tensor_tensor(sums[:, 0], sums[:, 0], sums[:, 1], ALU.add).then_inc(merged_ready, 1)
                    dve.wait_ge(merged_hi, 2 * i + c + 1)
                    dst = merged_parts[:, bass.ds(4 * i + 2 * c, 2), :]
                    V.tensor_tensor(dst[:, :, S:2 * S], sums[:, 0], dst[:, :, 0:S].bitcast(F32), ALU.subtract).then_inc(merged_lo, 1)
                    dve.wait_ge(merged_lo, 2 * i + c + 1)
            own.leave(B_IT)

            with dve.Fori(0, O_IT) as i:
                own.enter(i, 2)
                for c in range(2):
                    ahead("O", i, 2 * c)
                    ahead("O", i, 2 * c + 1)
                    add_group("O", i, c, sums[:, c])
                    for k in range(2):
                        dve.wait_ge(h2_hi, 4 * i + 2 * c + k + 1)
                        dst = h_parts[:, bass.ds(4 * i + 2 * c + k, 1), :]
                        V.scalar_tensor_tensor(dst[:, :, S:2 * S], sums[:, c, k:k + 1, :], vcol(4 * i + 2 * c + k + V_FFN),
                                               dst[:, :, 0:S].bitcast(F32), ALU.mult, ALU.subtract).then_inc(h2_lo, 1)
                    dve.wait_ge(x2_sq, 2 * i + c + 1)
                    own.add(V.tensor_tensor(acc[:], acc[:], squares[:], ALU.add))
                    own.settle()

                for c in range(2):
                    dve.wait_ge(x2_stored[c], 16 * i + 16)
            own.leave(O_IT)
            V.memset(u_conv_in[:, :, 0:2], 0.0).then_inc(acc_ready, 1)
            dve.wait_ge(rms_ready, 1)
            V.reciprocal(r_bc[:], r_bc[:]).then_inc(r_ready, 1)
            own.add(V.memset(acc[:], 0.0))
            own.settle()
            dve.wait_ge(r_ready, 1)
            r_two = r_bc[:].rearrange("p (o s) -> p o s", o=1).to_broadcast([P, 2, S])
            with dve.Fori(0, U_IT) as i:
                own.enter(i, 3)
                ahead("U", i, 0)
                ahead("U", i, 1)
                add_group("U", i, 0, sums[:, 0])
                summed("U", i, 0)
                V.tensor_tensor(u_conv_in[:, :, 2:2 + S], sums[:, 0], r_two, ALU.mult).then_inc(u_scaled, 1)
                for c in range(2):
                    dve.wait_ge(u_tap, 2 * i + c + 1)
                    own.add(V.scalar_tensor_tensor(u_conv_out[:, c, :], u_conv_in[:, c, 1:1 + S], vcol(2 * i + c + V_UW + KF),
                                                   u_conv_out[:, c, :], ALU.mult, ALU.add))
                own.settle()
                V.scalar_tensor_tensor(u_conv_out[:, 0, :], u_conv_in[:, 0, 0:S], vcol(2 * i + V_UW),
                                       u_conv_out[:, 0, :], ALU.mult, ALU.add)
                V.scalar_tensor_tensor(u_conv_out[:, 1, :], u_conv_in[:, 1, 0:S], vcol(2 * i + 1 + V_UW),
                                       u_conv_out[:, 1, :], ALU.mult, ALU.add).then_inc(u_conv, 1)
                ahead("U", i, 2)
                dve.wait_ge(u_conv, i + 1)
                ahead("U", i, 3)
                add_group("U", i, 1, sums[:, 1])
                summed("U", i, 1)
                own.add(V.tensor_tensor(sums[:, 1], sums[:, 1], r_two, ALU.mult))
                own.settle()
                dve.wait_ge(u_silu_done, i + 1)
                V.tensor_tensor(sums[:, 1], sums[:, 1], u_silu[:], ALU.mult).then_inc(u_act, 1)
                dve.wait_ge(act_hi, i + 1)
                dst = act_parts[:, bass.ds(2 * i, 2), :]
                V.tensor_tensor(dst[:, :, S:2 * S], sums[:, 1], dst[:, :, 0:S].bitcast(F32), ALU.subtract).then_inc(act_lo, 1)
                dve.wait_ge(act_lo, i + 1)
            own.leave(U_IT)

            def down(i, last):
                for c in range(2):
                    for k in range(NDT):
                        j = NDT * c + k
                        if not (last and j >= 2 * NDT - AHEAD):
                            ahead("D", i, j)
                    add_group("D", i, c, sums[:, c])
                    summed("D", i, c)
                    dve.wait_ge(x3_in, 16)
                    here = x3[:, bass.ds(4 * i + 2 * c, 2), :]
                    V.tensor_tensor(here, here, sums[:, c], ALU.add).then_inc(x3_ready, 1)
                    dve.wait_ge(x3_sq, 2 * i + c + 1)
                    own.add(V.tensor_tensor(acc[:], acc[:], squares[:], ALU.add))
                    own.settle()
                    for k in range(2):
                        one = x3[:, bass.ds(4 * i + 2 * c + k, 1), :]
                        V.tensor_scalar(one, one, vcol(4 * i + 2 * c + k + V_FIN), None, ALU.mult).then_inc(x3_final, 1)

            with dve.Fori(0, D_IT - 1) as i:
                own.enter(i, 2)
                down(i, False)
            own.leave(D_IT - 1)
            down(D_IT - 1, True)
            dve.wait_ge(fin_rms, 1)
            V.reciprocal(small[:, 4:6], small[:, 2:4]).then_inc(fin_r, 1)
            dve.wait_ge(fin_r, 1)
            for f in range(1, 8, 2):
                tt, q = f // 4, f % 4
                dve.wait_ge(rows_turned, f + 1)
                V.tensor_scalar(rows_out[:, tt, q * 512:(q + 1) * 512], row_bank(f), small[:, 4 + tt:5 + tt], None,
                                ALU.mult).then_inc(rows_v, 1)

        @block.tensor
        def _(pe):
            mm = nc.tensor.matmul

            def multiply(name, i, j, moving, k0, first, last):
                t0, g0, tiles, groups = seg[name]
                kh, c = tile_rows(j, name) // 2, group_of(name, j)
                for f in range(2):
                    pe.wait_ge(lo_ready, 2 * (t0 + j) + f + 1 + i * (2 * tiles))
                    if f == 0 and first and not (isinstance(i, int) and g0 + c - 1 + i * groups <= 0):
                        pe.wait_ge(group_summed, g0 + c - 1 + i * groups)
                    for k in range(kh):
                        for b in range(2):
                            w = parts[:, (2 * j + f) % HALF_SLOTS, k, :, b * P:(b + 1) * P]
                            start, stop = first and f == 0 and k == 0, last and f == 1 and k == kh - 1
                            bank, move = main[:, c % 2, b, :], moving[:, k0 + f * kh + k, :]
                            if stop:
                                mm(bank[:, 0:S], w[:, 1, :], move[:, 0:S], start=False, stop=False)
                                ins = mm(bank, w[:, 0, :], move, start=start, stop=True)
                            else:
                                mm(bank, w[:, 0, :], move, start=start, stop=False)
                                ins = mm(bank[:, 0:S], w[:, 1, :], move[:, 0:S], start=False, stop=False)
                    ins.then_inc(half_used, 1)

            def multiply_rows(name, i, j, k0, first, last):
                t0, g0, tiles, groups = seg[name]
                c = group_of(name, j)
                for f in range(2):
                    pe.wait_ge(lo_ready, 2 * (t0 + j) + f + 1 + i * (2 * tiles))
                    if f == 0 and first:
                        pe.wait_ge(group_summed, g0 + c - 1 + i * groups)
                    for k in range(HALF_K):
                        kk = k0 + f * HALF_K + k
                        for b in range(TT):
                            w = parts[:, (2 * j + f) % HALF_SLOTS, k].rearrange("p a c -> p (a c)")
                            stop, bank = last and f == 1 and k == HALF_K - 1, main[:, c % 2, b, :]
                            hi, lo = (h_parts[:, kk, a * S + b * P:a * S + (b + 1) * P] for a in range(2))
                            if stop:
                                mm(bank[:, 0:COLS], lo, w[:, 0:COLS], start=False, stop=False)
                                ins = mm(bank, hi, w, start=False, stop=True)
                            else:
                                mm(bank, hi, w, start=first and f == 0 and k == 0, stop=False)
                                ins = mm(bank[:, 0:COLS], lo, w[:, 0:COLS], start=False, stop=False)
                    ins.then_inc(half_used, 1)

            def group_of(name, j):
                return j // NDT if name == "D" else j if name == "B" else j // 2

            def project(name, i, c, moving=None):
                for k in range(2):
                    if moving is None:
                        multiply_rows(name, i, 2 * c + k, k * TILE_K, k == 0, k == 1)
                    else:
                        multiply(name, i, 2 * c + k, moving, k * TILE_K, k == 0, k == 1)

            pe.wait_ge(vec_in, 10 * 16)
            pe.wait_ge(pool_const, 4)
            nc.tensor.transpose(aux[:, 3, 0:P], vec_rows[:, 0, :], ident[:])
            nc.tensor.transpose(aux[:, 3, P:P + 2 * KF], vec_rows[0:2 * KF, 1, :], ident[0:2 * KF, 0:2 * KF])
            nc.tensor.transpose(aux[:, 3, P + 2 * KF:P + 4 * KF], vec_rows[0:2 * KF, 2, :],
                                ident[0:2 * KF, 0:2 * KF]).then_inc(vec_t, 1)
            pe.wait_ge(x_scaled, TT)
            for f in range(4):
                if f >= 2:
                    pe.wait_ge(h_lo, 4 * (f - 1))
                for q in range(4):
                    for tt in range(TT):
                        k = 4 * f + q
                        ins = nc.tensor.transpose(main[:, f % 2, q // 2, (q % 2) * S + tt * P:(q % 2) * S + (tt + 1) * P],
                                                  x_rows[:, tt, k * P:(k + 1) * P], ident[:])
                ins.then_inc(x_turned, 1)
            pe.wait_ge(h_lo, KD)
            pe.wait_ge(wif_lo, 1)
            for k in range(KD):
                if k < KD - 1:
                    mm(aux[:, 0, :], wif_parts[:, k, 0, :], h_parts[:, k, :], start=k == 0, stop=False)
                    mm(aux[:, 0, 0:S], wif_parts[:, k, 1, :], h_parts[:, k, 0:S], start=False, stop=False)
                else:
                    mm(aux[:, 0, 0:S], wif_parts[:, k, 1, :], h_parts[:, k, 0:S], start=False, stop=False)
                    ins = mm(aux[:, 0, :], wif_parts[:, k, 0, :], h_parts[:, k, :], start=False, stop=True)
            ins.then_inc(if_done, 1)

            for i in range(M_IT):
                project("M", i, 0, h_parts)
                if i == 0:
                    pe.wait_ge(c_row_ready, 2)
                    for tt in range(TT):
                        ins = nc.tensor.transpose(aux[:, 1, tt * M_H:(tt + 1) * M_H], li_row[:, tt * P:(tt + 1) * P],
                                                  ident[0:M_H, 0:M_H])
                    ins.then_inc(c_turned, 1)
                project("M", i, 1, h_parts)
                if i == 0:
                    pe.wait_ge(hankel_masked, 1)
                    pe.wait_ge(c_ready, 1)
                    for h in range(A_H):
                        for b in range(2):
                            ins = mm(aux[:, h // 2, (h % 2) * S + b * P:(h % 2) * S + (b + 1) * P], hankel[:, h, b, :], anti[:],
                                     start=True, stop=True)
                        if h % 2:
                            ins.then_inc(bias_mm, 1)
                project("M", i, 2)
                project("M", i, 3)
                pe.wait_ge(mqk_ready, 2 * i + 2)
                pe.wait_ge(bias_ready, 8)
                for h in range(2):
                    mm(aux[:, h, 0:S], mk[:, h, 0:P], mq[:, h, :], start=True, stop=True)
                    mm(aux[:, h, S:S + P], mk[:, h, P:S], mq[:, h, P:S], start=True, stop=True)
                    hd = 2 * i + h
                    mm(aux[:, 2 + h, 0:S], pick[:, hd, :], g_row[:], start=True, stop=False)
                    mm(aux[:, 2 + h, 0:P], ident[:], future[:], start=False, stop=True)
                    mm(aux[:, 2 + h, S:S + P], pick[:, hd, :], g_row[:, P:S], start=True, stop=False)
                    mm(aux[:, 2 + h, S:S + P], ident[:], future[:], start=False, stop=True).then_inc(mqk_done, 1)
                project("M", i, 4, h_parts)
                pe.wait_ge(group_summed, 6 * i + 4)
                for h in range(2):
                    pe.wait_ge(mprob_ready, 2 * i + h + 1)
                    for v in range(2):
                        dst = aux[:, h, v * S:(v + 1) * S]
                        cols = slice(h * DV + v * P, h * DV + (v + 1) * P)
                        mm(dst, mv[:, 0, cols], mprobs[:, h, 0:S], start=True, stop=False)
                        mm(dst[:, P:S], mv[:, 1, cols], mprobs[:, h, S:S + P], start=False, stop=True)
                    mm(aux[:, 2 + h, 0:S], ones[:, 0:P], mprobs[:, h, 0:S], start=True, stop=False)
                    mm(aux[:, 2 + h, P:S], ones[:, 0:P], mprobs[:, h, S:S + P], start=False, stop=True)
                    mm(aux[:, 2 + h, S:2 * S], pick[:, 2 * i + h, :], m_row[:], start=True, stop=True).then_inc(mnum_done, 1)
                project("M", i, 5, h_parts)
                for h in range(2):
                    pe.wait_ge(hsq_ready, 2 * i + h + 1)
                    mm(aux[:, 2, h * S:(h + 1) * S], ones[:, 0:P], hsq[:, h, 0, :], start=True, stop=False)
                    ins = mm(aux[:, 2, h * S:(h + 1) * S], ones[:, 0:P], hsq[:, h, 1, :], start=False, stop=True)
                ins.then_inc(mss_done, 1)

            with pe.Fori(0, A_IT) as i:
                project("A", i, 0, h_parts)
                project("A", i, 1, h_parts)
                project("A", i, 2)
                pe.wait_ge(group_summed, seg["A"][1] + 3 + 6 * i)
                for h in range(2):
                    mm(aux[:, h, 0:P], aq[:, h, 0:P], ak[:, h, 0:P], start=True, stop=True)
                    mm(aux[:, h, P:3 * P], aq[:, h, P:S], ak[:, h, :], start=True, stop=True).then_inc(a_scored, 1)
                project("A", i, 3, h_parts)
                for h in range(2):
                    pe.wait_ge(a_prob, 2 * i + h + 1)
                    for q in range(3):
                        ins = nc.tensor.transpose(aux[:, 2 + h, q * P:(q + 1) * P], scores[:, h, q * P:(q + 1) * P], ident[:])
                    ins.then_inc(a_turned, 1)
                project("A", i, 4, h_parts)
                pe.wait_ge(a_copied, 2 * i + 2)
                for h in range(2):
                    dst = aux[:, 0, h * S:(h + 1) * S]
                    mm(dst, av[:, 0, h * P:(h + 1) * P], probs_t[:, h, 0:S], start=True, stop=False)
                    ins = mm(dst[:, P:S], av[:, 1, h * P:(h + 1) * P], probs_t[:, h, S:S + P], start=False, stop=True)
                ins.then_inc(a_out, 1)
                project("A", i, 5, h_parts)
            with pe.Fori(0, G_IT) as i:
                for c in range(2):
                    project("G", i, c, h_parts)
            pe.wait_ge(hm_lo, M_H)
            pe.wait_ge(ha_lo, A_IT)
            with pe.Fori(0, B_IT) as i:
                for j in range(4):
                    multiply("B", i, j, ha_parts if j % 2 else hm_parts, 0, True, True)
            with pe.Fori(0, O_IT) as i:
                for c in range(2):
                    if c == 0:
                        pe.wait_ge(merged_lo, B_IT)
                    multiply("O", i, 2 * c, merged_parts, 0, True, False)
                    if c == 0:
                        pe.wait_ge(merged_lo, 2 * B_IT)
                    pe.wait_ge(xs_copied, 2 * i + c + 1)
                    for b in range(2):
                        for tt in range(TT):
                            mm(main[:, c % 2, b, tt * P:(tt + 1) * P], x_stage[:, tt, b * P:(b + 1) * P], ident[:],
                               start=False, stop=False, skip_group_check=True)
                    multiply("O", i, 2 * c + 1, merged_parts, TILE_K, False, True)
            pe.wait_ge(h2_lo, KD // 2)
            multiply("U", 0, 0, h_parts, 0, True, False)
            pe.wait_ge(acc_ready, 1)
            mm(aux[:, 0, 0:S], ones[:, 0:P], acc[:, 0, :], start=True, stop=False)
            mm(aux[:, 0, 0:S], ones[:, 0:P], acc[:, 1, :], start=False, stop=True).then_inc(ss_done, 1)
            pe.wait_ge(h2_lo, KD)
            multiply("U", 0, 1, h_parts, TILE_K, False, True)
            project("U", 0, 1, h_parts)
            with pe.Fori(1, U_IT) as i:
                for c in range(2):
                    project("U", i, c, h_parts)
            pe.wait_ge(act_lo, U_IT - 2)
            with pe.Fori(0, D_IT) as i:
                for c in range(2):
                    for k in range(NDT):
                        if c == 0 and k == NDT - 1:
                            pe.wait_ge(act_lo, U_IT)
                        multiply("D", i, NDT * c + k, act_parts, k * TILE_K, k == 0, k == NDT - 1)
            pe.wait_ge(x3_final, KD)
            for tt in range(TT):
                for a in range(2):
                    ins = mm(aux[:, 3, tt:tt + 1], acc[:, a, tt * P:(tt + 1) * P], ones[:, 0:1], start=a == 0, stop=a == 1)
            ins.then_inc(fin_ss, 1)
            for f in range(8):
                tt, q = f // 4, f % 4
                if f == 7:
                    pe.wait_ge(fin_rms, 1)
                for c in range(4):
                    ins = nc.tensor.transpose(row_bank(f)[:, c * P:(c + 1) * P], x3[:, 4 * q + c, tt * P:(tt + 1) * P], ident[:])
                ins.then_inc(rows_turned, 1)


_INS = ["x", "norm_mix", "w_in", "conv_qk_w", "conv_qk_b", "b_igate", "b_fgate", "m_norm", "rel_bias", "gate_bias",
        "w_branch_m", "w_branch_a", "w_out", "norm_ffn", "w_up", "conv_ffn_w", "conv_ffn_b", "w_down", "norm_final"]


def kernel(**inputs):
    import numpy as _np
    import concourse.bacc as _bacc
    from concourse import mybir as _mybir
    from concourse.bass_utils import run_bass_kernel_spmd as _run

    nc = _bacc.Bacc("TRN2", target_bir_lowering=False, num_devices=1)
    arrays, args = {}, []
    for name in _INS:
        a = _np.ascontiguousarray(inputs[name])
        arrays[f"in_{name}_dram"] = a
        args.append(nc.dram_tensor(f"in_{name}_dram", a.shape, _mybir.dt.from_np(a.dtype), kind="ExternalInput").ap())
    shape = arrays["in_x_dram"].shape
    args.append(nc.dram_tensor("out_0_dram", shape, _mybir.dt.float32, kind="ExternalOutput").ap())
    hybrid_block(nc, *args)
    r = _run(nc, [arrays], core_ids=[0])
    return r.results[0]["out_0_dram"]
```

```python
from contextlib import ExitStack

import concourse.bass as bass
from concourse import mybir

F32 = mybir.dt.float32
F32R = mybir.dt.float32r
ALU = mybir.AluOpType
ACT = mybir.ActivationFunctionType
AX_X = mybir.AxisListType.X

P = 128
CHUNK = 64
EPS = 1e-6
BIG = 1e30
COLS = 256
TILE_K = 8
AHEAD = 2
HALF_K = TILE_K // 2
RAW_SLOTS = 4
HALF_SLOTS = 2 * AHEAD


class OwnSteps:

    def __init__(self, eng, sem):
        self.eng, self.sem, self.base, self.count = eng, sem, 0, 0

    def add(self, ins):
        ins.then_inc(self.sem, 1)
        self.count += 1

    def settle(self):
        self.eng.wait_ge(self.sem, self.base + self.count)

    def enter(self, i, per):
        self.loop_base, self.per = self.base + self.count, per
        self.base, self.count = self.loop_base + i * per, 0

    def leave(self, times):
        assert self.count == self.per, (self.count, self.per)
        self.base, self.count = self.loop_base + times * self.per, 0


def hybrid_block(nc, x, norm_mix, w_in, conv_qk_w, conv_qk_b, b_igate, b_fgate, m_norm, rel_bias, gate_bias,
                 w_branch_m, w_branch_a, w_out, norm_ffn, w_up, conv_ffn_w, conv_ffn_b, w_down, norm_final, out):
    _, S, D = x.shape
    D_FF = w_down.shape[1]
    M_H = b_igate.shape[1]
    M_V = m_norm.shape[1]
    M_QK = conv_qk_w.shape[2] // 2
    DK, DV = M_QK // M_H, M_V // M_H
    A_H = rel_bias.shape[1]
    A_W = w_branch_a.shape[1]
    DH = A_W // A_H
    REL = rel_bias.shape[2]
    A_MAX_REL = REL // 2
    TT = S // P
    KD, KV, KF = D // P, M_V // P, D_FF // P
    assert (S, DK, DV, DH, TT, M_H, A_H, COLS) == (256, P, 2 * P, P, 2, 4, 8, S)
    assert KV == A_W // P == TILE_K and KD == 2 * TILE_K and KF % 4 == 0 and A_MAX_REL == P
    offset = {}
    at = 0
    for name, width in (("mq", M_QK), ("mk", M_QK), ("mv", M_V), ("mo", M_V), ("mi", M_H), ("mf", M_H),
                        ("aq", A_W), ("ak", A_W), ("av", A_W), ("gates", 2 * D)):
        offset[name] = at
        at += width
    assert at == w_in.shape[2]

    DOWN_TILES = [TILE_K] * (KF // TILE_K) + [KF % TILE_K]
    NDT = len(DOWN_TILES)
    M_IT, A_IT, G_IT, B_IT, O_IT, U_IT, D_IT = 2, A_H // 2, 2, 4, 4, D_FF // COLS, 4
    seg, t, g = {}, 0, 0
    for name, times, tiles, groups in (("M", M_IT, 12, 6), ("A", A_IT, 12, 6), ("G", G_IT, 4, 2), ("B", B_IT, 4, 4),
                                       ("O", O_IT, 4, 2), ("U", U_IT, 4, 2), ("D", D_IT, 2 * NDT, 2)):
        seg[name] = (t, g, tiles, groups)
        assert t % RAW_SLOTS == 0 and g % 2 == 0
        t, g = t + times * tiles, g + times * groups
    LAST_TILE, LAST_GROUP = t, g
    A_GATES = 3 * A_IT

    def place(name, i):
        t0, g0, tiles, groups = seg[name]
        return t0 + i * tiles, g0 + i * groups

    tpad = nc.dram_tensor("tpad_scratch", (A_H, 3 * P), F32, kind="Internal")
    x2_dram = nc.dram_tensor("x2_scratch", (P, KD * S), F32, kind="Internal").ap()

    with ExitStack() as ctx:
        def sb(name, shape, dt=F32):
            return ctx.enter_context(nc.sbuf_tensor(name, shape, dt))

        def sem(name):
            return ctx.enter_context(nc.semaphore(name))

        def region(kib, *sets):
            made = []
            for one in sets:
                with ExitStack() as s:
                    made += [s.enter_context(nc.sbuf_tensor(n, shape, dt)) for n, shape, dt in one]
            ctx.enter_context(nc.sbuf_tensor(f"hold_{made[0].name}", [P, kib * 256], F32))
            return made

        raw, rows_out = region(32, [("raw", [P, RAW_SLOTS, TILE_K, COLS], F32)], [("rows_out", [P, TT, D], F32)])
        parts = sb("parts", [P, HALF_SLOTS, HALF_K, 2, COLS], F32R)
        h_parts, x3 = region(32, [("h_parts", [P, KD, 2 * S], F32R)], [("x3", [P, KD, S], F32)])
        hm_size, ga_size = KV * 2 * S, 2 * KD * S
        stages = region(
            96,
            [("hm_parts", [P, KV, 2 * S], F32R), ("hold_a", [P, hm_size + ga_size], F32),
             ("merged_parts", [P, KD, 2 * S], F32R)],
            [("hold_b", [P, hm_size], F32), ("ha_parts", [P, KV, 2 * S], F32R), ("gates", [P, 2 * KD, S], F32),
             ("x_rows", [P, TT, D], F32), ("wif_raw", [P, KD, P], F32), ("vec_rows", [P, 3, P], F32),
             ("rel_rows", [A_H, 3 * P], F32)],
            [("junk", [P, D], F32), ("if_low_sb", [64, S], F32), ("if_sum", [64, S], F32), ("li_row", [M_H, S], F32),
             ("z_row", [M_H, S], F32), ("abs_row", [M_H, S], F32), ("log_row", [M_H, S], F32),
             ("if_bias", [64, 8], F32), ("hold_c", [P, 2 * hm_size - D - 6 * S - 8], F32),
             ("x_again", [P, D // COLS, TT, COLS], F32), ("x_stage", [P, TT, 2 * P], F32),
             ("hold_d", [P, ga_size - TT * D - 2 * S], F32), ("bias_qk", [P, A_H, 3 * P], F32),
             ("hankel", [P, A_H, 2, P], F32), ("aq", [P, 2, S], F32), ("ak", [P, 2, S], F32), ("av", [P, TT, 2 * P], F32),
             ("scores", [P, 2, 3 * P], F32), ("probs_t", [P, 2, 3 * P], F32)],
            [("hold_e", [P, hm_size], F32), ("mo_sum", [P, 2, 2, S], F32), ("conv_in", [P, 2, S + 4], F32),
             ("hold_f", [P, hm_size - 4 * S - 2 * (S + 4)], F32),
             ("mv", [P, TT, 2 * DV], F32), ("conv_out", [P, 2, S], F32), ("mq", [P, 2, S], F32), ("mk", [P, 2, S], F32),
             ("decay", [P, 2, 3 * P], F32), ("mprobs", [P, 2, 3 * P], F32), ("inv", [P, 2, S], F32),
             ("hval", [P, 2, 2, S], F32), ("hsq", [P, 2, 2, S], F32), ("pick", [M_H, M_H, P], F32),
             ("g_row", [M_H, S], F32), ("m_row", [M_H, S], F32), ("future", [P, P], F32), ("anti", [P, P], F32)],
            [("hold_g", [P, 2 * hm_size + TT * 2 * DV + 6 * S], F32), ("wif_parts", [P, KD, 2, P], F32R)],
            [("act_parts", [P, KF, 2 * S], F32R), ("u_conv_in", [P, 2, S + 2], F32), ("u_conv_out", [P, 2, S], F32),
             ("u_silu", [P, 2, S], F32)])
        named = {r.name: r for r in stages}
        hm_parts, ha_parts, gates, merged_parts = (named[n] for n in ("hm_parts", "ha_parts", "gates", "merged_parts"))
        x_rows, wif_raw, wif_parts, x_again, x_stage = (named[n] for n in ("x_rows", "wif_raw", "wif_parts", "x_again", "x_stage"))
        vec_rows, rel_rows, junk, if_low_sb, if_sum = (named[n] for n in ("vec_rows", "rel_rows", "junk", "if_low_sb", "if_sum"))
        li_row, z_row, abs_row, log_row, if_bias = (named[n] for n in ("li_row", "z_row", "abs_row", "log_row", "if_bias"))
        bias_qk, hankel, aq, ak, av = (named[n] for n in ("bias_qk", "hankel", "aq", "ak", "av"))
        scores, probs_t, mo_sum, conv_in, mv = (named[n] for n in ("scores", "probs_t", "mo_sum", "conv_in", "mv"))
        conv_out, mq, mk, decay, mprobs = (named[n] for n in ("conv_out", "mq", "mk", "decay", "mprobs"))
        inv, hval, hsq, pick, g_row, m_row = (named[n] for n in ("inv", "hval", "hsq", "pick", "g_row", "m_row"))
        future, anti = (named[n] for n in ("future", "anti"))
        act_parts, u_conv_in, u_conv_out, u_silu = (named[n] for n in ("act_parts", "u_conv_in", "u_conv_out", "u_silu"))

        ident = sb("ident", [P, P])
        ones = sb("ones", [P, S])
        lows = sb("lows", [P, 2, 2, S])
        sums = sb("sums", [P, 2, 2, S])
        squares = sb("squares", [P, 2, S])
        acc = sb("acc", [P, 2, S])
        r_bc = sb("r_bc", [P, S])
        vec = sb("vec", [P, P + 4 * KF])
        small = sb("small", [P, 32 + TT * M_H])
        ccol = small[:, 32:32 + TT * M_H]
        main = ctx.enter_context(nc.psum_tensor("main", [P, 2, 2, 512], F32))
        aux = ctx.enter_context(nc.psum_tensor("aux", [P, 4, 512], F32))

        def row_bank(f):
            return main[:, f // 2, f % 2, :] if f < 4 else aux[:, f - 4, :]

        x_in = [sem(f"x_in{k}") for k in range(2 * TT)]
        w_loaded = [sem(f"w_loaded{k}") for k in range(RAW_SLOTS)]
        mix_in, vec_in, wif_in, rel_in, tpad_out, hankel_in = (
            sem(n) for n in ("mix_in", "vec_in", "wif_in", "rel_in", "tpad_out", "hankel_in"))
        x3_in, rows_stored = (sem(n) for n in ("x3_in", "rows_stored"))
        x_again_in = [sem(f"x_again_in{k}") for k in range(2)]
        x2_stored = [sem(f"x2_stored{k}") for k in range(2)]
        hi_ready, lo_ready, half_used, low_copied, group_summed = (
            sem(n) for n in ("hi_ready", "lo_ready", "half_used", "low_copied", "group_summed"))
        pool_const, wif_hi, wif_lo, vec_t, vec_ready, rel_pad = (
            sem(n) for n in ("pool_const", "wif_hi", "wif_lo", "vec_t", "vec_ready", "rel_pad"))
        x_sq, x_ss, x_rms, diag_ready, x_turned, h_hi, h_lo = (
            sem(n) for n in ("x_sq", "x_ss", "x_rms", "diag_ready", "x_turned", "h_hi", "h_lo"))
        if_done, if_low, z_ready, log_term, c_row_ready, c_turned, c_ready, hankel_masked, bias_mm, bias_ready = (
            sem(n) for n in ("if_done", "if_low", "z_ready", "log_term", "c_row_ready", "c_turned", "c_ready",
                            "hankel_masked", "bias_mm", "bias_ready"))
        first_tap, conv_done, mqk_ready, mqk_done, decay_ready, mprob_ready, mnum_done, floor_ready = (
            sem(n) for n in ("first_tap", "conv_done", "mqk_ready", "mqk_done", "decay_ready", "mprob_ready",
                            "mnum_done", "floor_ready"))
        h_ready, hsq_ready, mss_done, mrms_ready, mo_ready, hm_ready, hm_hi, hm_lo, eps_ready = (
            sem(n) for n in ("h_ready", "hsq_ready", "mss_done", "mrms_ready", "mo_ready", "hm_ready", "hm_hi", "hm_lo",
                            "eps_ready"))
        a_scored, a_max, a_exp, a_prob, a_turned, a_copied, a_out, ha_hi, ha_lo, gate_done = (
            sem(n) for n in ("a_scored", "a_max", "a_exp", "a_prob", "a_turned", "a_copied", "a_out", "ha_hi", "ha_lo",
                            "gate_done"))
        merged_ready, merged_hi, merged_lo, xs_copied, x2_sq, h2_hi, h2_lo, acc_ready, ss_done, rms_ready, r_ready = (
            sem(n) for n in ("merged_ready", "merged_hi", "merged_lo", "xs_copied", "x2_sq", "h2_hi", "h2_lo",
                            "acc_ready", "ss_done", "rms_ready", "r_ready"))
        u_scaled, u_tap, u_conv, u_act, u_silu_done, act_hi, act_lo = (
            sem(n) for n in ("u_scaled", "u_tap", "u_conv", "u_act", "u_silu_done", "act_hi", "act_lo"))
        x3_ready, x3_sq, x3_final, fin_ss, fin_rms, fin_r, rows_turned, rows_a, rows_v = (
            sem(n) for n in ("x3_ready", "x3_sq", "x3_final", "fin_ss", "fin_rms", "fin_r", "rows_turned", "rows_a",
                            "rows_v"))
        act_own, dve_own, pool_own = sem("act_own"), sem("dve_own"), sem("pool_own")

        V_MIX, V_FFN, V_FIN, V_CW, V_CB, V_MN, V_GB = 0, 16, 32, 48, 80, 88, 96
        V_UW, V_UB = P, P + 3 * KF

        def vcol(c):
            return vec[:, bass.ds(c, 1)]

        def turn_bank(k):
            return (main[:, 1, k % 6, :] if k % 6 < 2 else aux[:, k % 6 - 2, :])[:, 0:S]

        diag = r_bc[:].rearrange("p (t q) -> p t q", t=TT)

        block = ctx.enter_context(nc.Block())

        def tile_rows(j_in_seg, name):
            return DOWN_TILES[j_in_seg % NDT] if name == "D" else TILE_K

        @block.sync
        def _(sp):
            xr = x[0].rearrange("(t p) d -> p t d", p=P)
            sp.dma_start(vec_rows[V_MIX:V_MIX + KD, 0, :], norm_mix[0].rearrange("(r p) -> r p", p=P)).then_inc(mix_in, 16)
            for k in range(2 * TT):
                tt, half = k % 2, slice(k // 2 * (D // 2), (k // 2 + 1) * (D // 2))
                sp.dma_start(x_rows[:, tt, half], xr[:, tt, half]).then_inc(x_in[k], 16)

            def load(n, j, w, k0, kn, col):
                if not (isinstance(n, int) and n < RAW_SLOTS):
                    sp.wait_ge(lo_ready, 2 * (n - RAW_SLOTS + 1))
                src = w[0, k0 * P:(k0 + kn) * P, bass.ds(col, COLS)].rearrange("(k p) c -> p k c", p=P)
                sp.dma_start(raw[:, j % RAW_SLOTS, 0:kn, :], src).then_inc(w_loaded[j % RAW_SLOTS], 16)

            def load_group(n, j, w, col, count=2):
                for k in range(count):
                    load(n + k, j + k, w, k * TILE_K, TILE_K, col)

            for i in range(M_IT):
                n, _ = place("M", i)
                for c, col in enumerate((offset["mq"] + i * COLS, offset["mk"] + i * COLS,
                                         offset["mv"] + 2 * i * COLS, offset["mv"] + (2 * i + 1) * COLS,
                                         offset["mo"] + 2 * i * COLS, offset["mo"] + (2 * i + 1) * COLS)):
                    load_group(n + 2 * c, 2 * c, w_in, col)
            with sp.Fori(0, A_IT) as i:
                n, _ = place("A", i)
                for c, name in enumerate(("aq", "ak", "av")):
                    load_group(n + 2 * c, 2 * c, w_in, offset[name] + i * COLS)
                for c in range(3):
                    load_group(n + 6 + 2 * c, 6 + 2 * c, w_in, offset["gates"] + (3 * i + c) * COLS)
            with sp.Fori(0, G_IT) as i:
                n, _ = place("G", i)
                for c in range(2):
                    load_group(n + 2 * c, 2 * c, w_in, offset["gates"] + A_GATES * COLS + (2 * i + c) * COLS)
            with sp.Fori(0, B_IT) as i:
                n, _ = place("B", i)
                for c in range(2):
                    load_group(n + 2 * c, 2 * c, w_branch_m, (2 * i + c) * COLS, 1)
                    load_group(n + 2 * c + 1, 2 * c + 1, w_branch_a, (2 * i + c) * COLS, 1)
            with sp.Fori(0, O_IT) as i:
                n, _ = place("O", i)
                for c in range(2):
                    load_group(n + 2 * c, 2 * c, w_out, (2 * i + c) * COLS)
            with sp.Fori(0, U_IT) as i:
                n, _ = place("U", i)
                load_group(n, 0, w_up, i * COLS)
                load_group(n + 2, 2, w_up, D_FF + i * COLS)
            with sp.Fori(0, D_IT) as i:
                n, _ = place("D", i)
                for c in range(2):
                    for k, kn in enumerate(DOWN_TILES):
                        load(n + NDT * c + k, NDT * c + k, w_down, k * TILE_K, kn, (2 * i + c) * COLS)
            outr = out[0].rearrange("(t p) d -> p t d", p=P)
            for f in range(8):
                tt, q = f // 4, f % 4
                sp.wait_ge(rows_a if f % 2 == 0 else rows_v, f // 2 + 1)
                sp.dma_start(outr[:, tt, q * 512:(q + 1) * 512], rows_out[:, tt, q * 512:(q + 1) * 512]).then_inc(rows_stored, 16)
            sp.wait_ge(rows_stored, 8 * 16)

        @block.gpsimd
        def _(pool):
            own = OwnSteps(pool, pool_own)
            own.add(nc.gpsimd.memset(ident[:], 0.0))
            own.settle()
            nc.gpsimd.affine_select(out=ident[:], in_=ident[:], compare_op=ALU.not_equal, fill=1.0, base=0,
                                    pattern=[[-1, P]], channel_multiplier=1).then_inc(pool_const, 1)
            own.add(nc.gpsimd.memset(wif_raw[:], 0.0))
            own.settle()
            wi = w_in[0].rearrange("(k p) c -> p k c", p=P)
            with nc.allow_non_contiguous_dma(reason="four columns of each gate"):
                pool.dma_start(wif_raw[:, :, 0:M_H], wi[:, :, offset["mi"]:offset["mi"] + M_H]).then_inc(wif_in, 16)
                pool.dma_start(wif_raw[:, :, 32:32 + M_H], wi[:, :, offset["mf"]:offset["mf"] + M_H]).then_inc(wif_in, 16)
                pool.dma_start(if_bias[0:M_H, 0:1], b_igate.rearrange("a h -> h a")).then_inc(wif_in, 16)
                pool.dma_start(if_bias[32:32 + M_H, 0:1], b_fgate.rearrange("a h -> h a")).then_inc(wif_in, 16)
            pool.dma_start(rel_rows[:, 0:REL], rel_bias[0]).then_inc(rel_in, 16)
            for buf, value in ((anti, 0.0), (future, 0.0), (pick, 0.0), (ones, 1.0)):
                own.add(nc.gpsimd.memset(buf[:], value))
            own.settle()
            nc.gpsimd.affine_select(out=anti[:], in_=anti[:], compare_op=ALU.not_equal, fill=1.0, base=1 - P,
                                    pattern=[[1, P]], channel_multiplier=1).then_inc(pool_const, 1)
            nc.gpsimd.affine_select(out=future[:], in_=future[:], compare_op=ALU.is_ge, fill=BIG, base=0,
                                    pattern=[[1, P]], channel_multiplier=-1).then_inc(pool_const, 1)
            nc.gpsimd.affine_select(out=pick[:], in_=pick[:], compare_op=ALU.not_equal, fill=1.0, base=0,
                                    pattern=[[-1, M_H], [0, P]], channel_multiplier=1).then_inc(pool_const, 1)
            pool.wait_ge(rel_pad, 1)
            pool.dma_start(tpad.ap(), rel_rows[:]).then_inc(tpad_out, 16)
            pool.wait_ge(tpad_out, 16)
            pool.wait_ge(x_turned, KD)
            pool.wait_ge(wif_lo, 1)
            for b in range(2):
                src = bass.AP(tensor=tpad, offset=1 + P * b, ap=[[1, P], [3 * P, A_H], [1, P]])
                pool.dma_start(hankel[:, :, b, :], src).then_inc(hankel_in, 16)
            pool.wait_ge(hankel_in, 32)
            nc.gpsimd.memset(hankel[0:CHUNK, :, 0, 0:CHUNK], -BIG).then_inc(hankel_masked, 1)
            for half in range(2):
                pool.wait_ge(merged_ready, (half + 1) * B_IT)
                for tt in range(TT):
                    pool.dma_start(x_again[:, half * B_IT:(half + 1) * B_IT, tt, :],
                                   x[0, tt * P:(tt + 1) * P, half * (D // 2):(half + 1) * (D // 2)].rearrange(
                                       "p (m c) -> p m c", c=COLS)).then_inc(x_again_in[half], 16)
            with pool.Fori(0, O_IT) as i:
                _, g = place("O", i)
                for c in range(2):
                    pool.wait_ge(group_summed, g + c + 1)
                    pool.dma_start(x2_dram[:, bass.ds((2 * i + c) * 2 * S, 2 * S)],
                                   sums[:, c].rearrange("p a s -> p (a s)")).then_inc(x2_stored[c], 16)
            for c in range(2):
                pool.wait_ge(x2_stored[c], O_IT * 16)
            pool.wait_ge(half_used, 2 * seg["D"][0])
            pool.dma_start(x3[:].rearrange("p k s -> p (k s)"), x2_dram).then_inc(x3_in, 16)

        @block.scalar
        def _(act):
            own = OwnSteps(act, act_own)
            A = nc.scalar.activation
            for r0, ap in ((V_FFN, norm_ffn[0].rearrange("(r p) -> r p", p=P)),
                           (V_FIN, norm_final.rearrange("(r p) -> r p", p=P)),
                           (V_CW, conv_qk_w[0].rearrange("k (r p) -> (k r) p", p=P)),
                           (V_CB, conv_qk_b[0].rearrange("(r p) -> r p", p=P)), (V_MN, m_norm[0].rearrange("(r p) -> r p", p=P)),
                           (V_GB, gate_bias[0].rearrange("k (r p) -> (k r) p", p=P))):
                act.dma_start(vec_rows[r0:r0 + ap.shape[0], 0, :], ap).then_inc(vec_in, 16)
            cw = conv_ffn_w[0].rearrange("k (r p) -> (k r) p", p=P)
            act.dma_start(vec_rows[0:2 * KF, 1, :], cw[0:2 * KF, :]).then_inc(vec_in, 16)
            act.dma_start(vec_rows[0:KF, 2, :], cw[2 * KF:3 * KF, :]).then_inc(vec_in, 16)
            act.dma_start(vec_rows[KF:2 * KF, 2, :], conv_ffn_b[0].rearrange("(r p) -> r p", p=P)).then_inc(vec_in, 16)

            def ahead(name, i, j):
                t0, _, tiles, _ = seg[name]
                slot, kh = (j + AHEAD) % RAW_SLOTS, tile_rows(j + AHEAD, name) // 2
                act.wait_ge(w_loaded[slot], 16 * ((t0 + j + AHEAD) // RAW_SLOTS + 1) + i * (16 * tiles // RAW_SLOTS))
                for f in range(2):
                    act.wait_ge(half_used, 2 * (t0 + j) + f + 1 + i * (2 * tiles))
                    A(parts[:, (2 * j + f) % HALF_SLOTS, 0:kh, 0, :], raw[:, slot, f * kh:(f + 1) * kh, :],
                      ACT.Copy).then_inc(hi_ready, 1)

            def copy_low(name, i, c, last_j, scale=1.0):
                t0, g0, tiles, groups = seg[name]
                act.wait_ge(half_used, 2 * (t0 + last_j + 1) + i * (2 * tiles))
                A(lows[:, c % 2], main[:, c % 2, :, S:2 * S], ACT.Copy, scale=scale).then_inc(low_copied, 1)

            def summed(name, i, c):
                _, g0, _, groups = seg[name]
                act.wait_ge(group_summed, g0 + c + 1 + i * groups)

            act.wait_ge(eps_ready, 1)
            own.add(A(small[:, 30:31], small[:, 31:32], ACT.Sqrt))
            for k in range(2 * TT):
                tt, half = k % 2, slice(k // 2 * (D // 2), (k // 2 + 1) * (D // 2))
                act.wait_ge(x_in[k], 16)
                if k >= 2:
                    act.wait_ge(x_sq, k - 1)
                A(junk[:, tt * (D // 2):(tt + 1) * (D // 2)], x_rows[:, tt, half], ACT.Square,
                  accum_out=small[:, k:k + 1]).then_inc(x_sq, 1)
            act.wait_ge(x_ss, 1)
            A(small[:, 6:8], small[:, 4:6], ACT.Sqrt, bias=small[:, 31:32], scale=1.0 / D).then_inc(x_rms, 1)
            act.wait_ge(vec_t, 1)
            A(vec[:, V_MIX:V_MIX + KD], aux[:, 3, 0:KD], ACT.Copy).then_inc(vec_ready, 1)
            act.wait_ge(vec_ready, 1)
            for q in range(4):
                for k in range(4 * q, 4 * q + 4):
                    act.wait_ge(x_turned, k + 1)
                    A(h_parts[:, k, 0:S], turn_bank(k), ACT.Copy, scale=vcol(V_MIX + k)).then_inc(h_hi, 1)
                j, f = q // 2, q % 2
                if f == 0:
                    act.wait_ge(w_loaded[j], 16)
                A(parts[:, q, :, 0, :], raw[:, j, f * HALF_K:(f + 1) * HALF_K], ACT.Copy).then_inc(hi_ready, 1)
            act.wait_ge(wif_in, 4 * 16)
            A(wif_parts[:, :, 0, :], wif_raw[:], ACT.Copy).then_inc(wif_hi, 1)

            def gates_low():
                act.wait_ge(if_done, 1)
                A(if_low_sb[:], aux[0:64, 0, S:2 * S], ACT.Copy).then_inc(if_low, 1)

            def gates_log():
                act.wait_ge(z_ready, 1)
                own.add(A(abs_row[:], z_row[:], ACT.Abs))
                own.settle()
                own.add(A(log_row[:], abs_row[:], ACT.Exp, scale=-1.0))
                own.settle()
                A(log_row[:], log_row[:], ACT.Ln, bias=1.0).then_inc(log_term, 1)

            def turn_c():
                act.wait_ge(c_turned, 1)
                A(ccol, aux[:, 1, 0:TT * M_H], ACT.Copy).then_inc(c_ready, 1)

            def bias_copies():
                for b in range(4):
                    act.wait_ge(bias_mm, b + 1)
                    src = aux[:, b, :].rearrange("p (h c) -> p h c", h=2)
                    A(bias_qk[:, 2 * b:2 * b + 2, 0:2 * P], src, ACT.Copy).then_inc(bias_ready, 1)
                    A(bias_qk[:, 2 * b:2 * b + 2, 2 * P:3 * P], src[:, :, 0:P], ACT.Copy).then_inc(bias_ready, 1)

            for i in range(M_IT):
                def first_taps(which):
                    summed("M", i, which)
                    for c in range(2):
                        ch = M_H * which + 2 * i + c
                        A(conv_out[:, c, :], conv_in[:, c, 4:4 + S], ACT.Identity, scale=vcol(V_CW + 3 * 8 + ch),
                          bias=vcol(V_CB + ch)).then_inc(first_tap, 1)

                def conv_silu(which):
                    act.wait_ge(conv_done, 2 * i + which + 1)
                    A((mq, mk)[which][:], conv_out[:], ACT.Silu).then_inc(mqk_ready, 1)

                def decays():
                    for h in range(2):
                        act.wait_ge(mqk_done, 2 * i + h + 1)
                        hd = 2 * i + h
                        own.add(A(decay[:, h, 0:S], aux[:, 2 + h, 0:S], ACT.Exp, bias=ccol[:, hd:hd + 1], scale=-1.0))
                        A(decay[:, h, S:S + P], aux[:, 2 + h, S:S + P], ACT.Exp, bias=ccol[:, M_H + hd:M_H + hd + 1],
                          scale=-1.0).then_inc(decay_ready, 1)

                ahead("M", i, 0)
                ahead("M", i, 1)
                copy_low("M", i, 0, 1)
                if i == 0:
                    act.wait_ge(vec_t, 2)
                    A(vec[:, KD:P + 4 * KF], aux[:, 3, KD:P + 4 * KF], ACT.Copy).then_inc(vec_ready, 1)
                    act.wait_ge(vec_ready, 2)
                first_taps(0)
                ahead("M", i, 2)
                conv_silu(0)
                if i == 0:
                    gates_low()
                else:
                    bias_copies()
                ahead("M", i, 3)
                if i == 0:
                    gates_log()
                copy_low("M", i, 1, 3)
                first_taps(1)
                ahead("M", i, 4)
                conv_silu(1)
                if i == 0:
                    turn_c()
                    act.wait_ge(c_ready, 1)
                ahead("M", i, 5)
                copy_low("M", i, 2, 5)
                ahead("M", i, 6)
                decays()
                ahead("M", i, 7)
                copy_low("M", i, 3, 7)
                ahead("M", i, 8)
                for h in range(2):
                    act.wait_ge(mnum_done, 2 * i + h + 1)
                    A(inv[:, h, :], aux[:, 2 + h, S:2 * S], ACT.Exp, scale=-1.0).then_inc(floor_ready, 1)
                for h in range(2):
                    act.wait_ge(h_ready, 2 * i + h + 1)
                    A(hsq[:, h], hval[:, h], ACT.Square).then_inc(hsq_ready, 1)
                ahead("M", i, 9)
                copy_low("M", i, 4, 9)
                summed("M", i, 4)
                A(mo_sum[:, 0], mo_sum[:, 0], ACT.Sigmoid).then_inc(mo_ready, 1)
                ahead("M", i, 10)
                act.wait_ge(mss_done, i + 1)
                A(inv[:], aux[:, 2, :].rearrange("p (h s) -> p h s", h=2), ACT.Sqrt, bias=small[:, 31:32],
                  scale=1.0 / DV).then_inc(mrms_ready, 1)
                ahead("M", i, 11)
                copy_low("M", i, 5, 11)
                summed("M", i, 5)
                A(mo_sum[:, 1], mo_sum[:, 1], ACT.Sigmoid).then_inc(mo_ready, 1)
                for h in range(2):
                    act.wait_ge(hm_ready, 2 * i + h + 1)
                    A(hm_parts[:, 4 * i + 2 * h:4 * i + 2 * h + 2, 0:S], hval[:, h], ACT.Copy).then_inc(hm_hi, 1)

            def gate(name, i, c, index):
                summed(name, i, c)
                for k in range(2):
                    A(gates[:, bass.ds(2 * index + k, 1), :], sums[:, 0, k:k + 1, :], ACT.Sigmoid,
                      bias=vcol(2 * index + k + V_GB)).then_inc(gate_done, 1)

            act.wait_ge(hm_lo, M_H)
            with act.Fori(0, A_IT) as i:
                for c in range(3):
                    ahead("A", i, 2 * c)
                    ahead("A", i, 2 * c + 1)
                    copy_low("A", i, c, 2 * c + 1, scale=DH ** -0.5 if c == 0 else 1.0)
                ahead("A", i, 6)
                for h in range(2):
                    act.wait_ge(a_max, 2 * i + h + 1)
                    A(scores[:, h, 0:P], scores[:, h, 0:P], ACT.Exp, bias=small[:, 8 + 2 * h:9 + 2 * h],
                      accum_out=small[:, 12 + 2 * h:13 + 2 * h]).then_inc(a_exp, 1)
                    A(scores[:, h, P:3 * P], scores[:, h, P:3 * P], ACT.Exp, bias=small[:, 9 + 2 * h:10 + 2 * h],
                      accum_out=small[:, 13 + 2 * h:14 + 2 * h]).then_inc(a_exp, 1)
                ahead("A", i, 7)
                copy_low("A", i, 3, 7)
                gate("A", i, 3, 3 * i)
                ahead("A", i, 8)
                for h in range(2):
                    act.wait_ge(a_turned, 2 * i + h + 1)
                    A(probs_t[:, h], aux[:, 2 + h, 0:3 * P], ACT.Copy).then_inc(a_copied, 1)
                ahead("A", i, 9)
                copy_low("A", i, 4, 9)
                gate("A", i, 4, 3 * i + 1)
                ahead("A", i, 10)
                act.wait_ge(a_out, i + 1)
                A(ha_parts[:, bass.ds(2 * i, 2), 0:S], aux[:, 0, :].rearrange("p (h s) -> p h s", h=2), ACT.Copy).then_inc(ha_hi, 1)
                ahead("A", i, 11)
                copy_low("A", i, 5, 11)
                gate("A", i, 5, 3 * i + 2)
            with act.Fori(0, G_IT) as i:
                for c in range(2):
                    ahead("G", i, 2 * c)
                    ahead("G", i, 2 * c + 1)
                    copy_low("G", i, c, 2 * c + 1)
                    gate("G", i, c, 2 * i + c + A_GATES)
            act.wait_ge(ha_lo, A_IT)
            with act.Fori(0, B_IT) as i:
                for c in range(2):
                    ahead("B", i, 2 * c)
                    copy_low("B", i, 2 * c, 2 * c)
                    ahead("B", i, 2 * c + 1)
                    copy_low("B", i, 2 * c + 1, 2 * c + 1)
                    act.wait_ge(merged_ready, 2 * i + c + 1)
                    A(merged_parts[:, bass.ds(4 * i + 2 * c, 2), 0:S], sums[:, 0], ACT.Copy).then_inc(merged_hi, 1)
            act.wait_ge(x_again_in[0], TT * 16)
            with act.Fori(0, O_IT) as i:
                for c in range(2):
                    A(x_stage[:].rearrange("p t (o c) -> p o t c", o=1), x_again[:, bass.ds(2 * i + c, 1), :, :], ACT.Copy).then_inc(xs_copied, 1)
                    ahead("O", i, 2 * c)
                    ahead("O", i, 2 * c + 1)
                    copy_low("O", i, c, 2 * c + 1)
                    summed("O", i, c)
                    for k in range(2):
                        A(h_parts[:, bass.ds(4 * i + 2 * c + k, 1), 0:S], sums[:, c, k:k + 1, :], ACT.Copy,
                          scale=vcol(4 * i + 2 * c + k + V_FFN)).then_inc(h2_hi, 1)
                    A(squares[:], sums[:, c], ACT.Square).then_inc(x2_sq, 1)
                act.wait_ge(x_again_in[1], TT * 16)

            def up(i, first):
                ahead("U", i, 0)
                ahead("U", i, 1)
                if first:
                    act.wait_ge(ss_done, 1)
                    A(r_bc[:], aux[:, 0, 0:S], ACT.Sqrt, bias=small[:, 31:32], scale=1.0 / D).then_inc(rms_ready, 1)
                copy_low("U", i, 0, 1)
                for k in range(2):
                    act.wait_ge(u_scaled, i + 1)
                    A(u_conv_out[:, k, :], u_conv_in[:, k, 2:2 + S], ACT.Identity, scale=vcol(2 * i + k + V_UW + 2 * KF),
                      bias=vcol(2 * i + k + V_UB)).then_inc(u_tap, 1)
                ahead("U", i, 2)
                act.wait_ge(u_conv, 2 * i + 2)
                A(u_silu[:], u_conv_out[:], ACT.Silu).then_inc(u_silu_done, 1)
                ahead("U", i, 3)
                copy_low("U", i, 1, 3)
                act.wait_ge(u_act, i + 1)
                A(act_parts[:, bass.ds(2 * i, 2), 0:S], sums[:, 1], ACT.Copy).then_inc(act_hi, 1)

            up(0, True)
            with act.Fori(1, U_IT) as i:
                up(i, False)

            def down(i, last):
                for c in range(2):
                    for k in range(NDT):
                        j = NDT * c + k
                        if not (last and j >= 2 * NDT - AHEAD):
                            ahead("D", i, j)
                    copy_low("D", i, c, NDT * (c + 1) - 1)
                    act.wait_ge(x3_ready, 2 * i + c + 1)
                    A(squares[:], x3[:, bass.ds(4 * i + 2 * c, 2), :], ACT.Square).then_inc(x3_sq, 1)

            with act.Fori(0, D_IT - 1) as i:
                down(i, False)
            down(D_IT - 1, True)
            act.wait_ge(fin_ss, 1)
            A(small[:, 2:4], aux[:, 3, 0:TT], ACT.Sqrt, bias=small[:, 31:32], scale=1.0 / D).then_inc(fin_rms, 1)
            act.wait_ge(fin_r, 1)
            for f in range(0, 8, 2):
                tt, q = f // 4, f % 4
                act.wait_ge(rows_turned, f + 1)
                A(rows_out[:, tt, q * 512:(q + 1) * 512], row_bank(f), ACT.Copy, scale=small[:, 4 + tt:5 + tt]).then_inc(rows_a, 1)

        @block.vector
        def _(dve):
            own = OwnSteps(dve, dve_own)
            V = nc.vector

            def ahead(name, i, j):
                t0, _, tiles, _ = seg[name]
                slot, kh = (j + AHEAD) % RAW_SLOTS, tile_rows(j + AHEAD, name) // 2
                for f in range(2):
                    dve.wait_ge(hi_ready, 2 * (t0 + j + AHEAD) + f + 1 + i * (2 * tiles))
                    place = parts[:, (2 * j + f) % HALF_SLOTS, 0:kh]
                    V.tensor_tensor(place[:, :, 1, :], raw[:, slot, f * kh:(f + 1) * kh, :],
                                    place[:, :, 0, :].bitcast(F32), ALU.subtract).then_inc(lo_ready, 1)

            def add_group(name, i, c, dst, scale=1.0):
                _, g0, _, groups = seg[name]
                dve.wait_ge(low_copied, g0 + c + 1 + i * groups)
                V.scalar_tensor_tensor(dst, main[:, c % 2, :, 0:S], scale, lows[:, c % 2], ALU.mult, ALU.add).then_inc(group_summed, 1)

            def summed(name, i, c):
                _, g0, _, groups = seg[name]
                dve.wait_ge(group_summed, g0 + c + 1 + i * groups)

            V.memset(small[:, 31:32], EPS).then_inc(eps_ready, 1)
            own.add(V.memset(acc[:], 0.0))
            own.add(V.memset(conv_in[:, :, 0:4], 0.0))
            dve.wait_ge(x_sq, 2 * TT)
            V.tensor_tensor(small[:, 4:6], small[:, 0:2], small[:, 2:4], ALU.add).then_inc(x_ss, 1)
            dve.wait_ge(x_rms, 1)
            own.add(V.reciprocal(small[:, 4:6], small[:, 6:8]))
            own.settle()
            dve.wait_ge(pool_const, 1)
            for tt in range(TT):
                V.tensor_scalar(diag[:, tt, :], ident[:], small[:, 4 + tt:5 + tt], None, ALU.mult).then_inc(diag_ready, 1)
            for q in range(4):
                for k in range(4 * q, 4 * q + 4):
                    dve.wait_ge(h_hi, k + 1)
                    V.scalar_tensor_tensor(h_parts[:, k, S:2 * S], turn_bank(k), vcol(V_MIX + k),
                                           h_parts[:, k, 0:S].bitcast(F32), ALU.mult, ALU.subtract).then_inc(h_lo, 1)
                dve.wait_ge(hi_ready, q + 1)
                V.tensor_tensor(parts[:, q, :, 1, :], raw[:, q // 2, (q % 2) * HALF_K:(q % 2 + 1) * HALF_K],
                                parts[:, q, :, 0, :].bitcast(F32), ALU.subtract).then_inc(lo_ready, 1)
            dve.wait_ge(wif_hi, 1)
            V.tensor_tensor(wif_parts[:, :, 1, :], wif_raw[:], wif_parts[:, :, 0, :].bitcast(F32), ALU.subtract).then_inc(wif_lo, 1)
            dve.wait_ge(rel_in, 16)
            V.tensor_copy(rel_rows[:, REL:3 * P],
                          rel_rows[:, REL - 1:REL].to_broadcast([A_H, 3 * P - REL])).then_inc(rel_pad, 1)

            def gate_rows():
                dve.wait_ge(if_low, 1)
                own.add(V.tensor_tensor(if_sum[:], aux[0:64, 0, 0:S], if_low_sb[:], ALU.add))
                own.settle()
                own.add(V.tensor_scalar(li_row[:], if_sum[0:M_H, :], if_bias[0:M_H, 0:1], None, ALU.add))
                V.tensor_scalar(z_row[:], if_sum[32:32 + M_H, :], if_bias[32:32 + M_H, 0:1], None, ALU.add).then_inc(z_ready, 1)

            def running_rows():
                dve.wait_ge(log_term, 1)
                own.add(V.scalar_tensor_tensor(z_row[:], z_row[:], 0.0, log_row[:], ALU.min, ALU.subtract))
                own.settle()
                dve.wait_ge(pool_const, 4)
                own.add(V.tensor_tensor_scan(abs_row[:], ones[0:M_H, :], z_row[:], 0.0, ALU.mult, ALU.add))
                own.settle()
                V.tensor_tensor(li_row[:], li_row[:], abs_row[:], ALU.subtract).then_inc(c_row_ready, 1)
                dve.wait_ge(c_row_ready, 1)
                own.add(V.tensor_tensor_scan(g_row[:], li_row[:], li_row[:], -3e38, ALU.max, ALU.max))
                own.settle()
                V.tensor_tensor(m_row[:], abs_row[:], g_row[:], ALU.add).then_inc(c_row_ready, 1)

            for i in range(M_IT):
                def conv(which):
                    for k, tap in enumerate((2, 1, 0)):
                        for c in range(2):
                            ch = M_H * which + 2 * i + c
                            if k == 0:
                                dve.wait_ge(first_tap, 4 * i + 2 * which + c + 1)
                            ins = V.scalar_tensor_tensor(conv_out[:, c, :], conv_in[:, c, tap + 1:tap + 1 + S],
                                                         vcol(V_CW + tap * 8 + ch), conv_out[:, c, :], ALU.mult, ALU.add)
                            if tap == 0 and c == 1:
                                ins.then_inc(conv_done, 1)
                            else:
                                own.add(ins)
                        if tap:
                            own.settle()

                for which in range(2):
                    ahead("M", i, 2 * which)
                    if i == 0 and which == 1:
                        gate_rows()
                    ahead("M", i, 2 * which + 1)
                    if i == 0 and which == 1:
                        running_rows()
                    add_group("M", i, which, conv_in[:, :, 4:4 + S])
                    conv(which)
                ahead("M", i, 4)
                ahead("M", i, 5)
                add_group("M", i, 2, mv[:, :, 0:DV])
                ahead("M", i, 6)
                for h in range(2):
                    dve.wait_ge(decay_ready, 2 * i + h + 1)
                    V.scalar_tensor_tensor(mprobs[:, h], aux[:, h, 0:3 * P], DK ** -0.5, decay[:, h], ALU.mult,
                                           ALU.mult).then_inc(mprob_ready, 1)
                ahead("M", i, 7)
                add_group("M", i, 3, mv[:, :, DV:2 * DV])
                ahead("M", i, 8)
                for h in range(2):
                    dve.wait_ge(floor_ready, 2 * i + h + 1)
                    own.add(V.scalar_tensor_tensor(inv[:, h, :], aux[:, 2 + h, 0:S], -1.0, inv[:, h, :], ALU.mult, ALU.max))
                    own.settle()
                    own.add(V.tensor_tensor(inv[:, h, :], aux[:, 2 + h, 0:S], inv[:, h, :], ALU.max))
                    own.settle()
                    own.add(V.reciprocal(inv[:, h, :], inv[:, h, :]))
                    own.settle()
                    V.tensor_tensor(hval[:, h], aux[:, h, :].rearrange("p (v s) -> p v s", v=2),
                                    inv[:, h:h + 1, :].to_broadcast([P, 2, S]), ALU.mult).then_inc(h_ready, 1)
                ahead("M", i, 9)
                add_group("M", i, 4, mo_sum[:, 0])
                ahead("M", i, 10)
                dve.wait_ge(mrms_ready, i + 1)
                own.add(V.reciprocal(inv[:], inv[:]))
                own.settle()
                for h in range(2):
                    own.add(V.tensor_tensor(hval[:, h], hval[:, h], inv[:, h:h + 1, :].to_broadcast([P, 2, S]), ALU.mult))
                own.settle()
                ahead("M", i, 11)
                add_group("M", i, 5, mo_sum[:, 1])
                for h in range(2):
                    dve.wait_ge(mo_ready, 2 * i + h + 1)
                    for c in range(2):
                        ins = V.scalar_tensor_tensor(hval[:, h, c, :], hval[:, h, c, :], vcol(V_MN + 4 * i + 2 * h + c),
                                                     mo_sum[:, h, c, :], ALU.mult, ALU.mult)
                        if c:
                            ins.then_inc(hm_ready, 1)
                        else:
                            own.add(ins)
                for h in range(2):
                    dve.wait_ge(hm_hi, 2 * i + h + 1)
                    dst = hm_parts[:, 4 * i + 2 * h:4 * i + 2 * h + 2]
                    V.tensor_tensor(dst[:, :, S:2 * S], hval[:, h], dst[:, :, 0:S].bitcast(F32), ALU.subtract).then_inc(hm_lo, 1)

            with dve.Fori(0, A_IT) as i:
                own.enter(i, 10)
                for c, dst in enumerate((aq[:], ak[:], av[:])):
                    ahead("A", i, 2 * c)
                    ahead("A", i, 2 * c + 1)
                    add_group("A", i, c, dst, scale=DH ** -0.5 if c == 0 else 1.0)
                ahead("A", i, 6)
                for h in range(2):
                    dve.wait_ge(a_scored, 2 * i + h + 1)
                    own.add(V.tensor_tensor(scores[:, h:h + 1, :], aux[:, h:h + 1, 0:3 * P],
                                            bias_qk[:, bass.ds(2 * i + h, 1), :], ALU.add))
                    own.settle()
                    own.add(V.tensor_reduce(small[:, 16 + 2 * h:17 + 2 * h], scores[:, h, 0:P], AX_X, ALU.max))
                    own.add(V.tensor_reduce(small[:, 17 + 2 * h:18 + 2 * h], scores[:, h, P:3 * P], AX_X, ALU.max))
                    own.settle()
                    V.tensor_scalar(small[:, 8 + 2 * h:10 + 2 * h], small[:, 16 + 2 * h:18 + 2 * h], -1.0, None,
                                    ALU.mult).then_inc(a_max, 1)
                for h in range(2):
                    dve.wait_ge(a_exp, 4 * i + 2 * h + 2)
                    own.add(V.reciprocal(small[:, 20 + 2 * h:22 + 2 * h], small[:, 12 + 2 * h:14 + 2 * h]))
                    own.settle()
                    own.add(V.tensor_scalar(scores[:, h, 0:P], scores[:, h, 0:P], small[:, 20 + 2 * h:21 + 2 * h], None, ALU.mult))
                    V.tensor_scalar(scores[:, h, P:3 * P], scores[:, h, P:3 * P], small[:, 21 + 2 * h:22 + 2 * h], None,
                                    ALU.mult).then_inc(a_prob, 1)
                for c in range(2):
                    ahead("A", i, 7 + 2 * c)
                    add_group("A", i, 3 + c, sums[:, 0])
                    ahead("A", i, 8 + 2 * c)
                dve.wait_ge(ha_hi, i + 1)
                dst = ha_parts[:, bass.ds(2 * i, 2), :]
                V.tensor_tensor(dst[:, :, S:2 * S], aux[:, 0, :].rearrange("p (h s) -> p h s", h=2),
                                dst[:, :, 0:S].bitcast(F32), ALU.subtract).then_inc(ha_lo, 1)
                ahead("A", i, 11)
                add_group("A", i, 5, sums[:, 0])
            own.leave(A_IT)
            with dve.Fori(0, G_IT) as i:
                for c in range(2):
                    ahead("G", i, 2 * c)
                    ahead("G", i, 2 * c + 1)
                    add_group("G", i, c, sums[:, 0])
            dve.wait_ge(gate_done, 2 * KD)
            with dve.Fori(0, B_IT) as i:
                own.enter(i, 4)
                for c in range(2):
                    for b in range(2):
                        ahead("B", i, 2 * c + b)
                        add_group("B", i, 2 * c + b, sums[:, b])
                        summed("B", i, 2 * c + b)
                        own.add(V.tensor_tensor(sums[:, b], sums[:, b], gates[:, bass.ds(4 * i + 2 * c + b * KD, 2), :], ALU.mult))
                    own.settle()
                    V.tensor_tensor(sums[:, 0], sums[:, 0], sums[:, 1], ALU.add).then_inc(merged_ready, 1)
                    dve.wait_ge(merged_hi, 2 * i + c + 1)
                    dst = merged_parts[:, bass.ds(4 * i + 2 * c, 2), :]
                    V.tensor_tensor(dst[:, :, S:2 * S], sums[:, 0], dst[:, :, 0:S].bitcast(F32), ALU.subtract).then_inc(merged_lo, 1)
                    dve.wait_ge(merged_lo, 2 * i + c + 1)
            own.leave(B_IT)

            with dve.Fori(0, O_IT) as i:
                for c in range(2):
                    ahead("O", i, 2 * c)
                    ahead("O", i, 2 * c + 1)
                    add_group("O", i, c, sums[:, c])
                    for k in range(2):
                        dve.wait_ge(h2_hi, 4 * i + 2 * c + k + 1)
                        dst = h_parts[:, bass.ds(4 * i + 2 * c + k, 1), :]
                        V.scalar_tensor_tensor(dst[:, :, S:2 * S], sums[:, c, k:k + 1, :], vcol(4 * i + 2 * c + k + V_FFN),
                                               dst[:, :, 0:S].bitcast(F32), ALU.mult, ALU.subtract).then_inc(h2_lo, 1)
                    dve.wait_ge(x2_sq, 2 * i + c + 1)
                    V.tensor_tensor(acc[:], acc[:], squares[:], ALU.add).then_inc(acc_ready, 1)
                    dve.wait_ge(acc_ready, 2 * i + c + 1)
                for c in range(2):
                    dve.wait_ge(x2_stored[c], 16 * i + 16)
            own.add(V.memset(u_conv_in[:, :, 0:2], 0.0))
            own.settle()
            r_two = r_bc[:].rearrange("p (o s) -> p o s", o=1).to_broadcast([P, 2, S])

            def up(i, first):
                ahead("U", i, 0)
                ahead("U", i, 1)
                if first:
                    dve.wait_ge(rms_ready, 1)
                    own.add(V.reciprocal(r_bc[:], r_bc[:]))
                    own.add(V.memset(acc[:], 0.0))
                    own.settle()
                add_group("U", i, 0, sums[:, 0])
                summed("U", i, 0)
                V.tensor_tensor(u_conv_in[:, :, 2:2 + S], sums[:, 0], r_two, ALU.mult).then_inc(u_scaled, 1)
                for c in range(2):
                    dve.wait_ge(u_tap, 2 * i + c + 1)
                    own.add(V.scalar_tensor_tensor(u_conv_out[:, c, :], u_conv_in[:, c, 1:1 + S], vcol(2 * i + c + V_UW + KF),
                                                   u_conv_out[:, c, :], ALU.mult, ALU.add))
                own.settle()
                for c in range(2):
                    V.scalar_tensor_tensor(u_conv_out[:, c, :], u_conv_in[:, c, 0:S], vcol(2 * i + c + V_UW),
                                           u_conv_out[:, c, :], ALU.mult, ALU.add).then_inc(u_conv, 1)
                ahead("U", i, 2)
                dve.wait_ge(u_conv, 2 * i + 2)
                ahead("U", i, 3)
                add_group("U", i, 1, sums[:, 1])
                summed("U", i, 1)
                own.add(V.tensor_tensor(sums[:, 1], sums[:, 1], r_two, ALU.mult))
                own.settle()
                dve.wait_ge(u_silu_done, i + 1)
                V.tensor_tensor(sums[:, 1], sums[:, 1], u_silu[:], ALU.mult).then_inc(u_act, 1)
                dve.wait_ge(act_hi, i + 1)
                dst = act_parts[:, bass.ds(2 * i, 2), :]
                V.tensor_tensor(dst[:, :, S:2 * S], sums[:, 1], dst[:, :, 0:S].bitcast(F32), ALU.subtract).then_inc(act_lo, 1)
                dve.wait_ge(act_lo, i + 1)

            up(0, True)
            with dve.Fori(1, U_IT) as i:
                own.enter(i - 1, 3)
                up(i, False)
            own.leave(U_IT - 1)

            def down(i, last):
                for c in range(2):
                    for k in range(NDT):
                        j = NDT * c + k
                        if not (last and j >= 2 * NDT - AHEAD):
                            ahead("D", i, j)
                    add_group("D", i, c, sums[:, c])
                    summed("D", i, c)
                    dve.wait_ge(x3_in, 16)
                    here = x3[:, bass.ds(4 * i + 2 * c, 2), :]
                    V.tensor_tensor(here, here, sums[:, c], ALU.add).then_inc(x3_ready, 1)
                    dve.wait_ge(x3_sq, 2 * i + c + 1)
                    own.add(V.tensor_tensor(acc[:], acc[:], squares[:], ALU.add))
                    own.settle()
                    for k in range(2):
                        one = x3[:, bass.ds(4 * i + 2 * c + k, 1), :]
                        V.tensor_scalar(one, one, vcol(4 * i + 2 * c + k + V_FIN), None, ALU.mult).then_inc(x3_final, 1)

            with dve.Fori(0, D_IT - 1) as i:
                own.enter(i, 2)
                down(i, False)
            own.leave(D_IT - 1)
            down(D_IT - 1, True)
            dve.wait_ge(fin_rms, 1)
            V.reciprocal(small[:, 4:6], small[:, 2:4]).then_inc(fin_r, 1)
            dve.wait_ge(fin_r, 1)
            for f in range(1, 8, 2):
                tt, q = f // 4, f % 4
                dve.wait_ge(rows_turned, f + 1)
                V.tensor_scalar(rows_out[:, tt, q * 512:(q + 1) * 512], row_bank(f), small[:, 4 + tt:5 + tt], None,
                                ALU.mult).then_inc(rows_v, 1)

        @block.tensor
        def _(pe):
            mm = nc.tensor.matmul

            def multiply(name, i, j, moving, k0, first, last, rows_so_far=None):
                t0, g0, tiles, groups = seg[name]
                kh, c = tile_rows(j, name) // 2, group_of(name, j)
                for f in range(2):
                    pe.wait_ge(lo_ready, 2 * (t0 + j) + f + 1 + i * (2 * tiles))
                    if rows_so_far:
                        rows_so_far(k0 + (f + 1) * kh)
                    if f == 0 and first and not (isinstance(i, int) and g0 + c - 1 + i * groups <= 0):
                        pe.wait_ge(group_summed, g0 + c - 1 + i * groups)
                    for k in range(kh):
                        for b in range(2):
                            w = parts[:, (2 * j + f) % HALF_SLOTS, k, :, b * P:(b + 1) * P]
                            start, stop = first and f == 0 and k == 0, last and f == 1 and k == kh - 1
                            bank, move = main[:, c % 2, b, :], moving[:, k0 + f * kh + k, :]
                            if stop:
                                mm(bank[:, 0:S], w[:, 1, :], move[:, 0:S], start=False, stop=False)
                                ins = mm(bank, w[:, 0, :], move, start=start, stop=True)
                            else:
                                mm(bank, w[:, 0, :], move, start=start, stop=False)
                                ins = mm(bank[:, 0:S], w[:, 1, :], move[:, 0:S], start=False, stop=False)
                    ins.then_inc(half_used, 1)

            def multiply_rows(name, i, j, k0, first, last):
                t0, g0, tiles, groups = seg[name]
                c = group_of(name, j)
                for f in range(2):
                    pe.wait_ge(lo_ready, 2 * (t0 + j) + f + 1 + i * (2 * tiles))
                    if f == 0 and first:
                        pe.wait_ge(group_summed, g0 + c - 1 + i * groups)
                    for k in range(HALF_K):
                        kk = k0 + f * HALF_K + k
                        for b in range(TT):
                            w = parts[:, (2 * j + f) % HALF_SLOTS, k].rearrange("p a c -> p (a c)")
                            stop, bank = last and f == 1 and k == HALF_K - 1, main[:, c % 2, b, :]
                            hi, lo = (h_parts[:, kk, a * S + b * P:a * S + (b + 1) * P] for a in range(2))
                            if stop:
                                mm(bank[:, 0:COLS], lo, w[:, 0:COLS], start=False, stop=False)
                                ins = mm(bank, hi, w, start=False, stop=True)
                            else:
                                mm(bank, hi, w, start=first and f == 0 and k == 0, stop=False)
                                ins = mm(bank[:, 0:COLS], lo, w[:, 0:COLS], start=False, stop=False)
                    ins.then_inc(half_used, 1)

            def group_of(name, j):
                return j // NDT if name == "D" else j if name == "B" else j // 2

            def project(name, i, c, moving=None):
                for k in range(2):
                    if moving is None:
                        multiply_rows(name, i, 2 * c + k, k * TILE_K, k == 0, k == 1)
                    else:
                        multiply(name, i, 2 * c + k, moving, k * TILE_K, k == 0, k == 1)

            pe.wait_ge(mix_in, 16)
            pe.wait_ge(pool_const, 1)
            nc.tensor.transpose(aux[:, 3, 0:KD], vec_rows[V_MIX:V_MIX + KD, 0, :], ident[0:KD, 0:KD]).then_inc(vec_t, 1)

            def turn(ks):
                for k in ks:
                    if k == 5:
                        pe.wait_ge(vec_ready, 1)
                    if k >= 6:
                        pe.wait_ge(h_lo, k - 5)
                    for tt in range(TT):
                        ins = mm(turn_bank(k)[:, tt * P:(tt + 1) * P], x_rows[:, tt, k * P:(k + 1) * P], diag[:, tt, :],
                                 start=True, stop=True)
                    ins.then_inc(x_turned, 1)

            pe.wait_ge(diag_ready, TT)
            turn(range(0, 8))
            for i in range(M_IT):
                if i == 0:
                    def follow(ready):
                        if ready > HALF_K:
                            turn(range(ready, min(ready + HALF_K, KD)) if ready >= 2 * HALF_K else range(0))
                        pe.wait_ge(h_lo, ready)

                    multiply("M", 0, 0, h_parts, 0, True, False, follow)
                    multiply("M", 0, 1, h_parts, TILE_K, False, True, follow)
                    pe.wait_ge(vec_in, 9 * 16)
                    nc.tensor.transpose(aux[:, 3, 0:P], vec_rows[:, 0, :], ident[:])
                    nc.tensor.transpose(aux[:, 3, P:P + 2 * KF], vec_rows[0:2 * KF, 1, :], ident[0:2 * KF, 0:2 * KF])
                    nc.tensor.transpose(aux[:, 3, P + 2 * KF:P + 4 * KF], vec_rows[0:2 * KF, 2, :],
                                        ident[0:2 * KF, 0:2 * KF]).then_inc(vec_t, 1)
                    pe.wait_ge(wif_lo, 1)
                    for k in range(KD):
                        if k < KD - 1:
                            mm(aux[:, 0, :], wif_parts[:, k, 0, :], h_parts[:, k, :], start=k == 0, stop=False)
                            mm(aux[:, 0, 0:S], wif_parts[:, k, 1, :], h_parts[:, k, 0:S], start=False, stop=False)
                        else:
                            mm(aux[:, 0, 0:S], wif_parts[:, k, 1, :], h_parts[:, k, 0:S], start=False, stop=False)
                            mm(aux[:, 0, :], wif_parts[:, k, 0, :], h_parts[:, k, :], start=False, stop=True).then_inc(if_done, 1)
                else:
                    project("M", i, 0, h_parts)
                    pe.wait_ge(hankel_masked, 1)
                    pe.wait_ge(mrms_ready, 1)
                    for h in range(A_H):
                        for b in range(2):
                            ins = mm(aux[:, h // 2, (h % 2) * S + b * P:(h % 2) * S + (b + 1) * P], hankel[:, h, b, :], anti[:],
                                     start=True, stop=True)
                        if h % 2:
                            ins.then_inc(bias_mm, 1)
                project("M", i, 1, h_parts)
                if i == 0:
                    pe.wait_ge(c_row_ready, 2)
                    for tt in range(TT):
                        ins = nc.tensor.transpose(aux[:, 1, tt * M_H:(tt + 1) * M_H], li_row[:, tt * P:(tt + 1) * P],
                                                  ident[0:M_H, 0:M_H])
                    ins.then_inc(c_turned, 1)
                project("M", i, 2)
                pe.wait_ge(mqk_ready, 2 * i + 2)
                if i == 0:
                    pe.wait_ge(c_ready, 1)
                    pe.wait_ge(pool_const, 4)
                else:
                    pe.wait_ge(bias_ready, 8)
                for h in range(2):
                    mm(aux[:, h, 0:S], mk[:, h, 0:P], mq[:, h, :], start=True, stop=True)
                    mm(aux[:, h, S:S + P], mk[:, h, P:S], mq[:, h, P:S], start=True, stop=True)
                    hd = 2 * i + h
                    mm(aux[:, 2 + h, 0:S], pick[:, hd, :], g_row[:], start=True, stop=False)
                    mm(aux[:, 2 + h, 0:P], ident[:], future[:], start=False, stop=True)
                    mm(aux[:, 2 + h, S:S + P], pick[:, hd, :], g_row[:, P:S], start=True, stop=False)
                    mm(aux[:, 2 + h, S:S + P], ident[:], future[:], start=False, stop=True).then_inc(mqk_done, 1)
                project("M", i, 3)
                for h in range(2):
                    pe.wait_ge(mprob_ready, 2 * i + h + 1)
                    mm(aux[:, 2 + h, 0:S], ones[:, 0:P], mprobs[:, h, 0:S], start=True, stop=False)
                    mm(aux[:, 2 + h, P:S], ones[:, 0:P], mprobs[:, h, S:S + P], start=False, stop=True)
                    mm(aux[:, 2 + h, S:2 * S], pick[:, 2 * i + h, :], m_row[:], start=True, stop=True)
                    pe.wait_ge(group_summed, 6 * i + 3 + h)
                    for v in range(2):
                        dst = aux[:, h, v * S:(v + 1) * S]
                        cols = slice(h * DV + v * P, h * DV + (v + 1) * P)
                        mm(dst, mv[:, 0, cols], mprobs[:, h, 0:S], start=True, stop=False)
                        ins = mm(dst[:, P:S], mv[:, 1, cols], mprobs[:, h, S:S + P], start=False, stop=True)
                    ins.then_inc(mnum_done, 1)
                project("M", i, 4, h_parts)
                multiply("M", i, 10, h_parts, 0, True, False)
                for h in range(2):
                    pe.wait_ge(hsq_ready, 2 * i + h + 1)
                    mm(aux[:, 2, h * S:(h + 1) * S], ones[:, 0:P], hsq[:, h, 0, :], start=True, stop=False)
                    ins = mm(aux[:, 2, h * S:(h + 1) * S], ones[:, 0:P], hsq[:, h, 1, :], start=False, stop=True)
                ins.then_inc(mss_done, 1)
                multiply("M", i, 11, h_parts, TILE_K, False, True)

            with pe.Fori(0, A_IT) as i:
                project("A", i, 0, h_parts)
                project("A", i, 1, h_parts)
                project("A", i, 2)
                pe.wait_ge(group_summed, seg["A"][1] + 2 + 6 * i)
                for h in range(2):
                    mm(aux[:, h, 0:P], aq[:, h, 0:P], ak[:, h, 0:P], start=True, stop=True)
                    mm(aux[:, h, P:3 * P], aq[:, h, P:S], ak[:, h, :], start=True, stop=True).then_inc(a_scored, 1)
                project("A", i, 3, h_parts)
                for h in range(2):
                    pe.wait_ge(a_prob, 2 * i + h + 1)
                    for q in range(3):
                        ins = nc.tensor.transpose(aux[:, 2 + h, q * P:(q + 1) * P], scores[:, h, q * P:(q + 1) * P], ident[:])
                    ins.then_inc(a_turned, 1)
                project("A", i, 4, h_parts)
                pe.wait_ge(a_copied, 2 * i + 2)
                pe.wait_ge(group_summed, seg["A"][1] + 3 + 6 * i)
                for h in range(2):
                    dst = aux[:, 0, h * S:(h + 1) * S]
                    mm(dst, av[:, 0, h * P:(h + 1) * P], probs_t[:, h, 0:S], start=True, stop=False)
                    ins = mm(dst[:, P:S], av[:, 1, h * P:(h + 1) * P], probs_t[:, h, S:S + P], start=False, stop=True)
                ins.then_inc(a_out, 1)
                project("A", i, 5, h_parts)
            with pe.Fori(0, G_IT) as i:
                for c in range(2):
                    project("G", i, c, h_parts)
            pe.wait_ge(hm_lo, M_H)
            pe.wait_ge(ha_lo, A_IT)
            with pe.Fori(0, B_IT) as i:
                for j in range(4):
                    multiply("B", i, j, ha_parts if j % 2 else hm_parts, 0, True, True)
            with pe.Fori(0, O_IT) as i:
                for c in range(2):
                    if c == 0:
                        pe.wait_ge(merged_lo, B_IT)
                    multiply("O", i, 2 * c, merged_parts, 0, True, False)
                    if c == 0:
                        pe.wait_ge(merged_lo, 2 * B_IT)
                    pe.wait_ge(xs_copied, 2 * i + c + 1)
                    for b in range(2):
                        for tt in range(TT):
                            mm(main[:, c % 2, b, tt * P:(tt + 1) * P], x_stage[:, tt, b * P:(b + 1) * P], ident[:],
                               start=False, stop=False, skip_group_check=True)
                    multiply("O", i, 2 * c + 1, merged_parts, TILE_K, False, True)
            pe.wait_ge(h2_lo, KD // 2)
            multiply("U", 0, 0, h_parts, 0, True, False)
            pe.wait_ge(h2_lo, KD)
            multiply("U", 0, 1, h_parts, TILE_K, False, True)
            pe.wait_ge(acc_ready, 2 * O_IT)
            mm(aux[:, 0, 0:S], ones[:, 0:P], acc[:, 0, :], start=True, stop=False)
            mm(aux[:, 0, 0:S], ones[:, 0:P], acc[:, 1, :], start=False, stop=True).then_inc(ss_done, 1)
            project("U", 0, 1, h_parts)
            with pe.Fori(1, U_IT) as i:
                for c in range(2):
                    project("U", i, c, h_parts)
            pe.wait_ge(act_lo, U_IT - 2)
            with pe.Fori(0, D_IT) as i:
                for c in range(2):
                    for k in range(NDT):
                        if c == 0 and k == NDT - 1:
                            pe.wait_ge(act_lo, U_IT)
                        multiply("D", i, NDT * c + k, act_parts, k * TILE_K, k == 0, k == NDT - 1)
            pe.wait_ge(x3_final, KD)
            for tt in range(TT):
                for a in range(2):
                    ins = mm(aux[:, 3, tt:tt + 1], acc[:, a, tt * P:(tt + 1) * P], ones[:, 0:1], start=a == 0, stop=a == 1)
            ins.then_inc(fin_ss, 1)
            for f in range(8):
                tt, q = f // 4, f % 4
                if f == 7:
                    pe.wait_ge(fin_rms, 1)
                for c in range(4):
                    ins = nc.tensor.transpose(row_bank(f)[:, c * P:(c + 1) * P], x3[:, 4 * q + c, tt * P:(tt + 1) * P], ident[:])
                ins.then_inc(rows_turned, 1)


_INS = ["x", "norm_mix", "w_in", "conv_qk_w", "conv_qk_b", "b_igate", "b_fgate", "m_norm", "rel_bias", "gate_bias",
        "w_branch_m", "w_branch_a", "w_out", "norm_ffn", "w_up", "conv_ffn_w", "conv_ffn_b", "w_down", "norm_final"]


def kernel(**inputs):
    import numpy as _np
    import concourse.bacc as _bacc
    from concourse import mybir as _mybir
    from concourse.bass_utils import run_bass_kernel_spmd as _run

    nc = _bacc.Bacc("TRN2", target_bir_lowering=False, num_devices=1)
    arrays, args = {}, []
    for name in _INS:
        a = _np.ascontiguousarray(inputs[name])
        arrays[f"in_{name}_dram"] = a
        args.append(nc.dram_tensor(f"in_{name}_dram", a.shape, _mybir.dt.from_np(a.dtype), kind="ExternalInput").ap())
    shape = arrays["in_x_dram"].shape
    args.append(nc.dram_tensor("out_0_dram", shape, _mybir.dt.float32, kind="ExternalOutput").ap())
    hybrid_block(nc, *args)
    r = _run(nc, [arrays], core_ids=[0])
    return r.results[0]["out_0_dram"]
```

```python
from contextlib import ExitStack

import concourse.bass as bass
from concourse import mybir

F32 = mybir.dt.float32
F32R = mybir.dt.float32r
BF16 = mybir.dt.bfloat16
ALU = mybir.AluOpType
ACT = mybir.ActivationFunctionType
AX_X = mybir.AxisListType.X

P = 128
CHUNK = 64
EPS = 1e-6
BIG = 1e30
COLS = 256
TILE_K = 8
AHEAD = 2
HALF_K = TILE_K // 2
RAW_SLOTS = 4
HALF_SLOTS = 2 * AHEAD
WARM_UP = 27
STAY_WARM = 12


class OwnSteps:

    def __init__(self, eng, sem):
        self.eng, self.sem, self.base, self.count = eng, sem, 0, 0

    def add(self, ins):
        ins.then_inc(self.sem, 1)
        self.count += 1

    def settle(self):
        self.eng.wait_ge(self.sem, self.base + self.count)

    def enter(self, i, per):
        self.loop_base, self.per = self.base + self.count, per
        self.base, self.count = self.loop_base + i * per, 0

    def leave(self, times):
        assert self.count == self.per, (self.count, self.per)
        self.base, self.count = self.loop_base + times * self.per, 0


def hybrid_block(nc, x, norm_mix, w_in, conv_qk_w, conv_qk_b, b_igate, b_fgate, m_norm, rel_bias, gate_bias,
                 w_branch_m, w_branch_a, w_out, norm_ffn, w_up, conv_ffn_w, conv_ffn_b, w_down, norm_final, out):
    _, S, D = x.shape
    D_FF = w_down.shape[1]
    M_H = b_igate.shape[1]
    M_V = m_norm.shape[1]
    M_QK = conv_qk_w.shape[2] // 2
    DK, DV = M_QK // M_H, M_V // M_H
    A_H = rel_bias.shape[1]
    A_W = w_branch_a.shape[1]
    DH = A_W // A_H
    REL = rel_bias.shape[2]
    A_MAX_REL = REL // 2
    TT = S // P
    KD, KV, KF = D // P, M_V // P, D_FF // P
    assert (S, DK, DV, DH, TT, M_H, A_H, COLS) == (256, P, 2 * P, P, 2, 4, 8, S)
    assert KV == A_W // P == TILE_K and KD == 2 * TILE_K and KF % 4 == 0 and A_MAX_REL == P
    offset = {}
    at = 0
    for name, width in (("mq", M_QK), ("mk", M_QK), ("mv", M_V), ("mo", M_V), ("mi", M_H), ("mf", M_H),
                        ("aq", A_W), ("ak", A_W), ("av", A_W), ("gates", 2 * D)):
        offset[name] = at
        at += width
    assert at == w_in.shape[2]

    DOWN_TILES = [TILE_K] * (KF // TILE_K) + [KF % TILE_K]
    NDT = len(DOWN_TILES)
    M_IT, A_IT, G_IT, B_IT, O_IT, U_IT, D_IT = 2, A_H // 2, 2, 4, 4, D_FF // COLS, 4
    seg, t, g = {}, 0, 0
    for name, times, tiles, groups in (("M", M_IT, 12, 6), ("A", A_IT, 12, 6), ("G", G_IT, 4, 2), ("B", B_IT, 4, 4),
                                       ("O", O_IT, 4, 2), ("U", U_IT, 4, 2), ("D", D_IT, 2 * NDT, 2)):
        seg[name] = (t, g, tiles, groups)
        assert t % RAW_SLOTS == 0 and g % 2 == 0
        t, g = t + times * tiles, g + times * groups
    LAST_TILE, LAST_GROUP = t, g
    A_GATES = 3 * A_IT

    def place(name, i):
        t0, g0, tiles, groups = seg[name]
        return t0 + i * tiles, g0 + i * groups

    tpad = nc.dram_tensor("tpad_scratch", (A_H, 3 * P), F32, kind="Internal")
    x2_dram = nc.dram_tensor("x2_scratch", (P, KD * S), F32, kind="Internal").ap()

    with ExitStack() as ctx:
        def sb(name, shape, dt=F32):
            return ctx.enter_context(nc.sbuf_tensor(name, shape, dt))

        def sem(name):
            return ctx.enter_context(nc.semaphore(name))

        def region(kib, *sets):
            made = []
            for one in sets:
                with ExitStack() as s:
                    made += [s.enter_context(nc.sbuf_tensor(n, shape, dt)) for n, shape, dt in one]
            ctx.enter_context(nc.sbuf_tensor(f"hold_{made[0].name}", [P, kib * 256], F32))
            return made

        raw, rows_out = region(32, [("raw", [P, RAW_SLOTS, TILE_K, COLS], F32)], [("rows_out", [P, TT, D], F32)])
        parts = sb("parts", [P, HALF_SLOTS, HALF_K, 2, COLS], F32R)
        h_parts, x3 = region(32, [("h_parts", [P, KD, 2 * S], F32R)], [("x3", [P, KD, S], F32)])
        hm_size, ga_size = KV * 2 * S, 2 * KD * S
        stages = region(
            96,
            [("hm_parts", [P, KV, 2 * S], F32R), ("hold_a", [P, hm_size + ga_size], F32),
             ("merged_parts", [P, KD, 2 * S], F32R)],
            [("hold_b", [P, hm_size], F32), ("ha_parts", [P, KV, 2 * S], F32R), ("gates", [P, 2 * KD, S], F32),
             ("x_rows", [P, TT, D], F32), ("wif_raw", [P, KD, P // 2], F32), ("vec_rows", [P, 3, P], F32),
             ("rel_rows", [A_H, 3 * P], F32)],
            [("junk", [P, D], F32), ("if_low_sb", [64, 2, S], F32), ("if_sum", [64, S], F32), ("li_row", [M_H, S], F32),
             ("z_row", [M_H, S], F32), ("abs_row", [M_H, S], F32), ("log_row", [M_H, S], F32),
             ("if_bias", [64, 8], F32), ("hold_c", [P, 2 * hm_size - D - 7 * S - 8], F32),
             ("x_again", [P, D // COLS, TT, COLS], F32), ("x_stage", [P, TT, 2 * P], F32),
             ("hold_d", [P, ga_size - TT * D - 2 * S], F32), ("bias_qk", [P, A_H, 3 * P], F32),
             ("hankel", [P, A_H, 2, P], F32), ("aq", [P, 2, S], F32), ("ak", [P, 2, S], F32), ("av", [P, TT, 2 * P], F32),
             ("scores", [P, 2, 3 * P], F32), ("probs_t", [P, 2, 3 * P], F32)],
            [("hm_values", [P, KV, 2 * S], F32), ("mo_sum", [P, 2, 2, S], F32), ("conv_in", [P, 2, S + 4], F32),
             ("hold_f", [P, hm_size - 4 * S - 2 * (S + 4)], F32),
             ("mv", [P, TT, 2 * DV], F32), ("conv_out", [P, 2, S], F32), ("mq", [P, 2, S], F32), ("mk", [P, 2, S], F32),
             ("decay", [P, 2, 3 * P], F32), ("mprobs", [P, 2, 3 * P], F32), ("inv", [P, 2, S], F32),
             ("hval", [P, 2, 2, S], F32), ("hsq", [P, 2, 2, S], F32), ("pick", [M_H, M_H, P], F32),
             ("g_row", [M_H, S], F32), ("m_row", [M_H, S], F32), ("future", [P, P], BF16), ("ident_half", [P, P], BF16)],
            [("hold_g", [P, 2 * hm_size + TT * 2 * DV + 6 * S], F32), ("wif_parts", [P, KD, 2, P // 2], F32R)],
            [("act_parts", [P, KF, 2 * S], F32R), ("u_conv_in", [P, 2, S + 2], F32), ("u_conv_out", [P, 2, S], F32),
             ("u_silu", [P, 2, S], F32)])
        named = {r.name: r for r in stages}
        hm_parts, ha_parts, gates, merged_parts = (named[n] for n in ("hm_parts", "ha_parts", "gates", "merged_parts"))
        hm_values = named["hm_values"]
        x_rows, wif_raw, wif_parts, x_again, x_stage = (named[n] for n in ("x_rows", "wif_raw", "wif_parts", "x_again", "x_stage"))
        vec_rows, rel_rows, junk, if_low_sb, if_sum = (named[n] for n in ("vec_rows", "rel_rows", "junk", "if_low_sb", "if_sum"))
        li_row, z_row, abs_row, log_row, if_bias = (named[n] for n in ("li_row", "z_row", "abs_row", "log_row", "if_bias"))
        bias_qk, hankel, aq, ak, av = (named[n] for n in ("bias_qk", "hankel", "aq", "ak", "av"))
        scores, probs_t, mo_sum, conv_in, mv = (named[n] for n in ("scores", "probs_t", "mo_sum", "conv_in", "mv"))
        conv_out, mq, mk, decay, mprobs = (named[n] for n in ("conv_out", "mq", "mk", "decay", "mprobs"))
        inv, hval, hsq, pick, g_row, m_row = (named[n] for n in ("inv", "hval", "hsq", "pick", "g_row", "m_row"))
        future, ident_half = (named[n] for n in ("future", "ident_half"))
        act_parts, u_conv_in, u_conv_out, u_silu = (named[n] for n in ("act_parts", "u_conv_in", "u_conv_out", "u_silu"))

        ident = sb("ident", [P, P])
        ones = sb("ones", [P, S])
        lows = sb("lows", [P, 2, 2, S])
        sums = sb("sums", [P, 2, 2, S])
        squares = sb("squares", [P, 2, S])
        acc = sb("acc", [P, 2, S])
        r_bc = sb("r_bc", [P, S])
        vec = sb("vec", [P, P + 4 * KF])
        small = sb("small", [P, 32 + TT * M_H])
        ccol = small[:, 32:32 + TT * M_H]
        main = ctx.enter_context(nc.psum_tensor("main", [P, 2, 2, 512], F32))
        aux = ctx.enter_context(nc.psum_tensor("aux", [P, 4, 512], F32))

        def row_bank(f):
            return aux[:, f, :] if f < 4 else main[:, f // 2 - 2, f % 2, :]

        x_in = [sem(f"x_in{k}") for k in range(2 * TT)]
        w_loaded = [sem(f"w_loaded{k}") for k in range(RAW_SLOTS)]
        mix_in, vec_in, wif_in, rel_in, tpad_out, hankel_in = (
            sem(n) for n in ("mix_in", "vec_in", "wif_in", "rel_in", "tpad_out", "hankel_in"))
        x3_in, rows_stored = (sem(n) for n in ("x3_in", "rows_stored"))
        x_again_in = [sem(f"x_again_in{k}") for k in range(2)]
        x2_stored = [sem(f"x2_stored{k}") for k in range(2)]
        hi_ready, lo_ready, half_used, low_copied, group_summed = (
            sem(n) for n in ("hi_ready", "lo_ready", "half_used", "low_copied", "group_summed"))
        pool_const, wif_hi, wif_lo, vec_t, vec_ready, rel_pad = (
            sem(n) for n in ("pool_const", "wif_hi", "wif_lo", "vec_t", "vec_ready", "rel_pad"))
        x_sq, x_ss, x_rms, x_r, x_scaled_a, x_scaled_v, x_turned, h_hi, h_lo, wif_placed = (
            sem(n) for n in ("x_sq", "x_ss", "x_rms", "x_r", "x_scaled_a", "x_scaled_v", "x_turned", "h_hi",
                            "h_lo", "wif_placed"))
        if_done, if_low, z_ready, log_term, c_row_ready, c_turned, c_ready, bias_ready = (
            sem(n) for n in ("if_done", "if_low", "z_ready", "log_term", "c_row_ready", "c_turned", "c_ready",
                            "bias_ready"))
        first_tap, conv_done, mqk_ready, mqk_done, decay_ready, mprob_ready, mnum_done, floor_ready = (
            sem(n) for n in ("first_tap", "conv_done", "mqk_ready", "mqk_done", "decay_ready", "mprob_ready",
                            "mnum_done", "floor_ready"))
        h_ready, hsq_ready, mss_done, mrms_ready, mo_ready, hm_ready, hm_hi, hm_lo, eps_ready, inv_ready, hsq_summed = (
            sem(n) for n in ("h_ready", "hsq_ready", "mss_done", "mrms_ready", "mo_ready", "hm_ready", "hm_hi", "hm_lo",
                            "eps_ready", "inv_ready", "hsq_summed"))
        a_scored, a_max, a_exp, a_prob, a_turned, a_copied, a_out, ha_hi, ha_lo, gate_done = (
            sem(n) for n in ("a_scored", "a_max", "a_exp", "a_prob", "a_turned", "a_copied", "a_out", "ha_hi", "ha_lo",
                            "gate_done"))
        merged_ready, merged_hi, merged_lo, xs_copied, x2_sq, h2_hi, h2_lo, acc_ready, ss_done, rms_ready, r_ready = (
            sem(n) for n in ("merged_ready", "merged_hi", "merged_lo", "xs_copied", "x2_sq", "h2_hi", "h2_lo",
                            "acc_ready", "ss_done", "rms_ready", "r_ready"))
        u_scaled, u_tap, u_conv, u_act, u_silu_done, act_hi, act_lo = (
            sem(n) for n in ("u_scaled", "u_tap", "u_conv", "u_act", "u_silu_done", "act_hi", "act_lo"))
        xt_done, x2_ready = sem("xt_done"), sem("x2_ready")
        x3_ready, x3_sq, x3_final, fin_ss, fin_rms, fin_r, rows_turned, rows_a, rows_v = (
            sem(n) for n in ("x3_ready", "x3_sq", "x3_final", "fin_ss", "fin_rms", "fin_r", "rows_turned", "rows_a",
                            "rows_v"))
        act_own, dve_own, pool_own = sem("act_own"), sem("dve_own"), sem("pool_own")

        V_MIX, V_FFN, V_FIN, V_CW, V_CB, V_MN, V_GB = 0, 16, 32, 48, 80, 88, 96
        V_UW, V_UB = P, P + 3 * KF

        def vcol(c):
            return vec[:, bass.ds(c, 1)]

        def turn_bank(k):
            bank = k // 2 % 6
            return (main[:, 1, bank, :] if bank < 2 else aux[:, bank - 2, :])[:, k % 2 * S:(k % 2 + 1) * S]

        def x_piece(q, tt):
            return x_rows[:, tt, q * (D // 4):(q + 1) * (D // 4)]

        block = ctx.enter_context(nc.Block())

        def tile_rows(j_in_seg, name):
            return DOWN_TILES[j_in_seg % NDT] if name == "D" else TILE_K

        @block.sync
        def _(sp):
            xr = x[0].rearrange("(t p) d -> p t d", p=P)
            sp.dma_start(vec_rows[V_MIX:V_MIX + KD, 0, :], norm_mix[0].rearrange("(r p) -> r p", p=P)).then_inc(mix_in, 16)
            for k in range(2 * TT):
                tt, half = k % 2, slice(k // 2 * (D // 2), (k // 2 + 1) * (D // 2))
                sp.dma_start(x_rows[:, tt, half], xr[:, tt, half]).then_inc(x_in[k], 16)

            def load(n, j, w, k0, kn, col):
                if not (isinstance(n, int) and n < RAW_SLOTS):
                    sp.wait_ge(lo_ready, 2 * (n - RAW_SLOTS + 1))
                src = w[0, k0 * P:(k0 + kn) * P, bass.ds(col, COLS)].rearrange("(k p) c -> p k c", p=P)
                sp.dma_start(raw[:, j % RAW_SLOTS, 0:kn, :], src).then_inc(w_loaded[j % RAW_SLOTS], 16)

            def load_group(n, j, w, col, count=2):
                for k in range(count):
                    load(n + k, j + k, w, k * TILE_K, TILE_K, col)

            def load_vectors():
                for r0, ap in ((V_FFN, norm_ffn[0].rearrange("(r p) -> r p", p=P)),
                               (V_FIN, norm_final.rearrange("(r p) -> r p", p=P)),
                               (V_CW, conv_qk_w[0].rearrange("k (r p) -> (k r) p", p=P)),
                               (V_CB, conv_qk_b[0].rearrange("(r p) -> r p", p=P)), (V_MN, m_norm[0].rearrange("(r p) -> r p", p=P)),
                               (V_GB, gate_bias[0].rearrange("k (r p) -> (k r) p", p=P))):
                    sp.dma_start(vec_rows[r0:r0 + ap.shape[0], 0, :], ap).then_inc(vec_in, 16)
                cw = conv_ffn_w[0].rearrange("k (r p) -> (k r) p", p=P)
                sp.dma_start(vec_rows[0:2 * KF, 1, :], cw[0:2 * KF, :]).then_inc(vec_in, 16)
                sp.dma_start(vec_rows[0:KF, 2, :], cw[2 * KF:3 * KF, :]).then_inc(vec_in, 16)
                sp.dma_start(vec_rows[KF:2 * KF, 2, :], conv_ffn_b[0].rearrange("(r p) -> r p", p=P)).then_inc(vec_in, 16)

            for i in range(M_IT):
                n, _ = place("M", i)
                for c, col in enumerate((offset["mq"] + i * COLS, offset["mk"] + i * COLS,
                                         offset["mv"] + 2 * i * COLS, offset["mv"] + (2 * i + 1) * COLS,
                                         offset["mo"] + 2 * i * COLS, offset["mo"] + (2 * i + 1) * COLS)):
                    if i == 0 and c == 2:
                        load_vectors()
                    load_group(n + 2 * c, 2 * c, w_in, col)
            with sp.Fori(0, A_IT) as i:
                n, _ = place("A", i)
                for c, name in enumerate(("aq", "ak", "av")):
                    load_group(n + 2 * c, 2 * c, w_in, offset[name] + i * COLS)
                for c in range(3):
                    load_group(n + 6 + 2 * c, 6 + 2 * c, w_in, offset["gates"] + (3 * i + c) * COLS)
            with sp.Fori(0, G_IT) as i:
                n, _ = place("G", i)
                for c in range(2):
                    load_group(n + 2 * c, 2 * c, w_in, offset["gates"] + A_GATES * COLS + (2 * i + c) * COLS)
            with sp.Fori(0, B_IT) as i:
                n, _ = place("B", i)
                for c in range(2):
                    load_group(n + 2 * c, 2 * c, w_branch_m, (2 * i + c) * COLS, 1)
                    load_group(n + 2 * c + 1, 2 * c + 1, w_branch_a, (2 * i + c) * COLS, 1)
            with sp.Fori(0, O_IT) as i:
                n, _ = place("O", i)
                for c in range(2):
                    load_group(n + 2 * c, 2 * c, w_out, (2 * i + c) * COLS)
            with sp.Fori(0, U_IT) as i:
                n, _ = place("U", i)
                load_group(n, 0, w_up, i * COLS)
                load_group(n + 2, 2, w_up, D_FF + i * COLS)
            with sp.Fori(0, D_IT) as i:
                n, _ = place("D", i)
                for c in range(2):
                    for k, kn in enumerate(DOWN_TILES):
                        load(n + NDT * c + k, NDT * c + k, w_down, k * TILE_K, kn, (2 * i + c) * COLS)
            outr = out[0].rearrange("(t p) d -> p t d", p=P)
            for f in range(8):
                tt, q = f % 2, f // 2
                sp.wait_ge(rows_a if f % 2 == 0 else rows_v, f // 2 + 1)
                sp.dma_start(outr[:, tt, q * 512:(q + 1) * 512], rows_out[:, tt, q * 512:(q + 1) * 512]).then_inc(rows_stored, 16)
            sp.wait_ge(rows_stored, 8 * 16)

        @block.gpsimd
        def _(pool):
            own = OwnSteps(pool, pool_own)
            own.add(nc.gpsimd.memset(ident[:], 0.0))
            own.settle()
            nc.gpsimd.affine_select(out=ident[:], in_=ident[:], compare_op=ALU.not_equal, fill=1.0, base=0,
                                    pattern=[[-1, P]], channel_multiplier=1).then_inc(pool_const, 1)
            own.add(nc.gpsimd.memset(wif_raw[:], 0.0))
            own.settle()
            wi = w_in[0].rearrange("(k p) c -> p k c", p=P)
            with nc.allow_non_contiguous_dma(reason="four columns of each gate"):
                pool.dma_start(wif_raw[:, :, 0:2 * M_H], wi[:, :, offset["mi"]:offset["mi"] + 2 * M_H]).then_inc(wif_in, 16)
                pool.dma_start(if_bias[0:M_H, 0:1], b_igate.rearrange("a h -> h a")).then_inc(wif_in, 16)
                pool.dma_start(if_bias[32:32 + M_H, 0:1], b_fgate.rearrange("a h -> h a")).then_inc(wif_in, 16)
            pool.dma_start(rel_rows[:, 0:REL], rel_bias[0]).then_inc(rel_in, 16)
            for buf, value in ((future, 0.0), (ident_half, 0.0), (pick, 0.0), (ones, 1.0)):
                own.add(nc.gpsimd.memset(buf[:], value))
            own.settle()
            nc.gpsimd.affine_select(out=future[:], in_=future[:], compare_op=ALU.is_ge, fill=BIG, base=0,
                                    pattern=[[1, P]], channel_multiplier=-1).then_inc(pool_const, 1)
            nc.gpsimd.affine_select(out=ident_half[:], in_=ident_half[:], compare_op=ALU.not_equal, fill=1.0, base=0,
                                    pattern=[[-1, P]], channel_multiplier=1).then_inc(pool_const, 1)
            nc.gpsimd.affine_select(out=pick[:], in_=pick[:], compare_op=ALU.not_equal, fill=1.0, base=0,
                                    pattern=[[-1, M_H], [0, P]], channel_multiplier=1).then_inc(pool_const, 1)
            pool.wait_ge(wif_in, 3 * 16)
            nc.gpsimd.tensor_copy(wif_raw[:, :, 32:32 + M_H], wif_raw[:, :, M_H:2 * M_H]).then_inc(wif_placed, 1)
            pool.wait_ge(rel_pad, 1)
            pool.dma_start(tpad.ap(), rel_rows[:]).then_inc(tpad_out, 16)
            pool.wait_ge(tpad_out, 16)
            pool.wait_ge(x_turned, KD)
            pool.wait_ge(wif_lo, 1)
            for b in range(2):
                src = bass.AP(tensor=tpad, offset=1 + P * b, ap=[[1, P], [3 * P, A_H], [1, P]])
                pool.dma_start(hankel[:, :, b, :], src).then_inc(hankel_in, 16)
            pool.wait_ge(hankel_in, 32)
            for part, b in ((0, 0), (1, 1), (2, 0)):
                own.add(nc.gpsimd.tensor_copy(bias_qk[:, :, part * P:(part + 1) * P], hankel[:, :, b, ::-1]))
            own.settle()
            for part in (0, 2):
                nc.gpsimd.memset(bias_qk[0:CHUNK, :, part * P + CHUNK:(part + 1) * P], -BIG).then_inc(bias_ready, 1)
            for i in range(M_IT):
                for h in range(2):
                    pool.wait_ge(hsq_ready, 2 * i + h + 1)
                    nc.gpsimd.tensor_tensor(hsq[:, h, 0], hsq[:, h, 0], hsq[:, h, 1], ALU.add).then_inc(hsq_summed, 1)
                for h in range(2):
                    pool.wait_ge(inv_ready, i + 1)
                    own.add(nc.gpsimd.tensor_tensor(hval[:, h], hval[:, h], inv[:, h:h + 1, :].to_broadcast([P, 2, S]), ALU.mult))
                    own.settle()
                    pool.wait_ge(mo_ready, 2 * i + h + 1)
                    nc.gpsimd.tensor_tensor(hm_values[:, 4 * i + 2 * h:4 * i + 2 * h + 2, 0:S], hval[:, h],
                                            mo_sum[:, h], ALU.mult).then_inc(hm_ready, 1)
            for half in range(2):
                pool.wait_ge(merged_ready, (half + 1) * B_IT)
                for tt in range(TT):
                    pool.dma_start(x_again[:, half * B_IT:(half + 1) * B_IT, tt, :],
                                   x[0, tt * P:(tt + 1) * P, half * (D // 2):(half + 1) * (D // 2)].rearrange(
                                       "p (m c) -> p m c", c=COLS)).then_inc(x_again_in[half], 16)
            with pool.Fori(0, O_IT) as i:
                for c in range(2):
                    pool.wait_ge(x2_ready, 2 * i + c + 1)
                    pool.dma_start(x2_dram[:, bass.ds((2 * i + c) * 2 * S, 2 * S)],
                                   sums[:, c].rearrange("p a s -> p (a s)")).then_inc(x2_stored[c], 16)
            for c in range(2):
                pool.wait_ge(x2_stored[c], O_IT * 16)
            pool.wait_ge(half_used, 2 * seg["D"][0])
            pool.dma_start(x3[:].rearrange("p k s -> p (k s)"), x2_dram).then_inc(x3_in, 16)

        @block.scalar
        def _(act):
            own = OwnSteps(act, act_own)
            A = nc.scalar.activation
            def ahead(name, i, j):
                t0, _, tiles, _ = seg[name]
                slot, kh = (j + AHEAD) % RAW_SLOTS, tile_rows(j + AHEAD, name) // 2
                act.wait_ge(w_loaded[slot], 16 * ((t0 + j + AHEAD) // RAW_SLOTS + 1) + i * (16 * tiles // RAW_SLOTS))
                for f in range(2):
                    act.wait_ge(half_used, 2 * (t0 + j) + f + 1 + i * (2 * tiles))
                    A(parts[:, (2 * j + f) % HALF_SLOTS, 0:kh, 0, :], raw[:, slot, f * kh:(f + 1) * kh, :],
                      ACT.Copy).then_inc(hi_ready, 1)

            def copy_low(name, i, c, last_j, scale=1.0):
                t0, g0, tiles, groups = seg[name]
                act.wait_ge(half_used, 2 * (t0 + last_j + 1) + i * (2 * tiles))
                A(lows[:, c % 2], main[:, c % 2, :, S:2 * S], ACT.Copy, scale=scale).then_inc(low_copied, 1)

            def summed(name, i, c):
                _, g0, _, groups = seg[name]
                act.wait_ge(group_summed, g0 + c + 1 + i * groups)

            act.wait_ge(eps_ready, 1)
            own.add(A(small[:, 30:31], small[:, 31:32], ACT.Sqrt))
            for k in range(2 * TT):
                tt, half = k % 2, slice(k // 2 * (D // 2), (k // 2 + 1) * (D // 2))
                act.wait_ge(x_in[k], 16)
                if k >= 2:
                    act.wait_ge(x_sq, k - 1)
                A(junk[:, tt * (D // 2):(tt + 1) * (D // 2)], x_rows[:, tt, half], ACT.Square,
                  accum_out=small[:, k:k + 1]).then_inc(x_sq, 1)
            act.wait_ge(x_ss, 1)
            A(small[:, 6:8], small[:, 4:6], ACT.Sqrt, bias=small[:, 31:32], scale=1.0 / D).then_inc(x_rms, 1)
            act.wait_ge(vec_t, 1)
            A(vec[:, V_MIX:V_MIX + KD], aux[:, 3, 0:KD], ACT.Copy).then_inc(vec_ready, 1)
            act.wait_ge(x_r, 1)

            def scale_x(*quarters):
                for q in quarters:
                    A(x_piece(q, 1), x_piece(q, 1), ACT.Copy, scale=small[:, 5:6]).then_inc(x_scaled_a, 1)

            scale_x(0, 1)
            act.wait_ge(vec_ready, 1)
            for q in range(4):
                if q == 1:
                    scale_x(2, 3)
                for k in range(4 * q, 4 * q + 4):
                    act.wait_ge(x_turned, k // 2 * 2 + 2)
                    A(h_parts[:, k, 0:S], turn_bank(k), ACT.Copy, scale=vcol(V_MIX + k)).then_inc(h_hi, 1)
                j, f = q // 2, q % 2
                if f == 0:
                    act.wait_ge(w_loaded[j], 16)
                A(parts[:, q, :, 0, :], raw[:, j, f * HALF_K:(f + 1) * HALF_K], ACT.Copy).then_inc(hi_ready, 1)
            act.wait_ge(wif_placed, 1)
            A(wif_parts[:, :, 0, :], wif_raw[:], ACT.Copy).then_inc(wif_hi, 1)

            def gates_low():
                act.wait_ge(if_done, 1)
                own.add(A(if_low_sb[:, 0, :], aux[0:64, 0, S:2 * S], ACT.Copy))
                A(if_low_sb[:, 1, :], aux[64:128, 0, 0:S], ACT.Copy).then_inc(if_low, 1)

            def gates_log():
                act.wait_ge(z_ready, 1)
                own.add(A(abs_row[:], z_row[:], ACT.Abs))
                own.settle()
                own.add(A(log_row[:], abs_row[:], ACT.Exp, scale=-1.0))
                own.settle()
                A(log_row[:], log_row[:], ACT.Ln, bias=1.0).then_inc(log_term, 1)

            def turn_c():
                act.wait_ge(c_turned, 1)
                A(ccol, aux[:, 1, 0:TT * M_H], ACT.Copy).then_inc(c_ready, 1)

            for i in range(M_IT):
                def first_taps(which):
                    summed("M", i, which)
                    for c in range(2):
                        ch = M_H * which + 2 * i + c
                        A(conv_out[:, c, :], conv_in[:, c, 4:4 + S], ACT.Identity, scale=vcol(V_CW + 3 * 8 + ch),
                          bias=vcol(V_CB + ch)).then_inc(first_tap, 1)

                def conv_silu(which):
                    act.wait_ge(conv_done, 2 * i + which + 1)
                    A((mq, mk)[which][:], conv_out[:], ACT.Silu).then_inc(mqk_ready, 1)

                def decays():
                    for h in range(2):
                        act.wait_ge(mqk_done, 2 * i + h + 1)
                        hd = 2 * i + h
                        own.add(A(decay[:, h, 0:S], aux[:, 2 + h, 0:S], ACT.Exp, bias=ccol[:, hd:hd + 1], scale=-1.0))
                        A(decay[:, h, S:S + P], aux[:, 2 + h, S:S + P], ACT.Exp, bias=ccol[:, M_H + hd:M_H + hd + 1],
                          scale=-1.0).then_inc(decay_ready, 1)

                ahead("M", i, 0)
                ahead("M", i, 1)
                copy_low("M", i, 0, 1)
                if i == 0:
                    act.wait_ge(vec_t, 2)
                    A(vec[:, KD:P + 4 * KF], aux[:, 3, KD:P + 4 * KF], ACT.Copy).then_inc(vec_ready, 1)
                    act.wait_ge(vec_ready, 2)
                first_taps(0)
                ahead("M", i, 2)
                conv_silu(0)
                if i == 0:
                    gates_low()
                ahead("M", i, 3)
                copy_low("M", i, 1, 3)
                first_taps(1)
                ahead("M", i, 4)
                conv_silu(1)
                if i == 0:
                    gates_log()
                ahead("M", i, 5)
                copy_low("M", i, 2, 5)
                ahead("M", i, 6)
                if i == 0:
                    turn_c()
                    act.wait_ge(c_ready, 1)
                decays()
                ahead("M", i, 7)
                copy_low("M", i, 3, 7)
                ahead("M", i, 8)
                for h in range(2):
                    act.wait_ge(mnum_done, 2 * i + h + 1)
                    if i:
                        act.wait_ge(hm_ready, M_H // 2)
                    A(inv[:, h, :], aux[:, 2 + h, S:2 * S], ACT.Exp, scale=-1.0).then_inc(floor_ready, 1)
                for h in range(2):
                    act.wait_ge(h_ready, 2 * i + h + 1)
                    A(hsq[:, h], hval[:, h], ACT.Square).then_inc(hsq_ready, 1)
                ahead("M", i, 9)
                copy_low("M", i, 4, 9)
                summed("M", i, 4)
                A(mo_sum[:, 0], mo_sum[:, 0], ACT.Sigmoid).then_inc(mo_ready, 1)
                ahead("M", i, 10)
                act.wait_ge(mss_done, i + 1)
                A(inv[:], aux[:, 2, :].rearrange("p (h s) -> p h s", h=2), ACT.Sqrt, bias=small[:, 31:32],
                  scale=1.0 / DV).then_inc(mrms_ready, 1)
                ahead("M", i, 11)
                copy_low("M", i, 5, 11)
                summed("M", i, 5)
                A(mo_sum[:, 1], mo_sum[:, 1], ACT.Sigmoid).then_inc(mo_ready, 1)

            def gate(name, i, c, index):
                summed(name, i, c)
                for k in range(2):
                    A(gates[:, bass.ds(2 * index + k, 1), :], sums[:, 0, k:k + 1, :], ACT.Sigmoid,
                      bias=vcol(2 * index + k + V_GB)).then_inc(gate_done, 1)

            with act.Fori(0, A_IT) as i:
                for c in range(3):
                    ahead("A", i, 2 * c)
                    ahead("A", i, 2 * c + 1)
                    copy_low("A", i, c, 2 * c + 1, scale=DH ** -0.5 if c == 0 else 1.0)
                ahead("A", i, 6)
                for h in range(2):
                    act.wait_ge(a_max, 2 * i + h + 1)
                    A(scores[:, h, 0:P], scores[:, h, 0:P], ACT.Exp, bias=small[:, 8 + 2 * h:9 + 2 * h],
                      accum_out=small[:, 12 + 2 * h:13 + 2 * h]).then_inc(a_exp, 1)
                    A(scores[:, h, P:3 * P], scores[:, h, P:3 * P], ACT.Exp, bias=small[:, 9 + 2 * h:10 + 2 * h],
                      accum_out=small[:, 13 + 2 * h:14 + 2 * h]).then_inc(a_exp, 1)
                ahead("A", i, 7)
                copy_low("A", i, 3, 7)
                act.wait_ge(hm_ready, M_H)
                gate("A", i, 3, 3 * i)
                ahead("A", i, 8)
                for h in range(2):
                    act.wait_ge(a_turned, 2 * i + h + 1)
                    A(probs_t[:, h], aux[:, 2 + h, 0:3 * P], ACT.Copy).then_inc(a_copied, 1)
                ahead("A", i, 9)
                copy_low("A", i, 4, 9)
                gate("A", i, 4, 3 * i + 1)
                ahead("A", i, 10)
                act.wait_ge(a_out, i + 1)
                A(ha_parts[:, bass.ds(2 * i, 2), 0:S], aux[:, 0, :].rearrange("p (h s) -> p h s", h=2), ACT.Copy).then_inc(ha_hi, 1)
                ahead("A", i, 11)
                copy_low("A", i, 5, 11)
                gate("A", i, 5, 3 * i + 2)
            with act.Fori(0, G_IT) as i:
                for c in range(2):
                    ahead("G", i, 2 * c)
                    for k in range(2):
                        both, values = (buf[:, bass.ds(4 * i + 2 * c + k, 1), :] for buf in (hm_parts, hm_values))
                        A(both[:, :, S:2 * S], values[:, :, 0:S], ACT.Copy,
                          scale=vcol(4 * i + 2 * c + k + V_MN)).then_inc(hm_hi, 1)
                    ahead("G", i, 2 * c + 1)
                    copy_low("G", i, c, 2 * c + 1)
                    gate("G", i, c, 2 * i + c + A_GATES)
            act.wait_ge(ha_lo, A_IT)
            with act.Fori(0, B_IT) as i:
                for c in range(2):
                    ahead("B", i, 2 * c)
                    copy_low("B", i, 2 * c, 2 * c)
                    ahead("B", i, 2 * c + 1)
                    copy_low("B", i, 2 * c + 1, 2 * c + 1)
                    act.wait_ge(merged_ready, 2 * i + c + 1)
                    A(merged_parts[:, bass.ds(4 * i + 2 * c, 2), 0:S], sums[:, 0], ACT.Copy).then_inc(merged_hi, 1)
            act.wait_ge(x_again_in[0], TT * 16)
            with act.Fori(0, O_IT) as i:
                for c in range(2):
                    A(x_stage[:].rearrange("p t (o c) -> p o t c", o=1), x_again[:, bass.ds(2 * i + c, 1), :, :], ACT.Copy).then_inc(xs_copied, 1)
                    ahead("O", i, 2 * c)
                    ahead("O", i, 2 * c + 1)
                    copy_low("O", i, c, 2 * c + 1)
                    act.wait_ge(x2_ready, 2 * i + c + 1)
                    for k in range(2):
                        A(h_parts[:, bass.ds(4 * i + 2 * c + k, 1), 0:S], sums[:, c, k:k + 1, :], ACT.Copy,
                          scale=vcol(4 * i + 2 * c + k + V_FFN)).then_inc(h2_hi, 1)
                    A(squares[:], sums[:, c], ACT.Square).then_inc(x2_sq, 1)
                act.wait_ge(x_again_in[1], TT * 16)

            def up(i, first):
                ahead("U", i, 0)
                ahead("U", i, 1)
                if first:
                    act.wait_ge(ss_done, 1)
                    A(r_bc[:], aux[:, 0, 0:S], ACT.Sqrt, bias=small[:, 31:32], scale=1.0 / D).then_inc(rms_ready, 1)
                copy_low("U", i, 0, 1)
                for k in range(2):
                    act.wait_ge(u_scaled, i + 1)
                    A(u_conv_out[:, k, :], u_conv_in[:, k, 2:2 + S], ACT.Identity, scale=vcol(2 * i + k + V_UW + 2 * KF),
                      bias=vcol(2 * i + k + V_UB)).then_inc(u_tap, 1)
                ahead("U", i, 2)
                act.wait_ge(u_conv, 2 * i + 2)
                A(u_silu[:], u_conv_out[:], ACT.Silu).then_inc(u_silu_done, 1)
                ahead("U", i, 3)
                copy_low("U", i, 1, 3)
                act.wait_ge(u_act, i + 1)
                A(act_parts[:, bass.ds(2 * i, 2), 0:S], sums[:, 1], ACT.Copy).then_inc(act_hi, 1)

            up(0, True)
            with act.Fori(1, U_IT) as i:
                up(i, False)

            def down(i, last):
                for c in range(2):
                    for k in range(NDT):
                        j = NDT * c + k
                        if not (last and j >= 2 * NDT - AHEAD):
                            ahead("D", i, j)
                    copy_low("D", i, c, NDT * (c + 1) - 1)
                    act.wait_ge(x3_ready, 2 * i + c + 1)
                    A(squares[:], x3[:, bass.ds(4 * i + 2 * c, 2), :], ACT.Square).then_inc(x3_sq, 1)

            own.add(A(small[:, 30:31], small[:, 31:32], ACT.Sqrt))
            with act.Fori(0, D_IT - 1) as i:
                down(i, False)
            down(D_IT - 1, True)
            act.wait_ge(fin_ss, 1)
            A(small[:, 2:4], row_bank(7)[:, 0:TT], ACT.Sqrt, bias=small[:, 31:32], scale=1.0 / D).then_inc(fin_rms, 1)
            act.wait_ge(fin_r, 1)
            for f in range(0, 8, 2):
                tt, q = f % 2, f // 2
                act.wait_ge(rows_turned, f + 1)
                A(rows_out[:, tt, q * 512:(q + 1) * 512], row_bank(f), ACT.Copy, scale=small[:, 4 + tt:5 + tt]).then_inc(rows_a, 1)

        @block.vector
        def _(dve):
            own = OwnSteps(dve, dve_own)
            V = nc.vector

            def ahead(name, i, j):
                t0, _, tiles, _ = seg[name]
                slot, kh = (j + AHEAD) % RAW_SLOTS, tile_rows(j + AHEAD, name) // 2
                for f in range(2):
                    dve.wait_ge(hi_ready, 2 * (t0 + j + AHEAD) + f + 1 + i * (2 * tiles))
                    place = parts[:, (2 * j + f) % HALF_SLOTS, 0:kh]
                    V.tensor_tensor(place[:, :, 1, :], raw[:, slot, f * kh:(f + 1) * kh, :],
                                    place[:, :, 0, :].bitcast(F32), ALU.subtract).then_inc(lo_ready, 1)

            def add_group(name, i, c, dst, scale=1.0):
                _, g0, _, groups = seg[name]
                dve.wait_ge(low_copied, g0 + c + 1 + i * groups)
                V.scalar_tensor_tensor(dst, main[:, c % 2, :, 0:S], scale, lows[:, c % 2], ALU.mult, ALU.add).then_inc(group_summed, 1)

            def summed(name, i, c):
                _, g0, _, groups = seg[name]
                dve.wait_ge(group_summed, g0 + c + 1 + i * groups)

            V.memset(small[:, 31:32], EPS).then_inc(eps_ready, 1)
            own.add(V.memset(acc[:], 0.0))
            own.add(V.memset(conv_in[:, :, 0:4], 0.0))
            dve.wait_ge(x_sq, 2 * TT)
            V.tensor_tensor(small[:, 4:6], small[:, 0:2], small[:, 2:4], ALU.add).then_inc(x_ss, 1)
            dve.wait_ge(x_rms, 1)
            V.reciprocal(small[:, 4:6], small[:, 6:8]).then_inc(x_r, 1)
            dve.wait_ge(x_r, 1)

            def scale_x(*quarters):
                for q in quarters:
                    V.tensor_scalar(x_piece(q, 0), x_piece(q, 0), small[:, 4:5], None, ALU.mult).then_inc(x_scaled_v, 1)

            scale_x(0, 1)
            for q in range(4):
                if q == 1:
                    scale_x(2, 3)
                for k in range(4 * q, 4 * q + 4):
                    dve.wait_ge(h_hi, k // 2 * 2 + 2)
                    V.scalar_tensor_tensor(h_parts[:, k, S:2 * S], turn_bank(k), vcol(V_MIX + k),
                                           h_parts[:, k, 0:S].bitcast(F32), ALU.mult, ALU.subtract).then_inc(h_lo, 1)
                dve.wait_ge(hi_ready, q + 1)
                V.tensor_tensor(parts[:, q, :, 1, :], raw[:, q // 2, (q % 2) * HALF_K:(q % 2 + 1) * HALF_K],
                                parts[:, q, :, 0, :].bitcast(F32), ALU.subtract).then_inc(lo_ready, 1)
            dve.wait_ge(wif_hi, 1)
            V.tensor_tensor(wif_parts[:, :, 1, :], wif_raw[:], wif_parts[:, :, 0, :].bitcast(F32), ALU.subtract).then_inc(wif_lo, 1)
            dve.wait_ge(rel_in, 16)
            V.tensor_copy(rel_rows[:, REL:3 * P],
                          rel_rows[:, REL - 1:REL].to_broadcast([A_H, 3 * P - REL])).then_inc(rel_pad, 1)

            def gate_rows():
                dve.wait_ge(if_low, 1)
                own.add(V.tensor_tensor(if_sum[:], aux[0:64, 0, 0:S], if_low_sb[:, 0, :], ALU.add))
                own.settle()
                own.add(V.tensor_tensor(if_sum[:], if_sum[:], if_low_sb[:, 1, :], ALU.add))
                own.settle()
                own.add(V.tensor_scalar(li_row[:], if_sum[0:M_H, :], if_bias[0:M_H, 0:1], None, ALU.add))
                V.tensor_scalar(z_row[:], if_sum[32:32 + M_H, :], if_bias[32:32 + M_H, 0:1], None, ALU.add).then_inc(z_ready, 1)

            def running_rows():
                dve.wait_ge(log_term, 1)
                own.add(V.scalar_tensor_tensor(z_row[:], z_row[:], 0.0, log_row[:], ALU.min, ALU.subtract))
                own.settle()
                dve.wait_ge(pool_const, 4)
                own.add(V.tensor_tensor_scan(abs_row[:], ones[0:M_H, :], z_row[:], 0.0, ALU.mult, ALU.add))
                own.settle()
                V.tensor_tensor(li_row[:], li_row[:], abs_row[:], ALU.subtract).then_inc(c_row_ready, 1)
                dve.wait_ge(c_row_ready, 1)
                own.add(V.tensor_tensor_scan(g_row[:], li_row[:], li_row[:], -3e38, ALU.max, ALU.max))
                own.settle()
                V.tensor_tensor(m_row[:], abs_row[:], g_row[:], ALU.add).then_inc(c_row_ready, 1)

            for i in range(M_IT):
                def conv(which):
                    for k, tap in enumerate((2, 1, 0)):
                        for c in range(2):
                            ch = M_H * which + 2 * i + c
                            if k == 0:
                                dve.wait_ge(first_tap, 4 * i + 2 * which + c + 1)
                            ins = V.scalar_tensor_tensor(conv_out[:, c, :], conv_in[:, c, tap + 1:tap + 1 + S],
                                                         vcol(V_CW + tap * 8 + ch), conv_out[:, c, :], ALU.mult, ALU.add)
                            if tap == 0 and c == 1:
                                ins.then_inc(conv_done, 1)
                            else:
                                own.add(ins)
                        if tap:
                            own.settle()

                for which in range(2):
                    ahead("M", i, 2 * which)
                    if i == 0 and which == 1:
                        gate_rows()
                    ahead("M", i, 2 * which + 1)
                    add_group("M", i, which, conv_in[:, :, 4:4 + S])
                    conv(which)
                ahead("M", i, 4)
                if i == 0:
                    running_rows()
                ahead("M", i, 5)
                add_group("M", i, 2, mv[:, :, 0:DV])
                ahead("M", i, 6)
                for h in range(2):
                    dve.wait_ge(decay_ready, 2 * i + h + 1)
                    V.scalar_tensor_tensor(mprobs[:, h], aux[:, h, 0:3 * P], DK ** -0.5, decay[:, h], ALU.mult,
                                           ALU.mult).then_inc(mprob_ready, 1)
                ahead("M", i, 7)
                add_group("M", i, 3, mv[:, :, DV:2 * DV])
                ahead("M", i, 8)
                for h in range(2):
                    dve.wait_ge(floor_ready, 2 * i + h + 1)
                    if i:
                        dve.wait_ge(hm_ready, M_H // 2)
                    own.add(V.scalar_tensor_tensor(inv[:, h, :], aux[:, 2 + h, 0:S], -1.0, inv[:, h, :], ALU.mult, ALU.max))
                    own.settle()
                    own.add(V.tensor_tensor(inv[:, h, :], aux[:, 2 + h, 0:S], inv[:, h, :], ALU.max))
                    own.settle()
                    own.add(V.reciprocal(inv[:, h, :], inv[:, h, :]))
                    own.settle()
                    V.tensor_tensor(hval[:, h], aux[:, h, :].rearrange("p (v s) -> p v s", v=2),
                                    inv[:, h:h + 1, :].to_broadcast([P, 2, S]), ALU.mult).then_inc(h_ready, 1)
                ahead("M", i, 9)
                if i:
                    dve.wait_ge(hm_ready, M_H // 2)
                add_group("M", i, 4, mo_sum[:, 0])
                ahead("M", i, 10)
                dve.wait_ge(mrms_ready, i + 1)
                V.reciprocal(inv[:], inv[:]).then_inc(inv_ready, 1)
                ahead("M", i, 11)
                add_group("M", i, 5, mo_sum[:, 1])

            with dve.Fori(0, A_IT) as i:
                own.enter(i, 10)
                for c, dst in enumerate((aq[:], ak[:], av[:])):
                    ahead("A", i, 2 * c)
                    ahead("A", i, 2 * c + 1)
                    add_group("A", i, c, dst, scale=DH ** -0.5 if c == 0 else 1.0)
                ahead("A", i, 6)
                dve.wait_ge(bias_ready, 2)
                for h in range(2):
                    dve.wait_ge(a_scored, 2 * i + h + 1)
                    own.add(V.tensor_tensor(scores[:, h:h + 1, :], aux[:, h:h + 1, 0:3 * P],
                                            bias_qk[:, bass.ds(2 * i + h, 1), :], ALU.add))
                    own.settle()
                    own.add(V.tensor_reduce(small[:, 16 + 2 * h:17 + 2 * h], scores[:, h, 0:P], AX_X, ALU.max))
                    own.add(V.tensor_reduce(small[:, 17 + 2 * h:18 + 2 * h], scores[:, h, P:3 * P], AX_X, ALU.max))
                    own.settle()
                    V.tensor_scalar(small[:, 8 + 2 * h:10 + 2 * h], small[:, 16 + 2 * h:18 + 2 * h], -1.0, None,
                                    ALU.mult).then_inc(a_max, 1)
                for h in range(2):
                    dve.wait_ge(a_exp, 4 * i + 2 * h + 2)
                    own.add(V.reciprocal(small[:, 20 + 2 * h:22 + 2 * h], small[:, 12 + 2 * h:14 + 2 * h]))
                    own.settle()
                    own.add(V.tensor_scalar(scores[:, h, 0:P], scores[:, h, 0:P], small[:, 20 + 2 * h:21 + 2 * h], None, ALU.mult))
                    V.tensor_scalar(scores[:, h, P:3 * P], scores[:, h, P:3 * P], small[:, 21 + 2 * h:22 + 2 * h], None,
                                    ALU.mult).then_inc(a_prob, 1)
                for c in range(2):
                    ahead("A", i, 7 + 2 * c)
                    add_group("A", i, 3 + c, sums[:, 0])
                    ahead("A", i, 8 + 2 * c)
                dve.wait_ge(ha_hi, i + 1)
                dst = ha_parts[:, bass.ds(2 * i, 2), :]
                V.tensor_tensor(dst[:, :, S:2 * S], aux[:, 0, :].rearrange("p (h s) -> p h s", h=2),
                                dst[:, :, 0:S].bitcast(F32), ALU.subtract).then_inc(ha_lo, 1)
                ahead("A", i, 11)
                add_group("A", i, 5, sums[:, 0])
            own.leave(A_IT)
            with dve.Fori(0, G_IT) as i:
                for c in range(2):
                    ahead("G", i, 2 * c)
                    for k in range(2):
                        dve.wait_ge(hm_hi, 4 * i + 2 * c + k + 1)
                        both, values = (buf[:, bass.ds(4 * i + 2 * c + k, 1), :] for buf in (hm_parts, hm_values))
                        V.scalar_tensor_tensor(both[:, :, 0:S], values[:, :, 0:S], vcol(4 * i + 2 * c + k + V_MN),
                                               both[:, :, S:2 * S].bitcast(F32), ALU.mult, ALU.subtract).then_inc(hm_lo, 1)
                    ahead("G", i, 2 * c + 1)
                    add_group("G", i, c, sums[:, 0])
            dve.wait_ge(gate_done, 2 * KD)
            with dve.Fori(0, B_IT) as i:
                own.enter(i, 4)
                for c in range(2):
                    for b in range(2):
                        ahead("B", i, 2 * c + b)
                        add_group("B", i, 2 * c + b, sums[:, b])
                        summed("B", i, 2 * c + b)
                        own.add(V.tensor_tensor(sums[:, b], sums[:, b], gates[:, bass.ds(4 * i + 2 * c + b * KD, 2), :], ALU.mult))
                    own.settle()
                    V.tensor_tensor(sums[:, 0], sums[:, 0], sums[:, 1], ALU.add).then_inc(merged_ready, 1)
                    dve.wait_ge(merged_hi, 2 * i + c + 1)
                    dst = merged_parts[:, bass.ds(4 * i + 2 * c, 2), :]
                    V.tensor_tensor(dst[:, :, S:2 * S], sums[:, 0], dst[:, :, 0:S].bitcast(F32), ALU.subtract).then_inc(merged_lo, 1)
                    dve.wait_ge(merged_lo, 2 * i + c + 1)
            own.leave(B_IT)

            with dve.Fori(0, O_IT) as i:
                for c in range(2):
                    ahead("O", i, 2 * c)
                    ahead("O", i, 2 * c + 1)
                    add_group("O", i, c, sums[:, c])
                    summed("O", i, c)
                    dve.wait_ge(xt_done, 2 * i + c + 1)
                    V.tensor_tensor(sums[:, c], sums[:, c], aux[:, c, :].rearrange("p (k s) -> p k s", k=2),
                                    ALU.add).then_inc(x2_ready, 1)
                    dve.wait_ge(x2_ready, 2 * i + c + 1)
                    for k in range(2):
                        dve.wait_ge(h2_hi, 4 * i + 2 * c + k + 1)
                        dst = h_parts[:, bass.ds(4 * i + 2 * c + k, 1), :]
                        V.scalar_tensor_tensor(dst[:, :, S:2 * S], sums[:, c, k:k + 1, :], vcol(4 * i + 2 * c + k + V_FFN),
                                               dst[:, :, 0:S].bitcast(F32), ALU.mult, ALU.subtract).then_inc(h2_lo, 1)
                    dve.wait_ge(x2_sq, 2 * i + c + 1)
                    V.tensor_tensor(acc[:], acc[:], squares[:], ALU.add).then_inc(acc_ready, 1)
                    dve.wait_ge(acc_ready, 2 * i + c + 1)
                for c in range(2):
                    dve.wait_ge(x2_stored[c], 16 * i + 16)
            own.add(V.memset(u_conv_in[:, :, 0:2], 0.0))
            own.settle()
            r_two = r_bc[:].rearrange("p (o s) -> p o s", o=1).to_broadcast([P, 2, S])

            def up(i, first):
                ahead("U", i, 0)
                ahead("U", i, 1)
                if first:
                    dve.wait_ge(rms_ready, 1)
                    own.add(V.reciprocal(r_bc[:], r_bc[:]))
                    own.add(V.memset(acc[:], 0.0))
                    own.settle()
                add_group("U", i, 0, sums[:, 0])
                summed("U", i, 0)
                V.tensor_tensor(u_conv_in[:, :, 2:2 + S], sums[:, 0], r_two, ALU.mult).then_inc(u_scaled, 1)
                for c in range(2):
                    dve.wait_ge(u_tap, 2 * i + c + 1)
                    own.add(V.scalar_tensor_tensor(u_conv_out[:, c, :], u_conv_in[:, c, 1:1 + S], vcol(2 * i + c + V_UW + KF),
                                                   u_conv_out[:, c, :], ALU.mult, ALU.add))
                own.settle()
                for c in range(2):
                    V.scalar_tensor_tensor(u_conv_out[:, c, :], u_conv_in[:, c, 0:S], vcol(2 * i + c + V_UW),
                                           u_conv_out[:, c, :], ALU.mult, ALU.add).then_inc(u_conv, 1)
                ahead("U", i, 2)
                dve.wait_ge(u_conv, 2 * i + 2)
                ahead("U", i, 3)
                add_group("U", i, 1, sums[:, 1])
                summed("U", i, 1)
                own.add(V.tensor_tensor(sums[:, 1], sums[:, 1], r_two, ALU.mult))
                own.settle()
                dve.wait_ge(u_silu_done, i + 1)
                V.tensor_tensor(sums[:, 1], sums[:, 1], u_silu[:], ALU.mult).then_inc(u_act, 1)
                dve.wait_ge(act_hi, i + 1)
                dst = act_parts[:, bass.ds(2 * i, 2), :]
                V.tensor_tensor(dst[:, :, S:2 * S], sums[:, 1], dst[:, :, 0:S].bitcast(F32), ALU.subtract).then_inc(act_lo, 1)
                dve.wait_ge(act_lo, i + 1)

            up(0, True)
            with dve.Fori(1, U_IT) as i:
                own.enter(i - 1, 3)
                up(i, False)
            own.leave(U_IT - 1)

            def down(i, last):
                for c in range(2):
                    for k in range(NDT):
                        j = NDT * c + k
                        if not (last and j >= 2 * NDT - AHEAD):
                            ahead("D", i, j)
                    add_group("D", i, c, sums[:, c])
                    summed("D", i, c)
                    dve.wait_ge(x3_in, 16)
                    here = x3[:, bass.ds(4 * i + 2 * c, 2), :]
                    V.tensor_tensor(here, here, sums[:, c], ALU.add).then_inc(x3_ready, 1)
                    dve.wait_ge(x3_sq, 2 * i + c + 1)
                    if not (last and c):
                        own.add(V.tensor_tensor(acc[:], acc[:], squares[:], ALU.add))
                        own.settle()
                    for k in range(2):
                        one = x3[:, bass.ds(4 * i + 2 * c + k, 1), :]
                        V.tensor_scalar(one, one, vcol(4 * i + 2 * c + k + V_FIN), None, ALU.mult).then_inc(x3_final, 1)

            with dve.Fori(0, D_IT - 1) as i:
                own.enter(i, 2)
                down(i, False)
            own.leave(D_IT - 1)
            down(D_IT - 1, True)
            dve.wait_ge(fin_rms, 1)
            V.reciprocal(small[:, 4:6], small[:, 2:4]).then_inc(fin_r, 1)
            dve.wait_ge(fin_r, 1)
            for f in range(1, 8, 2):
                tt, q = f % 2, f // 2
                dve.wait_ge(rows_turned, f + 1)
                V.tensor_scalar(rows_out[:, tt, q * 512:(q + 1) * 512], row_bank(f), small[:, 4 + tt:5 + tt], None,
                                ALU.mult).then_inc(rows_v, 1)

        @block.tensor
        def _(pe):
            mm = nc.tensor.matmul

            def multiply(name, i, j, moving, k0, first, last, rows_so_far=None, high=0):
                t0, g0, tiles, groups = seg[name]
                hi = slice(high, high + S)
                kh, c = tile_rows(j, name) // 2, group_of(name, j)
                for f in range(2):
                    if rows_so_far:
                        rows_so_far(k0 + (f + 1) * kh)
                    pe.wait_ge(lo_ready, 2 * (t0 + j) + f + 1 + i * (2 * tiles))
                    if f == 0 and first and not (isinstance(i, int) and g0 + c - 1 + i * groups <= 0):
                        pe.wait_ge(group_summed, g0 + c - 1 + i * groups)
                    for k in range(kh):
                        for b in range(2):
                            w = parts[:, (2 * j + f) % HALF_SLOTS, k, :, b * P:(b + 1) * P]
                            start, stop = first and f == 0 and k == 0, last and f == 1 and k == kh - 1
                            bank, move = main[:, c % 2, b, :], moving[:, k0 + f * kh + k, :]
                            if stop:
                                mm(bank[:, hi], w[:, 1, :], move[:, hi], start=False, stop=False)
                                ins = mm(bank, w[:, 0, :], move, start=start, stop=True)
                            else:
                                mm(bank, w[:, 0, :], move, start=start, stop=False)
                                ins = mm(bank[:, hi], w[:, 1, :], move[:, hi], start=False, stop=False)
                    ins.then_inc(half_used, 1)

            def multiply_rows(name, i, j, k0, first, last):
                t0, g0, tiles, groups = seg[name]
                c = group_of(name, j)
                for f in range(2):
                    pe.wait_ge(lo_ready, 2 * (t0 + j) + f + 1 + i * (2 * tiles))
                    if f == 0 and first:
                        pe.wait_ge(group_summed, g0 + c - 1 + i * groups)
                    for k in range(HALF_K):
                        kk = k0 + f * HALF_K + k
                        for b in range(TT):
                            w = parts[:, (2 * j + f) % HALF_SLOTS, k].rearrange("p a c -> p (a c)")
                            stop, bank = last and f == 1 and k == HALF_K - 1, main[:, c % 2, b, :]
                            hi, lo = (h_parts[:, kk, a * S + b * P:a * S + (b + 1) * P] for a in range(2))
                            if stop:
                                mm(bank[:, 0:COLS], lo, w[:, 0:COLS], start=False, stop=False)
                                ins = mm(bank, hi, w, start=False, stop=True)
                            else:
                                mm(bank, hi, w, start=first and f == 0 and k == 0, stop=False)
                                ins = mm(bank[:, 0:COLS], lo, w[:, 0:COLS], start=False, stop=False)
                    ins.then_inc(half_used, 1)

            def group_of(name, j):
                return j // NDT if name == "D" else j if name == "B" else j // 2

            def project(name, i, c, moving=None):
                for k in range(2):
                    if moving is None:
                        multiply_rows(name, i, 2 * c + k, k * TILE_K, k == 0, k == 1)
                    else:
                        multiply(name, i, 2 * c + k, moving, k * TILE_K, k == 0, k == 1)

            def keep_clock(products):
                for _ in range(products):
                    mm(aux[:, 2, 0:P], ident[:], ident[:], start=True, stop=True)

            pe.wait_ge(pool_const, 1)
            keep_clock(WARM_UP)
            pe.wait_ge(mix_in, 16)
            nc.tensor.transpose(aux[:, 3, 0:KD], vec_rows[V_MIX:V_MIX + KD, 0, :], ident[0:KD, 0:KD]).then_inc(vec_t, 1)

            def turn(ks):
                for k in ks:
                    if k == 10:
                        pe.wait_ge(vec_ready, 1)
                    if k >= 12:
                        pe.wait_ge(h_lo, k // 2 * 2 - 10)
                    if k % 4 == 0:
                        pe.wait_ge(x_scaled_a, k // 4 + 1)
                        pe.wait_ge(x_scaled_v, k // 4 + 1)
                    for tt in range(TT):
                        ins = nc.tensor.transpose(turn_bank(k)[:, tt * P:(tt + 1) * P], x_rows[:, tt, k * P:(k + 1) * P], ident[:])
                    ins.then_inc(x_turned, 1)

            turn(range(0, 8))
            keep_clock(STAY_WARM)
            for i in range(M_IT):
                if i == 0:
                    def follow(ready):
                        if ready == 2 * HALF_K:
                            turn(range(8, KD))
                        pe.wait_ge(h_lo, ready)

                    multiply("M", 0, 0, h_parts, 0, True, False, follow)
                    multiply("M", 0, 1, h_parts, TILE_K, False, True, follow)
                    pe.wait_ge(vec_in, 9 * 16)
                    nc.tensor.transpose(aux[:, 3, 0:P], vec_rows[:, 0, :], ident[:])
                    nc.tensor.transpose(aux[:, 3, P:P + 2 * KF], vec_rows[0:2 * KF, 1, :], ident[0:2 * KF, 0:2 * KF])
                    nc.tensor.transpose(aux[:, 3, P + 2 * KF:P + 4 * KF], vec_rows[0:2 * KF, 2, :],
                                        ident[0:2 * KF, 0:2 * KF]).then_inc(vec_t, 1)
                    pe.wait_ge(wif_lo, 1)
                    for k in range(KD):
                        ins = mm(aux[:, 0, :], wif_parts[:, k].rearrange("p a c -> p (a c)"), h_parts[:, k, :],
                                 start=k == 0, stop=k == KD - 1)
                    ins.then_inc(if_done, 1)
                else:
                    project("M", i, 0, h_parts)
                project("M", i, 1, h_parts)
                project("M", i, 2)
                multiply_rows("M", i, 6, 0, True, False)
                if i == 0:
                    pe.wait_ge(c_row_ready, 2)
                    for tt in range(TT):
                        ins = nc.tensor.transpose(aux[:, 1, tt * M_H:(tt + 1) * M_H], li_row[:, tt * P:(tt + 1) * P],
                                                  ident[0:M_H, 0:M_H])
                    ins.then_inc(c_turned, 1)
                pe.wait_ge(mqk_ready, 2 * i + 2)
                if i == 0:
                    pe.wait_ge(c_ready, 1)
                    pe.wait_ge(pool_const, 4)
                for h in range(2):
                    mm(aux[:, h, 0:S], mk[:, h, 0:P], mq[:, h, :], start=True, stop=True)
                    mm(aux[:, h, S:S + P], mk[:, h, P:S], mq[:, h, P:S], start=True, stop=True)
                    hd = 2 * i + h
                    mm(aux[:, 2 + h, 0:S], pick[:, hd, :], g_row[:], start=True, stop=False)
                    mm(aux[:, 2 + h, 0:P], ident_half[:], future[:], start=False, stop=True)
                    mm(aux[:, 2 + h, S:S + P], pick[:, hd, :], g_row[:, P:S], start=True, stop=False)
                    mm(aux[:, 2 + h, S:S + P], ident_half[:], future[:], start=False, stop=True).then_inc(mqk_done, 1)
                multiply_rows("M", i, 7, TILE_K, False, True)
                multiply("M", i, 8, h_parts, 0, True, False)
                for h in range(2):
                    pe.wait_ge(mprob_ready, 2 * i + h + 1)
                    mm(aux[:, 2 + h, 0:S], ones[:, 0:P], mprobs[:, h, 0:S], start=True, stop=False)
                    mm(aux[:, 2 + h, P:S], ones[:, 0:P], mprobs[:, h, S:S + P], start=False, stop=True)
                    mm(aux[:, 2 + h, S:2 * S], pick[:, 2 * i + h, :], m_row[:], start=True, stop=True)
                    pe.wait_ge(group_summed, 6 * i + 3 + h)
                    for v in range(2):
                        dst = aux[:, h, v * S:(v + 1) * S]
                        cols = slice(h * DV + v * P, h * DV + (v + 1) * P)
                        mm(dst, mv[:, 0, cols], mprobs[:, h, 0:S], start=True, stop=False)
                        ins = mm(dst[:, P:S], mv[:, 1, cols], mprobs[:, h, S:S + P], start=False, stop=True)
                    ins.then_inc(mnum_done, 1)
                multiply("M", i, 9, h_parts, TILE_K, False, True)
                multiply("M", i, 10, h_parts, 0, True, False)
                for h in range(2):
                    pe.wait_ge(hsq_summed, 2 * i + h + 1)
                    ins = mm(aux[:, 2, h * S:(h + 1) * S], ones[:, 0:P], hsq[:, h, 0, :], start=True, stop=True)
                ins.then_inc(mss_done, 1)
                multiply("M", i, 11, h_parts, TILE_K, False, True)

            with pe.Fori(0, A_IT) as i:
                project("A", i, 0, h_parts)
                project("A", i, 1, h_parts)
                project("A", i, 2)
                pe.wait_ge(group_summed, seg["A"][1] + 2 + 6 * i)
                for h in range(2):
                    mm(aux[:, h, 0:P], aq[:, h, 0:P], ak[:, h, 0:P], start=True, stop=True)
                    mm(aux[:, h, P:3 * P], aq[:, h, P:S], ak[:, h, :], start=True, stop=True).then_inc(a_scored, 1)
                project("A", i, 3, h_parts)
                multiply("A", i, 8, h_parts, 0, True, False)
                for h in range(2):
                    pe.wait_ge(a_prob, 2 * i + h + 1)
                    for q in range(3):
                        ins = nc.tensor.transpose(aux[:, 2 + h, q * P:(q + 1) * P], scores[:, h, q * P:(q + 1) * P], ident[:])
                    ins.then_inc(a_turned, 1)
                multiply("A", i, 9, h_parts, TILE_K, False, True)
                multiply("A", i, 10, h_parts, 0, True, False)
                pe.wait_ge(a_copied, 2 * i + 2)
                pe.wait_ge(group_summed, seg["A"][1] + 3 + 6 * i)
                for h in range(2):
                    dst = aux[:, 0, h * S:(h + 1) * S]
                    mm(dst, av[:, 0, h * P:(h + 1) * P], probs_t[:, h, 0:S], start=True, stop=False)
                    ins = mm(dst[:, P:S], av[:, 1, h * P:(h + 1) * P], probs_t[:, h, S:S + P], start=False, stop=True)
                ins.then_inc(a_out, 1)
                multiply("A", i, 11, h_parts, TILE_K, False, True)
            with pe.Fori(0, G_IT) as i:
                for c in range(2):
                    project("G", i, c, h_parts)
            pe.wait_ge(hm_lo, KV)
            pe.wait_ge(ha_lo, A_IT)
            with pe.Fori(0, B_IT) as i:
                for j in range(4):
                    if j % 2 == 0:
                        multiply("B", i, j, hm_parts, 0, True, True, high=S)
                    else:
                        multiply("B", i, j, ha_parts, 0, True, True)
            with pe.Fori(0, O_IT) as i:
                for c in range(2):
                    if c == 0:
                        pe.wait_ge(merged_lo, B_IT)
                    multiply("O", i, 2 * c, merged_parts, 0, True, False)
                    if c == 0:
                        pe.wait_ge(merged_lo, 2 * B_IT)
                    multiply("O", i, 2 * c + 1, merged_parts, TILE_K, False, True)
                    pe.wait_ge(xs_copied, 2 * i + c + 1)
                    for b in range(2):
                        for tt in range(TT):
                            ins = nc.tensor.transpose(aux[:, c, b * S + tt * P:b * S + (tt + 1) * P],
                                                      x_stage[:, tt, b * P:(b + 1) * P], ident[:])
                    ins.then_inc(xt_done, 1)
            pe.wait_ge(h2_lo, KD // 2)
            multiply("U", 0, 0, h_parts, 0, True, False)
            pe.wait_ge(h2_lo, KD)
            multiply("U", 0, 1, h_parts, TILE_K, False, True)
            pe.wait_ge(acc_ready, 2 * O_IT)
            mm(aux[:, 0, 0:S], ones[:, 0:P], acc[:, 0, :], start=True, stop=False)
            mm(aux[:, 0, 0:S], ones[:, 0:P], acc[:, 1, :], start=False, stop=True).then_inc(ss_done, 1)
            project("U", 0, 1, h_parts)
            with pe.Fori(1, U_IT) as i:
                for c in range(2):
                    project("U", i, c, h_parts)
            pe.wait_ge(act_lo, U_IT - 2)
            with pe.Fori(0, D_IT) as i:
                for c in range(2):
                    for k in range(NDT):
                        if c == 0 and k == NDT - 1:
                            pe.wait_ge(act_lo, U_IT)
                        multiply("D", i, NDT * c + k, act_parts, k * TILE_K, k == 0, k == NDT - 1)
            def turn_rows(f):
                tt, q = f % 2, f // 2
                for c in range(4):
                    ins = nc.tensor.transpose(row_bank(f)[:, c * P:(c + 1) * P], x3[:, 4 * q + c, tt * P:(tt + 1) * P], ident[:])
                ins.then_inc(rows_turned, 1)

            pe.wait_ge(x3_final, KD - 2)
            for f in range(6):
                turn_rows(f)
            pe.wait_ge(x3_sq, 2 * D_IT)
            for tt in range(TT):
                for a, part in enumerate((acc[:, 0], acc[:, 1], squares[:, 0], squares[:, 1])):
                    ins = mm(row_bank(7)[:, tt:tt + 1], part[:, tt * P:(tt + 1) * P], ones[:, 0:1], start=a == 0, stop=a == 3)
            ins.then_inc(fin_ss, 1)
            pe.wait_ge(x3_final, KD)
            turn_rows(6)
            pe.wait_ge(fin_rms, 1)
            turn_rows(7)


_INS = ["x", "norm_mix", "w_in", "conv_qk_w", "conv_qk_b", "b_igate", "b_fgate", "m_norm", "rel_bias", "gate_bias",
        "w_branch_m", "w_branch_a", "w_out", "norm_ffn", "w_up", "conv_ffn_w", "conv_ffn_b", "w_down", "norm_final"]


def kernel(**inputs):
    import numpy as _np
    import concourse.bacc as _bacc
    from concourse import mybir as _mybir
    from concourse.bass_utils import run_bass_kernel_spmd as _run

    nc = _bacc.Bacc("TRN2", target_bir_lowering=False, num_devices=1)
    arrays, args = {}, []
    for name in _INS:
        a = _np.ascontiguousarray(inputs[name])
        arrays[f"in_{name}_dram"] = a
        args.append(nc.dram_tensor(f"in_{name}_dram", a.shape, _mybir.dt.from_np(a.dtype), kind="ExternalInput").ap())
    shape = arrays["in_x_dram"].shape
    args.append(nc.dram_tensor("out_0_dram", shape, _mybir.dt.float32, kind="ExternalOutput").ap())
    hybrid_block(nc, *args)
    r = _run(nc, [arrays], core_ids=[0])
    return r.results[0]["out_0_dram"]
```
